# Optimizing a Trainium2 kernel written in Bass

```python
import math
import jax
import jax.numpy as jnp
from jax import lax
import numpy as np

D_MODEL = 1024
BATCH = 1
SEQ = 1024
DEPTH = 1

CHUNK = 64
Q_BLOCK = 128
EPS = 1e-6
NEG_BIG = -1e30
EXP_CLIP = 60.0

D_MIX = D_MODEL
N_MIXERS = 4
GROUP_W = D_MIX // N_MIXERS

S5_CH = 16
S5_GROUPS = GROUP_W // S5_CH
S5_STATE = 64
S5_DT_MIN = 1e-3
S5_DT_MAX = 1e-1

HG_HEADS = 4
HG_DH = GROUP_W // HG_HEADS

FOX_HEADS = 4
FOX_DH = GROUP_W // FOX_HEADS

ML_HEADS = 4
ML_DH = GROUP_W // ML_HEADS
ML_CONV = 4

D_FF = int(math.ceil(8 * D_MODEL / 3 / 256)) * 256

COL_WIDTHS = (GROUP_W,) * 8 + (FOX_HEADS,) + (GROUP_W,) * 4 + (ML_HEADS, ML_HEADS)
D_IN = sum(COL_WIDTHS)
SPLIT_IDX = tuple(int(c) for c in np.cumsum(COL_WIDTHS)[:-1])


F32 = jnp.float32

def rms_norm(x, gain):
    xf = x.astype(F32)
    y = xf * lax.rsqrt(jnp.mean(xf * xf, axis=-1, keepdims=True) + EPS)
    return (y * gain.astype(F32)).astype(x.dtype)

def headwise_rms_norm(x, gain, head_dim):
    shp = x.shape
    xf = x.astype(F32).reshape(shp[:-1] + (shp[-1] // head_dim, head_dim))
    y = xf * lax.rsqrt(jnp.mean(xf * xf, axis=-1, keepdims=True) + EPS)
    return (y.reshape(shp) * gain.astype(F32)).astype(x.dtype)

def causal_depthwise_conv(x, w):
    k_w, ch = w.shape
    return lax.conv_general_dilated(
        x, w[:, None, :].astype(x.dtype), window_strides=(1,), padding=[(k_w - 1, 0)],
        dimension_numbers=('NWC', 'WIO', 'NWC'), feature_group_count=ch)

def to_chunks(t):
    b, s, h, d = t.shape
    return t.reshape(b, s // CHUNK, CHUNK, h, d).transpose(1, 0, 3, 2, 4)

def from_chunks(t):
    nc, b, h, l, d = t.shape
    return t.transpose(1, 0, 3, 2, 4).reshape(b, nc * l, h, d)

def _complex_affine_combine(e1, e2):
    a1r, a1i, b1r, b1i = e1
    a2r, a2i, b2r, b2i = e2
    return (a2r * a1r - a2i * a1i, a2r * a1i + a2i * a1r,
            a2r * b1r - a2i * b1i + b2r, a2r * b1i + a2i * b1r + b2i)

def s5_mixer(u, lam_re, lam_im, b_re, b_im, c_re, c_im, d_skip, log_dt, w_glu, gain):
    bsz, seq, _ = u.shape
    uf = u.astype(F32)
    ug = uf.reshape(bsz, seq, S5_GROUPS, S5_CH)
    lr = jnp.minimum(lam_re.astype(F32), -1e-4)
    li = lam_im.astype(F32)
    dt = jnp.exp(log_dt.astype(F32))[:, None]
    mag = jnp.exp(lr * dt)
    ab_re = mag * jnp.cos(li * dt)
    ab_im = mag * jnp.sin(li * dt)
    den = lr * lr + li * li
    cf_re = ((ab_re - 1.0) * lr + ab_im * li) / den
    cf_im = (ab_im * lr - (ab_re - 1.0) * li) / den
    bre = b_re.astype(F32)
    bim = b_im.astype(F32)
    bb_re = cf_re[..., None] * bre - cf_im[..., None] * bim
    bb_im = cf_re[..., None] * bim + cf_im[..., None] * bre
    bu_re = jnp.einsum('bsgp,gnp->bsgn', ug, bb_re)
    bu_im = jnp.einsum('bsgp,gnp->bsgn', ug, bb_im)
    a_re = jnp.broadcast_to(ab_re, bu_re.shape)
    a_im = jnp.broadcast_to(ab_im, bu_im.shape)
    _, _, x_re, x_im = lax.associative_scan(
        _complex_affine_combine, (a_re, a_im, bu_re, bu_im), axis=1)
    y = (jnp.einsum('bsgn,gpn->bsgp', x_re, c_re.astype(F32))
         - jnp.einsum('bsgn,gpn->bsgp', x_im, c_im.astype(F32))).reshape(bsz, seq, GROUP_W)
    y = y + d_skip.astype(F32) * uf
    g = jax.nn.gelu(y)
    y = g * jax.nn.sigmoid(g @ w_glu.astype(F32))
    return rms_norm(y, gain).astype(u.dtype)

def _hgrn2_chunk(state, inp):
    q, k, v, lf = inp
    l = q.shape[2]
    b = jnp.cumsum(lf, axis=2)
    o_inter = jnp.einsum('bhtk,bhkv->bhtv', q * jnp.exp(b), state)
    causal = jnp.tril(jnp.ones((l, l), dtype=bool))
    diff = b[:, :, :, None, :] - b[:, :, None, :, :]
    decay = jnp.exp(jnp.where(causal[:, :, None], diff, NEG_BIG))
    scores = jnp.einsum('bhtk,bhsk,bhtsk->bhts', q, k, decay)
    o_intra = jnp.einsum('bhts,bhsv->bhtv', scores, v)
    b_last = b[:, :, -1:, :]
    new_state = (jnp.exp(b_last[:, :, 0, :])[..., None] * state
                 + jnp.einsum('bhsk,bhsv->bhkv', k * jnp.exp(b_last - b), v))
    return new_state, o_inter + o_intra

def hgrn2_mixer(q, fz, i, g, lb, gain):
    bsz, seq, _ = q.shape
    z = fz.astype(F32)
    logf = jax.nn.log_sigmoid(z) + jnp.log1p(lb * jnp.exp(jnp.minimum(-z, EXP_CLIP)))
    k = (1.0 - lb) * jax.nn.sigmoid(-z)

    def heads(t):
        return to_chunks(t.astype(F32).reshape(bsz, seq, HG_HEADS, HG_DH))

    s0 = jnp.zeros((bsz, HG_HEADS, HG_DH, HG_DH), F32)
    _, o = lax.scan(_hgrn2_chunk, s0, (heads(q), heads(k), heads(i), heads(logf)))
    o = from_chunks(o).reshape(bsz, seq, GROUP_W)
    o = headwise_rms_norm(o, gain, HG_DH) * jax.nn.silu(g.astype(F32))
    return o.astype(q.dtype)

def fox_mixer(q, k, v, fz, gain):
    bsz, seq, _ = q.shape

    def heads(t):
        return t.reshape(bsz, seq, FOX_HEADS, FOX_DH).transpose(0, 2, 1, 3)

    qh, kh, vh = heads(q), heads(k), heads(v)
    cum_logf = jnp.cumsum(jax.nn.log_sigmoid(fz.astype(F32)), axis=1).transpose(0, 2, 1)
    n_blk = seq // Q_BLOCK
    q_blocks = qh.reshape(bsz, FOX_HEADS, n_blk, Q_BLOCK, FOX_DH).transpose(2, 0, 1, 3, 4)
    f_blocks = cum_logf.reshape(bsz, FOX_HEADS, n_blk, Q_BLOCK).transpose(2, 0, 1, 3)
    k_pos = jnp.arange(seq)
    scale = FOX_DH ** -0.5

    def attend(args):
        blk, qb, fq = args
        q_pos = blk * Q_BLOCK + jnp.arange(Q_BLOCK)
        s = (jnp.einsum('bhqd,bhkd->bhqk', qb, kh).astype(F32) * scale
             + fq[..., None] - cum_logf[:, :, None, :])
        s = jnp.where(k_pos[None, :] <= q_pos[:, None], s, NEG_BIG)
        p = jax.nn.softmax(s, axis=-1)
        return jnp.einsum('bhqk,bhkd->bhqd', p.astype(vh.dtype), vh)

    out = lax.map(attend, (jnp.arange(n_blk), q_blocks, f_blocks))
    out = out.transpose(1, 0, 3, 2, 4).reshape(bsz, seq, GROUP_W)
    return headwise_rms_norm(out, gain, FOX_DH)

def _mlstm_chunk(carry, inp):
    c_mat, n_vec, m_prev = carry
    q, k, v, ig, lf = inp
    l = q.shape[2]
    b = jnp.cumsum(lf, axis=-1)
    causal = jnp.tril(jnp.ones((l, l), dtype=bool))
    d_log = jnp.where(causal, b[..., :, None] - b[..., None, :] + ig[..., None, :], NEG_BIG)
    inter_log = b + m_prev[..., None]
    m_t = jnp.maximum(inter_log, jnp.max(d_log, axis=-1))
    w_inter = jnp.exp(inter_log - m_t)
    qk = jnp.einsum('bhtd,bhsd->bhts', q, k) * jnp.exp(d_log - m_t[..., None])
    num = (w_inter[..., None] * jnp.einsum('bhtk,bhkv->bhtv', q, c_mat)
           + jnp.einsum('bhts,bhsv->bhtv', qk, v))
    den = w_inter * jnp.einsum('bhtk,bhk->bht', q, n_vec) + jnp.sum(qk, axis=-1)
    h = num / jnp.maximum(jnp.abs(den), jnp.exp(-m_t))[..., None]
    b_last = b[..., -1]
    src_log = b_last[..., None] - b + ig
    m_new = jnp.maximum(b_last + m_prev, jnp.max(src_log, axis=-1))
    w_src = jnp.exp(src_log - m_new[..., None])
    decay = jnp.exp(b_last + m_prev - m_new)
    c_new = decay[..., None, None] * c_mat + jnp.einsum('bhs,bhsk,bhsv->bhkv', w_src, k, v)
    n_new = decay[..., None] * n_vec + jnp.einsum('bhs,bhsk->bhk', w_src, k)
    return (c_new, n_new, m_new), h

def mlstm_mixer(q, k, v, o, ig, fz, conv_w, gain):
    bsz, seq, _ = q.shape
    qk = jax.nn.silu(causal_depthwise_conv(jnp.concatenate([q, k], axis=-1), conv_w))
    q_c, k_c = qk[..., :GROUP_W], qk[..., GROUP_W:]

    def heads(t):
        return to_chunks(t.astype(F32).reshape(bsz, seq, ML_HEADS, ML_DH))

    def gates(t):
        return to_chunks(t.astype(F32)[..., None])[..., 0]

    lf = jax.nn.log_sigmoid(fz.astype(F32))
    init = (jnp.zeros((bsz, ML_HEADS, ML_DH, ML_DH), F32),
            jnp.zeros((bsz, ML_HEADS, ML_DH), F32),
            jnp.zeros((bsz, ML_HEADS), F32))
    _, h = lax.scan(_mlstm_chunk, init,
                    (heads(q_c), heads(k_c * ML_DH ** -0.5), heads(v), gates(ig), gates(lf)))
    h = from_chunks(h).reshape(bsz, seq, GROUP_W)
    h = headwise_rms_norm(h, gain, ML_DH) * jax.nn.sigmoid(o.astype(F32))
    return h.astype(q.dtype)

def first_inputs(seed: int = 0) -> dict:
    key = jax.random.key(seed)
    ks = jax.random.split(key, 26)

    def nrm(k, shape, scale):
        return scale * jax.random.normal(k, shape, F32)

    x = nrm(ks[0], (BATCH, SEQ, D_MODEL), 1.0)
    w_in = nrm(ks[1], (DEPTH, D_MODEL, D_IN), D_MODEL ** -0.5)
    fox_fb = 2.0 + nrm(ks[2], (DEPTH, FOX_HEADS), 0.1)
    ml_ib = nrm(ks[3], (DEPTH, ML_HEADS), 0.1)
    ml_fb = jnp.linspace(3.0, 6.0, ML_HEADS, dtype=F32)[None, :] + nrm(ks[4], (DEPTH, ML_HEADS), 0.1)
    gate_bias = jnp.concatenate([fox_fb, ml_ib, ml_fb], axis=-1)
    n_idx = jnp.arange(S5_STATE, dtype=F32)
    s5_lambda_re = -0.5 + nrm(ks[5], (DEPTH, S5_GROUPS, S5_STATE), 0.01)
    s5_lambda_im = math.pi * n_idx + nrm(ks[6], (DEPTH, S5_GROUPS, S5_STATE), 0.01)
    s5_b_re = nrm(ks[7], (DEPTH, S5_GROUPS, S5_STATE, S5_CH), (2 * S5_CH) ** -0.5)
    s5_b_im = nrm(ks[8], (DEPTH, S5_GROUPS, S5_STATE, S5_CH), (2 * S5_CH) ** -0.5)
    s5_c_re = nrm(ks[9], (DEPTH, S5_GROUPS, S5_CH, S5_STATE), (2 * S5_STATE) ** -0.5)
    s5_c_im = nrm(ks[10], (DEPTH, S5_GROUPS, S5_CH, S5_STATE), (2 * S5_STATE) ** -0.5)
    s5_d = nrm(ks[11], (DEPTH, GROUP_W), 1.0)
    s5_log_dt = jax.random.uniform(ks[12], (DEPTH, S5_GROUPS), F32,
                                   math.log(S5_DT_MIN), math.log(S5_DT_MAX))
    s5_w_glu = nrm(ks[13], (DEPTH, GROUP_W, GROUP_W), GROUP_W ** -0.5)
    hgrn_lb_logits = nrm(ks[14], (DEPTH, GROUP_W), 0.5)
    mlstm_conv_w = nrm(ks[15], (DEPTH, ML_CONV, 2 * GROUP_W), ML_CONV ** -0.5)
    mix_gain = 1.0 + nrm(ks[16], (DEPTH, D_MIX), 0.02)
    w_out = nrm(ks[17], (DEPTH, D_MIX, D_MODEL), D_MIX ** -0.5)
    ln_mix_pre = 1.0 + nrm(ks[18], (DEPTH, D_MODEL), 0.02)
    ln_mix_post = 1.0 + nrm(ks[19], (DEPTH, D_MODEL), 0.02)
    ln_ffn_pre = 1.0 + nrm(ks[20], (DEPTH, D_MODEL), 0.02)
    ln_ffn_post = 1.0 + nrm(ks[21], (DEPTH, D_MODEL), 0.02)
    w_ffn_gate = nrm(ks[22], (DEPTH, D_MODEL, D_FF), D_MODEL ** -0.5)
    w_ffn_up = nrm(ks[23], (DEPTH, D_MODEL, D_FF), D_MODEL ** -0.5)
    w_ffn_down = nrm(ks[24], (DEPTH, D_FF, D_MODEL), D_FF ** -0.5)
    return {'x': x, 'w_in': w_in, 'gate_bias': gate_bias,
            's5_lambda_re': s5_lambda_re, 's5_lambda_im': s5_lambda_im,
            's5_b_re': s5_b_re, 's5_b_im': s5_b_im, 's5_c_re': s5_c_re, 's5_c_im': s5_c_im,
            's5_d': s5_d, 's5_log_dt': s5_log_dt, 's5_w_glu': s5_w_glu,
            'hgrn_lb_logits': hgrn_lb_logits, 'mlstm_conv_w': mlstm_conv_w,
            'mix_gain': mix_gain, 'w_out': w_out,
            'ln_mix_pre': ln_mix_pre, 'ln_mix_post': ln_mix_post,
            'ln_ffn_pre': ln_ffn_pre, 'ln_ffn_post': ln_ffn_post,
            'w_ffn_gate': w_ffn_gate, 'w_ffn_up': w_ffn_up, 'w_ffn_down': w_ffn_down}

def first_block(x, w_in, gate_bias, s5_lambda_re, s5_lambda_im, s5_b_re, s5_b_im, s5_c_re, s5_c_im,
              s5_d, s5_log_dt, s5_w_glu, hgrn_lb_logits, mlstm_conv_w, mix_gain, w_out,
              ln_mix_pre, ln_mix_post, ln_ffn_pre, ln_ffn_post, w_ffn_gate, w_ffn_up, w_ffn_down):
    lb_prob = jax.nn.softmax(hgrn_lb_logits.astype(F32), axis=0)
    lb_all = jnp.maximum(jnp.cumsum(lb_prob, axis=0) - lb_prob[0:1], 0.0)

    h = x
    for l in range(DEPTH):
        a = rms_norm(h, ln_mix_pre[l])
        proj = a @ w_in[l]
        (s5_u, hg_q, hg_f, hg_i, hg_g, fox_q, fox_k, fox_v, fox_f,
         ml_q, ml_k, ml_v, ml_o, ml_i, ml_f) = jnp.split(proj, SPLIT_IDX, axis=-1)
        gb = gate_bias[l]
        gain = mix_gain[l]
        y_a = s5_mixer(s5_u, s5_lambda_re[l], s5_lambda_im[l], s5_b_re[l], s5_b_im[l],
                       s5_c_re[l], s5_c_im[l], s5_d[l], s5_log_dt[l], s5_w_glu[l],
                       gain[0:GROUP_W])
        y_b = hgrn2_mixer(hg_q, hg_f, hg_i, hg_g, lb_all[l], gain[GROUP_W:2 * GROUP_W])
        y_c = fox_mixer(fox_q, fox_k, fox_v, fox_f + gb[0:FOX_HEADS],
                        gain[2 * GROUP_W:3 * GROUP_W])
        y_d = mlstm_mixer(ml_q, ml_k, ml_v, ml_o,
                          ml_i + gb[FOX_HEADS:FOX_HEADS + ML_HEADS],
                          ml_f + gb[FOX_HEADS + ML_HEADS:FOX_HEADS + 2 * ML_HEADS],
                          mlstm_conv_w[l], gain[3 * GROUP_W:4 * GROUP_W])
        mix = jnp.concatenate([y_a, y_b, y_c, y_d], axis=-1) @ w_out[l]
        h = h + rms_norm(mix, ln_mix_post[l])

        a = rms_norm(h, ln_ffn_pre[l])
        ff = (jax.nn.silu(a @ w_ffn_gate[l]) * (a @ w_ffn_up[l])) @ w_ffn_down[l]
        h = h + rms_norm(ff, ln_ffn_post[l])
    return h


HEAD_DIM = 64
NSA_HEADS = 8
NSA_KV_HEADS = 2
NSA_GROUP = NSA_HEADS // NSA_KV_HEADS
SWA_HEADS = 8
SWA_KV_HEADS = 2
SWA_GROUP = SWA_HEADS // SWA_KV_HEADS
NSA_WIDTH = NSA_HEADS * HEAD_DIM
SWA_WIDTH = SWA_HEADS * HEAD_DIM
NSA_KV_WIDTH = NSA_KV_HEADS * HEAD_DIM
SWA_KV_WIDTH = SWA_KV_HEADS * HEAD_DIM
CMP_LEN = 32
CMP_STRIDE = 16
CMP_HIDDEN = 256
SLC_LEN = 64
SLC_TOPK = 8
NSA_WINDOW = 256
SLC_QUERY_CHUNK = 64
SWA_WINDOW = 128
BAND_BLOCK = 128
N_GROUPS = 4
EXPERTS_PER_GROUP = 8
N_EXPERTS = N_GROUPS * EXPERTS_PER_GROUP
EXPERT_TOPK = 2
EXPERT_FF = 256
MOE_BLOCK = 128
IN_SIZES = (NSA_WIDTH, NSA_KV_WIDTH, NSA_KV_WIDTH, NSA_KV_WIDTH, NSA_KV_WIDTH, NSA_KV_WIDTH, NSA_KV_WIDTH,
            3 * NSA_HEADS, SWA_WIDTH, SWA_KV_WIDTH, SWA_KV_WIDTH, 2 * D_MODEL)
IN_WIDTH = sum(IN_SIZES)
RMS_EPS = 1e-6
NEG_INF = -1e30
FORCE_SCORE = 1e9


def rms_norm_2(x, g):
    x32 = x.astype(jnp.float32)
    y = x32 * lax.rsqrt(jnp.mean(x32 * x32, axis=-1, keepdims=True) + RMS_EPS)
    return (y * g.astype(jnp.float32)).astype(x.dtype)

def masked_softmax(s, mask):
    s = jnp.where(mask, s, NEG_INF)
    m = jnp.max(s, axis=-1, keepdims=True)
    e = jnp.where(mask, jnp.exp(s - m), 0.0)
    z = jnp.sum(e, axis=-1, keepdims=True)
    return e / jnp.where(z > 0, z, 1.0)

def alibi_slopes():
    n = NSA_HEADS + SWA_HEADS
    s = 2.0 ** (-8.0 * np.arange(1, n + 1) / n)
    return jnp.asarray(s[:SWA_HEADS], jnp.float32), jnp.asarray(s[SWA_HEADS:], jnp.float32)

def compress_blocks(kv, pos, w1, w2):
    B, S, H, d = kv.shape
    r = CMP_LEN // CMP_STRIDE
    nc = S // CMP_STRIDE - r + 1
    kc = kv.reshape(B, S // CMP_STRIDE, CMP_STRIDE, H, d)
    blocks = jnp.concatenate([kc[:, i:i + nc] for i in range(r)], axis=2)
    blocks = blocks + pos[None, None, :, None, :]
    flat = jnp.transpose(blocks, (0, 1, 3, 2, 4)).reshape(B, nc, H, CMP_LEN * d)
    return jax.nn.silu(flat @ w1) @ w2

def compressed_branch(q, kc, vc, slopes):
    B, S, Hkv, G, d = q.shape
    nc = kc.shape[1]
    s = jnp.einsum('bshgd,bchd->bhgsc', q, kc, preferred_element_type=jnp.float32) * (d ** -0.5)
    end = jnp.arange(nc) * CMP_STRIDE + CMP_LEN - 1
    dist = jnp.arange(S)[:, None] - end[None, :]
    s = s - slopes.reshape(Hkv, G, 1, 1) * dist.astype(jnp.float32)
    p = masked_softmax(s, dist >= 0)
    o = jnp.einsum('bhgsc,bchd->bshgd', p.astype(vc.dtype), vc)
    return o, p

def select_blocks(p_cmp, S):
    nc = p_cmp.shape[-1]
    ns = S // SLC_LEN
    c0 = np.arange(nc) * CMP_STRIDE
    s0 = np.arange(ns) * SLC_LEN
    ov = np.clip(np.minimum(c0[:, None] + CMP_LEN, s0[None, :] + SLC_LEN)
                 - np.maximum(c0[:, None], s0[None, :]), 0, None) / CMP_LEN
    imp = jnp.einsum('bhsc,cj->bhsj', jnp.sum(p_cmp, axis=2), jnp.asarray(ov, jnp.float32))
    t = jnp.arange(S)[:, None]
    j = jnp.arange(ns)[None, :]
    cur = t // SLC_LEN
    valid = j * SLC_LEN <= t
    forced = (j == 0) | (j == cur) | (j == cur - 1)
    score = jnp.where(forced, FORCE_SCORE, jnp.where(valid, imp, NEG_INF))
    vals, idx = lax.top_k(score, min(SLC_TOPK, ns))
    return idx, vals > 0.5 * NEG_INF

def selected_branch(q, k, v, idx, valid, slopes):
    B, S, Hkv, G, d = q.shape
    ns = S // SLC_LEN
    n = idx.shape[-1]
    QC = SLC_QUERY_CHUNK
    nq = S // QC
    kb = jnp.transpose(k.reshape(B, ns, SLC_LEN, Hkv, d), (0, 3, 1, 2, 4))
    vb = jnp.transpose(v.reshape(B, ns, SLC_LEN, Hkv, d), (0, 3, 1, 2, 4))
    qc = jnp.swapaxes(q.reshape(B, nq, QC, Hkv, G, d), 0, 1)
    ic = jnp.transpose(idx.reshape(B, Hkv, nq, QC, n), (2, 0, 1, 3, 4))
    vc = jnp.transpose(valid.reshape(B, Hkv, nq, QC, n), (2, 0, 1, 3, 4))
    tc = jnp.arange(S).reshape(nq, QC)
    bi = jnp.arange(B)[:, None, None, None]
    hi = jnp.arange(Hkv)[None, :, None, None]
    sl = slopes.reshape(1, Hkv, G, 1, 1, 1)
    scale = d ** -0.5

    def chunk(args):
        qq, ii, vv, tt = args
        kg = kb[bi, hi, ii]
        vg = vb[bi, hi, ii]
        s = jnp.einsum('bqhgd,bhqnld->bhgqnl', qq, kg, preferred_element_type=jnp.float32) * scale
        kpos = ii[..., None] * SLC_LEN + jnp.arange(SLC_LEN)
        dist = tt[None, None, :, None, None] - kpos
        mask = (vv[..., None] & (dist >= 0))[:, :, None]
        s = s - sl * dist[:, :, None].astype(jnp.float32)
        p = masked_softmax(s.reshape(B, Hkv, G, QC, n * SLC_LEN), mask.reshape(B, Hkv, 1, QC, n * SLC_LEN))
        return jnp.einsum('bhgqk,bhqkd->bqhgd', p.astype(vg.dtype), vg.reshape(B, Hkv, QC, n * SLC_LEN, d))

    out = lax.map(chunk, (qc, ic, vc, tc))
    return jnp.swapaxes(out, 0, 1).reshape(B, S, Hkv, G, d)

def banded_attention(q, k, v, slopes, window, sinks):
    B, S, Hkv, G, d = q.shape
    nb = S // BAND_BLOCK
    nprev = -(-(window - 1) // BAND_BLOCK)
    pad = nprev * BAND_BLOCK
    kw = (nprev + 1) * BAND_BLOCK

    def band(a):
        ap = jnp.pad(a, ((0, 0), (pad, 0), (0, 0), (0, 0))).reshape(B, nb + nprev, BAND_BLOCK, Hkv, d)
        return jnp.concatenate([ap[:, j:j + nb] for j in range(nprev + 1)], axis=2)

    kb, vb = band(k), band(v)
    qb = q.reshape(B, nb, BAND_BLOCK, Hkv, G, d)
    s = jnp.einsum('bnqhgd,bnkhd->bnhgqk', qb, kb, preferred_element_type=jnp.float32) * (d ** -0.5)
    blk = jnp.arange(nb)[:, None] * BAND_BLOCK
    tpos = blk + jnp.arange(BAND_BLOCK)
    kpos = blk - pad + jnp.arange(kw)
    dist = tpos[:, :, None] - kpos[:, None, :]
    mask = ((dist >= 0) & (dist < window) & (kpos[:, None, :] >= 0))[None, :, None, None]
    s = s - slopes.reshape(1, 1, Hkv, G, 1, 1) * dist.astype(jnp.float32)[None, :, None, None]
    s = jnp.where(mask, s, NEG_INF)
    m = jnp.max(s, axis=-1, keepdims=True)
    if sinks is not None:
        sk = sinks.astype(jnp.float32).reshape(1, 1, Hkv, G, 1, 1)
        m = jnp.maximum(m, sk)
    e = jnp.where(mask, jnp.exp(s - m), 0.0)
    z = jnp.sum(e, axis=-1, keepdims=True)
    if sinks is not None:
        z = z + jnp.exp(sk - m)
    p = e / z
    o = jnp.einsum('bnhgqk,bnkhd->bnqhgd', p.astype(v.dtype), vb)
    return o.reshape(B, S, Hkv, G, d)

def hier_moe(h, w_group, b_group, w_expert, b_expert, w_gate_e, w_up_e, w_down_e):
    B, S, D = h.shape
    N = B * S
    hf = h.reshape(N, D)
    g_logits = (hf @ w_group).astype(jnp.float32) + b_group.astype(jnp.float32)
    g_prob = jax.nn.softmax(g_logits, axis=-1)
    grp = jnp.argmax(g_logits, axis=-1)
    p_grp = jnp.take_along_axis(g_prob, grp[:, None], axis=-1)[:, 0]
    e_logits = ((hf @ w_expert).astype(jnp.float32) + b_expert.astype(jnp.float32)).reshape(N, N_GROUPS, EXPERTS_PER_GROUP)
    e_in = jnp.take_along_axis(e_logits, grp[:, None, None], axis=1)[:, 0]
    top_v, top_i = lax.top_k(e_in, EXPERT_TOPK)
    weight = p_grp[:, None] * jax.nn.softmax(top_v, axis=-1)
    eid = (grp[:, None] * EXPERTS_PER_GROUP + top_i).reshape(-1)
    w_f = weight.reshape(-1)
    NK = N * EXPERT_TOPK
    tok = jnp.arange(NK) // EXPERT_TOPK
    order = jnp.argsort(eid)
    e_sorted = eid[order]
    counts = jnp.bincount(eid, length=N_EXPERTS)
    padded = (counts + MOE_BLOCK - 1) // MOE_BLOCK * MOE_BLOCK
    pad_end = jnp.cumsum(padded)
    pad_start = pad_end - padded
    cnt_start = jnp.cumsum(counts) - counts
    dest = pad_start[e_sorted] + jnp.arange(NK) - cnt_start[e_sorted]
    n_blocks = -(-(NK + N_EXPERTS * (MOE_BLOCK - 1)) // MOE_BLOCK)
    buf = jnp.zeros((n_blocks * MOE_BLOCK, D), h.dtype).at[dest].set(hf[tok[order]])
    block_e = jnp.minimum(jnp.searchsorted(pad_end, jnp.arange(n_blocks) * MOE_BLOCK, side='right'), N_EXPERTS - 1)

    def expert_block(args):
        xb, e = args
        return (jax.nn.silu(xb @ w_gate_e[e]) * (xb @ w_up_e[e])) @ w_down_e[e]

    yb = lax.map(expert_block, (buf.reshape(n_blocks, MOE_BLOCK, D), block_e)).reshape(-1, D)
    y_slot = yb[dest] * w_f[order][:, None].astype(yb.dtype)
    y = jnp.zeros((N, D), h.dtype).at[tok[order]].add(y_slot)
    return y.reshape(B, S, D)

def second_inputs(seed: int = 0) -> dict:
    key = jax.random.key(seed)
    ks = jax.random.split(key, 24)
    f32 = jnp.float32
    L = DEPTH
    d = HEAD_DIM

    def nrm(k, shape, scale):
        return jax.random.normal(k, shape, f32) * scale

    return {
        "x": nrm(ks[0], (BATCH, SEQ, D_MODEL), 1.0),
        "norm_mix_g": 1.0 + nrm(ks[1], (L, D_MODEL), 0.02),
        "w_in": nrm(ks[2], (L, D_MODEL, IN_WIDTH), D_MODEL ** -0.5),
        "cmp_pos_k": nrm(ks[3], (L, CMP_LEN, d), 0.1),
        "cmp_w1_k": nrm(ks[4], (L, CMP_LEN * d, CMP_HIDDEN), (CMP_LEN * d) ** -0.5),
        "cmp_w2_k": nrm(ks[5], (L, CMP_HIDDEN, d), CMP_HIDDEN ** -0.5),
        "cmp_pos_v": nrm(ks[6], (L, CMP_LEN, d), 0.1),
        "cmp_w1_v": nrm(ks[7], (L, CMP_LEN * d, CMP_HIDDEN), (CMP_LEN * d) ** -0.5),
        "cmp_w2_v": nrm(ks[8], (L, CMP_HIDDEN, d), CMP_HIDDEN ** -0.5),
        "sinks": nrm(ks[9], (L, SWA_HEADS), 0.5),
        "w_a": nrm(ks[10], (L, NSA_WIDTH, D_MODEL), NSA_WIDTH ** -0.5),
        "w_b": nrm(ks[11], (L, SWA_WIDTH, D_MODEL), SWA_WIDTH ** -0.5),
        "w_o": nrm(ks[12], (L, D_MODEL, D_MODEL), D_MODEL ** -0.5),
        "norm_ffn_g": 1.0 + nrm(ks[13], (L, D_MODEL), 0.02),
        "w_group": nrm(ks[14], (L, D_MODEL, N_GROUPS), D_MODEL ** -0.5),
        "b_group": nrm(ks[15], (L, N_GROUPS), 0.01),
        "w_expert": nrm(ks[16], (L, D_MODEL, N_EXPERTS), D_MODEL ** -0.5),
        "b_expert": nrm(ks[17], (L, N_EXPERTS), 0.01),
        "w_gate_e": nrm(ks[18], (L, N_EXPERTS, D_MODEL, EXPERT_FF), D_MODEL ** -0.5),
        "w_up_e": nrm(ks[19], (L, N_EXPERTS, D_MODEL, EXPERT_FF), D_MODEL ** -0.5),
        "w_down_e": nrm(ks[20], (L, N_EXPERTS, EXPERT_FF, D_MODEL), EXPERT_FF ** -0.5),
        "norm_final_g": 1.0 + nrm(ks[21], (D_MODEL,), 0.02),
    }

def second_block(x, norm_mix_g, w_in, cmp_pos_k, cmp_w1_k, cmp_w2_k, cmp_pos_v, cmp_w1_v, cmp_w2_v,
              sinks, w_a, w_b, w_o, norm_ffn_g, w_group, b_group, w_expert, b_expert,
              w_gate_e, w_up_e, w_down_e, norm_final_g):
    B, S, _ = x.shape
    slopes_swa, slopes_nsa = alibi_slopes()
    split_points = [int(c) for c in np.cumsum(IN_SIZES)[:-1]]
    for l in range(DEPTH):
        h = rms_norm_2(x, norm_mix_g[l])
        proj = h @ w_in[l]
        (q_a, k_cmp, v_cmp, k_slc, v_slc, k_win, v_win, g_nsa,
         q_b, k_b, v_b, g_merge) = jnp.split(proj, split_points, axis=-1)
        q_a = q_a.reshape(B, S, NSA_KV_HEADS, NSA_GROUP, HEAD_DIM)
        kv_a = [t.reshape(B, S, NSA_KV_HEADS, HEAD_DIM) for t in (k_cmp, v_cmp, k_slc, v_slc, k_win, v_win)]
        kc = compress_blocks(kv_a[0], cmp_pos_k[l], cmp_w1_k[l], cmp_w2_k[l])
        vc = compress_blocks(kv_a[1], cmp_pos_v[l], cmp_w1_v[l], cmp_w2_v[l])
        o_cmp, p_cmp = compressed_branch(q_a, kc, vc, slopes_nsa)
        idx, valid = select_blocks(p_cmp, S)
        o_slc = selected_branch(q_a, kv_a[2], kv_a[3], idx, valid, slopes_nsa)
        o_win = banded_attention(q_a, kv_a[4], kv_a[5], slopes_nsa, NSA_WINDOW, None)
        g = jax.nn.sigmoid(g_nsa).reshape(B, S, NSA_KV_HEADS, NSA_GROUP, 3)
        o_a = (g[..., 0:1] * o_cmp + g[..., 1:2] * o_slc + g[..., 2:3] * o_win).reshape(B, S, NSA_WIDTH)
        q_b = q_b.reshape(B, S, SWA_KV_HEADS, SWA_GROUP, HEAD_DIM)
        k_b = k_b.reshape(B, S, SWA_KV_HEADS, HEAD_DIM)
        v_b = v_b.reshape(B, S, SWA_KV_HEADS, HEAD_DIM)
        o_b = banded_attention(q_b, k_b, v_b, slopes_swa, SWA_WINDOW, sinks[l]).reshape(B, S, SWA_WIDTH)
        gate_a, gate_b = jnp.split(jax.nn.sigmoid(g_merge), 2, axis=-1)
        mix = (gate_a * (o_a @ w_a[l]) + gate_b * (o_b @ w_b[l])) @ w_o[l]
        x = x + mix
        x = x + hier_moe(rms_norm_2(x, norm_ffn_g[l]), w_group[l], b_group[l], w_expert[l], b_expert[l],
                         w_gate_e[l], w_up_e[l], w_down_e[l])
    return rms_norm_2(x, norm_final_g)


def setup_inputs(seed=0):
    out = dict(first_inputs(seed))
    for name, value in second_inputs(seed + 1).items():
        if name != "x":
            out[name + "_2"] = value
    return out


def reference(
    x, w_in, gate_bias, s5_lambda_re, s5_lambda_im, s5_b_re, s5_b_im, s5_c_re, s5_c_im, s5_d,
    s5_log_dt, s5_w_glu, hgrn_lb_logits, mlstm_conv_w, mix_gain, w_out, ln_mix_pre, ln_mix_post,
    ln_ffn_pre, ln_ffn_post, w_ffn_gate, w_ffn_up, w_ffn_down, norm_mix_g_2, w_in_2,
    cmp_pos_k_2, cmp_w1_k_2, cmp_w2_k_2, cmp_pos_v_2, cmp_w1_v_2, cmp_w2_v_2, sinks_2, w_a_2,
    w_b_2, w_o_2, norm_ffn_g_2, w_group_2, b_group_2, w_expert_2, b_expert_2, w_gate_e_2,
    w_up_e_2, w_down_e_2, norm_final_g_2,
):
    x = first_block(
        x, w_in, gate_bias, s5_lambda_re, s5_lambda_im, s5_b_re, s5_b_im, s5_c_re, s5_c_im,
        s5_d, s5_log_dt, s5_w_glu, hgrn_lb_logits, mlstm_conv_w, mix_gain, w_out, ln_mix_pre,
        ln_mix_post, ln_ffn_pre, ln_ffn_post, w_ffn_gate, w_ffn_up, w_ffn_down,
    )
    return second_block(
        x, norm_mix_g_2, w_in_2, cmp_pos_k_2, cmp_w1_k_2, cmp_w2_k_2, cmp_pos_v_2, cmp_w1_v_2,
        cmp_w2_v_2, sinks_2, w_a_2, w_b_2, w_o_2, norm_ffn_g_2, w_group_2, b_group_2,
        w_expert_2, b_expert_2, w_gate_e_2, w_up_e_2, w_down_e_2, norm_final_g_2,
    )


_drawn_inputs = setup_inputs


def setup_inputs(seed=0):
    import zlib

    import numpy as np

    out = dict(_drawn_inputs(seed))
    spreads = {}
    factors = {'s5_lambda_re': 200.0,
     'ln_ffn_post': 2.883,
     'norm_mix_g_2': 4.737,
     'cmp_pos_k_2': 8.0,
     'cmp_pos_v_2': 3.692,
     'norm_ffn_g_2': 2.892,
     'b_group_2': 4.493,
     'b_expert_2': 5.617,
     'norm_final_g_2': 22.858,
     'sinks_2': 54.188}
    for name, (base, spread) in spreads.items():
        noise = np.random.default_rng([zlib.crc32(name.encode()), seed]).standard_normal(out[name].shape)
        drawn = base * np.exp(spread * noise) if base else spread * noise
        out[name] = jnp.asarray(drawn.astype(out[name].dtype))
    for name, factor in factors.items():
        out[name] = (out[name] * factor).astype(out[name].dtype)
    return out
```

```python
import numpy as np
import concourse.bass as bass
from concourse import mybir
from concourse.alu_op_type import AluOpType as ALU

F32 = mybir.dt.float32
BF16 = mybir.dt.bfloat16
ACT = mybir.ActivationFunctionType
AX = mybir.AxisListType.X

P = 128
S = 1024
D = 1024
NT = S // P
KD = D // P
GW = 256
FF = 2816
EPS = 1e-6
NEG = -1e30
TWO_PI = 6.283185307179586
ROUND = 12582912.0

IN1 = dict(s5=0, hq=256, hf=512, hi=768, hg=1024, fq=1280, fk=1536, fv=1792, ff=2048,
           mq=2052, mk=2308, mv=2564, mo=2820, mi=3076, mf=3080)
IN2 = dict(q=0, kc=512, vc=640, ks=768, vs=896, kw=1024, vw=1152, g=1280, qb=1304, kb=1816,
           vb=1944, ga=2072, gb=3096)
NC = 63
NE, EG, NG, EF = 32, 8, 4, 256
LEVELS = 7


class Lane:

    turns = True
    partner = None

    def __init__(self, sem, chained):
        self.sem, self.chained, self.count, self.steps, self.held = sem, chained, 0, [], []

    def do(self, step, after=(), chain=True):
        waits = self.held + [m for m in after if m is not None]
        self.held = []
        if self.chained and chain and self.count:
            waits.append((self.sem, self.count))
        if self.partner is not None and Lane.turns and self.partner.count:
            waits.append((self.partner.sem, self.partner.count))
        self.count += 1
        self.steps.append((waits, step, self.sem, 1))
        return (self.sem, self.count)

    def dma(self, out, in_, arrival, after=()):
        waits = self.held + [m for m in after if m is not None]
        self.held = []
        arrival.count += 16
        self.steps.append((waits, lambda e: e.dma_start(out, in_), arrival.sem, 16))
        return (arrival.sem, arrival.count)

    def emit(self, eng):
        passed = {}
        for waits, step, sem, by in self.steps:
            for s, v in waits:
                if passed.get(s.name, 0) < v:
                    eng.wait_ge(s, v)
                    passed[s.name] = v
            step(eng).then_inc(sem, by)


class Arrival:

    def __init__(self, sem):
        self.sem, self.count = sem, 0


class Region:

    def __init__(self, whole, lo, hi):
        self.whole, self.at, self.hi, self.peak = whole, lo, hi, lo

    def take(self, words, parts=P):
        lo = self.at
        self.at += words
        self.peak = max(self.peak, self.at)
        assert self.at <= self.hi, (self.at, self.hi)
        return self.whole[0:parts, lo:lo + words]


def build(nc, t, out):
    from contextlib import ExitStack
    ctx = ExitStack()
    with ctx:
        def sem(name):
            return ctx.enter_context(nc.semaphore(name))

        WORDS = 52600
        sb = ctx.enter_context(nc.sbuf_tensor("arena", [P, WORDS], F32))
        ps = ctx.enter_context(nc.psum_tensor("banks", [P, 4096], F32))
        arena = Region(sb, 0, WORDS)

        pe, act, dve, pool, sp = (Lane(sem("pe_done"), False), Lane(sem("act_done"), True),
                                  Lane(sem("dve_done"), True), Lane(sem("pool_done"), True),
                                  Lane(sem("sp_done"), False))
        lanes = [pe, act, dve, pool, sp]
        act.partner, dve.partner = dve, act
        arrivals = []

        def arrival(name):
            a = Arrival(sem(name))
            arrivals.append(a)
            return a

        def now():
            return [(l.sem, l.count) for l in lanes if l.count] + \
                   [(a.sem, a.count) for a in arrivals if a.count]

        def fence():
            marks = now()
            for l in lanes:
                l.held = list(marks)

        def tt(o, a, b, op, after=(), chain=True):
            return dve.do(lambda e: e.tensor_tensor(o, a, b, op), after, chain)

        def ts(o, a, s1, s2, op0, op1=None, after=(), chain=True):
            if op1 is None:
                return dve.do(lambda e: e.tensor_scalar(o, a, s1, None, op0), after, chain)
            return dve.do(lambda e: e.tensor_scalar(o, a, s1, s2, op0, op1), after, chain)

        def stt(o, a, s, b, op0, op1, after=(), chain=True):
            return dve.do(lambda e: e.scalar_tensor_tensor(o, a, s, b, op0, op1), after, chain)

        def scan(o, a, b, init, op0, op1, after=()):
            return dve.do(lambda e: e.tensor_tensor_scan(o, a, b, init, op0, op1), after)

        def vcopy(o, a, after=(), chain=True):
            return dve.do(lambda e: e.tensor_copy(o, a), after, chain)

        def red(o, a, op, after=(), negate=False):
            return dve.do(lambda e: e.tensor_reduce(o, a, AX, op, negate=negate), after)

        def rec(o, a, after=()):
            return dve.do(lambda e: e.reciprocal(o, a), after)

        def vset(o, v, after=()):
            return dve.do(lambda e: e.memset(o, v), after)

        def fn(o, a, f, after=(), chain=True, **k):
            return act.do(lambda e: e.activation(o, a, f, **k), after, chain)

        def acopy(o, a, after=(), chain=True):
            return act.do(lambda e: e.activation(o, a, ACT.Copy), after, chain)

        def mm(out_, pairs, after=()):
            mark = None
            for n, (l, r) in enumerate(pairs):
                first, last = n == 0, n == len(pairs) - 1
                mark = pe.do(lambda e, l=l, r=r, f=first, z=last: e.matmul(out_, l, r, start=f, stop=z),
                             after if first else ())
            return mark

        def tr(out_, in_, after=()):
            n = in_.shape[0]
            lo = in_.start_partition if isinstance(in_.start_partition, int) else in_.start_partition()
            return pe.do(lambda e: e.transpose(out_, in_, ident[lo:lo + n, lo:lo + n]), after)

        def bank(n, width=512):
            return ps[:, 512 * n:512 * n + width]

        class Banks:

            def __init__(self, banks):
                self.banks, self.n, self.free = banks, 0, {b: None for b in banks}

            def take(self):
                b = self.banks[self.n % len(self.banks)]
                self.n += 1
                return b, self.free[b]

        class Slots:

            def __init__(self, name, words, n, lane):
                self.bufs = [arena.take(words) for _ in range(n)]
                self.arr = [arrival(f"{name}{i}") for i in range(n)]
                self.n, self.free, self.lane = 0, [None] * n, lane

            def load(self, shape, sources, parts=P):
                i = self.n % len(self.bufs)
                self.n += 1
                v = shape(self.bufs[i])
                mark = None
                for pick, src in sources:
                    mark = self.lane.dma(pick(v), src, self.arr[i], [self.free[i]])
                return i, v, mark

        a_const = arrival("const_landed")
        cf = arena.take(t["c_f32"].shape[1])
        sp.dma(cf, t["c_f32"], a_const)
        ident = cf[:, 0:128]
        ones = cf[:, 128:256]
        scanmask = cf[:, 256:1280]
        at = 1280
        onehot = cf[0:4, at:at + 512].rearrange("p (h c) -> p h c", h=4)
        at += 512
        ov = cf[:, at:at + 16]
        at += 16
        iota8 = cf[:, at:at + 8]
        at += 8
        iota4 = iota8[:, 0:4]
        nb = t["c_bf16"].shape[1] // 2
        cb = arena.take(nb).bitcast(BF16)
        sp.dma(cb, t["c_bf16"], a_const)
        ident_b = cb[:, 0:128]
        causal_n = cb[:, 128:256]
        causal_t = cb[:, 256:384]
        win_mask = cb[:, 384:768]
        swa_mask = cb[:, 768:1024]
        win_l = cb[0:6, 1024:1152]
        win_r = cb[0:6, 1152:1152 + 8 * 384].rearrange("p (h c) -> p h c", h=8)
        swa_r = cb[0:6, 4224:4224 + 8 * 384].rearrange("p (h c) -> p h c", h=8)
        m8 = arena.take(512).bitcast(BF16)
        sp.dma(m8, t["c_mask"], a_const)
        level_mask = m8.bitcast(mybir.dt.uint16).rearrange("p (l c) -> p l c", l=8)
        small = {}
        for name in ("g1pre", "g2pre", "gmix", "gffn", "gmoe", "lam", "s5d", "ldt", "lbl", "convw",
                     "gate_b", "sinks", "pos_k", "pos_v"):
            a = t[name]
            v = arena.take(a.shape[1], a.shape[0])
            sp.dma(v, a, a_const)
            small[name] = v
        consts = (a_const.sem, a_const.count)
        for l in (pe, act, dve, pool):
            l.held = [consts]

        XW = arena.take(NT * D)
        X = XW.rearrange("p (t d) -> p t d", t=NT)
        aTW = arena.take(KD * S)
        aT = aTW.rearrange("p (k s) -> p k s", k=KD)
        stat = arena.take(1024)
        base = arena.at

        def rstd_of(dst, src, n, after=()):
            ts(dst, src, 1.0 / n, EPS, ALU.mult, ALU.add, after)
            fn(dst, dst, ACT.Ln, [(dve.sem, dve.count)])
            return fn(dst, dst, ACT.Exp, scale=-0.5)

        def norm_to_T(gain, ready, scratch):
            ring = Banks([0, 1, 2, 3])
            ss, rs = stat[:, 0:NT], stat[:, NT:2 * NT]
            for i in range(NT):
                m = act.do(lambda e, i=i: e.activation(scratch[:, 0:D], X[:, i, :], ACT.Square,
                                                       accum_out=ss[:, i:i + 1]), [ready[i]])
            r = rstd_of(rs, ss, D, [m])
            for i in range(NT):
                xs = scratch[:, D * (1 + i % 2):D * (2 + i % 2)]
                m = ts(xs, X[:, i, :], rs[:, i:i + 1], None, ALU.mult,
                       after=[r, norm_to_T.read[i % 2]])
                for half in range(2):
                    b, freed = ring.take()
                    for q in range(4):
                        k = 4 * half + q
                        mt = tr(bank(b)[:, P * q:P * q + P], xs[:, P * k:P * k + P], [m, freed])
                    g = gain[:, 4 * half:4 * half + 4].unsqueeze(2).broadcast_to([P, 4, P])
                    ring.free[b] = tt(aT[:, 4 * half:4 * half + 4, P * i:P * i + P],
                                      bank(b).rearrange("p (q c) -> p q c", q=4), g, ALU.mult, [mt])
                norm_to_T.read[i % 2] = mt
            norm_to_T.read = [None, None]
            return ring.free[b]

        norm_to_T.read = [None, None]

        a_x = [arrival(f"x{i}_landed") for i in range(NT)]
        xin = t["x"].rearrange("(t p) d -> t p d", p=P)
        ready = [sp.dma(X[:, i, :], xin[i], a_x[i]) for i in range(NT)]
        sp.held = []
        scratch = arena.take(3 * D)
        a_ready = norm_to_T(small["g1pre"], ready, scratch)
        fence()
        arena.at = base
        yT = XW.rearrange("p (k s) -> p k s", k=KD)

        wslots = Slots("w_landed", 2048, 2, sp)
        base_w = arena.at
        proj_banks = Banks([0, 1, 2, 3])
        turn = [0]

        def evac(o, i, after):
            turn[0] += 1
            return acopy(o, i, after) if turn[0] % 2 else vcopy(o, i, after)

        def w_load(w, cols):
            src = w.rearrange("(k p) c -> p k c", p=P)
            picks, at_ = [], 0
            for c, n in cols:
                picks.append((lambda v, a=at_, n=n: v[:, :, a:a + n], src[:, :, c:c + n]))
                at_ += n
            return wslots.load(lambda b: b[:, 0:KD * at_].rearrange("p (k c) -> p k c", k=KD), picks)

        def proj_T(w, cols, dsts):
            slot, wv, landed = w_load(w, cols)
            for m, dst in enumerate(dsts):
                for n in range(2):
                    b, freed = proj_banks.take()
                    mk = mm(bank(b), [(wv[:, k, P * m:P * m + P], aT[:, k, 512 * n:512 * n + 512])
                                      for k in range(KD)], [landed, freed])
                    proj_banks.free[b] = e = evac(dst[:, 512 * n:512 * n + 512], bank(b), [mk])
            wslots.free[slot] = mk
            return e

        def proj_N(w, cols, put):
            width = sum(n for _, n in cols)
            slot, wv, landed = w_load(w, cols)
            for i in range(NT):
                b, freed = proj_banks.take()
                mk = mm(bank(b, width), [(aT[:, k, P * i:P * i + P], wv[:, k, :]) for k in range(KD)],
                        [landed, freed])
                proj_banks.free[b] = e = evac(put(i, bank(b, width))[0], put(i, bank(b, width))[1], [mk])
            wslots.free[slot] = mk
            return e

        def v2(w, a="a"):
            return w.rearrange("p (a s) -> p a s", a=2)

        def sigmoid_(o, i, tmp=None):
            fn(o, i, ACT.Exp, now(), scale=-1.0)
            ts(o, o, 1.0, None, ALU.add, after=[(act.sem, act.count)])
            return rec(o, o)

        def head_norm_gate(o, sq, gate, col, extra):
            ss = stat[:, 64:96]
            m = tt(sq, o, o, ALU.mult, now())
            red(ss, sq.rearrange("p (n c) -> p n c", c=64), ALU.add)
            r = rstd_of(ss, ss, 64)
            ov_ = o.rearrange("p (n c) -> p n c", c=64)
            m = tt(ov_, ov_, ss.unsqueeze(2).broadcast_to([P, 32, 64]), ALU.mult, [r])
            if gate is not None:
                m = tt(o, o, gate, ALU.mult)
            o3 = o.rearrange("p (t c) -> p t c", t=NT)
            for f in range(2):
                for n in range(2):
                    b, freed = proj_banks.take()
                    for q in range(4):
                        mt = tr(bank(b)[:, P * q:P * q + P], o3[:, 4 * n + q, P * f:P * f + P], [m, freed])
                    proj_banks.free[b] = ts(yT[:, col + f, 512 * n:512 * n + 512], bank(b),
                                            small["gmix"][:, col + f:col + f + 1], None, ALU.mult,
                                            after=[mt])

        w_in = t["w_in"]

        u = arena.take(2 * S)
        uT = v2(u)
        proj_T(w_in, [(IN1["s5"], 256)], [uT[:, 0], uT[:, 1]])
        lam = small["lam"]
        lr, li = lam[:, 0:8], lam[:, 8:16]
        w8 = arena.take(8 * 16)
        sl = lambda n: w8[:, 8 * n:8 * n + 8]
        dt_, mag, cs, sn, th, kk, den, cfr, cfi, tmp, abr, abi, lrc, tm2 = (sl(n) for n in range(14))
        fn(dt_, small["ldt"], ACT.Exp)
        ts(lrc, lr, -1e-4, None, ALU.min)
        tt(tmp, lrc, dt_, ALU.mult, [(act.sem, act.count)])
        fn(mag, tmp, ACT.Exp, [(dve.sem, dve.count)])
        tt(th, li, dt_, ALU.mult)
        ts(kk, th, 1.0 / TWO_PI, ROUND, ALU.mult, ALU.add)
        ts(kk, kk, ROUND, None, ALU.subtract)
        for part in (6.28125, 0.0019350051879882812, 3.019916e-07):
            stt(th, kk, -part, th, ALU.mult, ALU.add)
        ts(th, th, 3.1415925, -3.1415925, ALU.min, ALU.max)
        stt(tmp, th, -1.0, th, ALU.mult, ALU.max)
        ts(tmp, tmp, -1.0, TWO_PI / 4, ALU.mult, ALU.add)
        fn(sn, th, ACT.Sin, [(dve.sem, dve.count)])
        m = fn(cs, tmp, ACT.Sin)
        tt(abr, mag, cs, ALU.mult, [m])
        tt(abi, mag, sn, ALU.mult)
        tt(den, lrc, lrc, ALU.mult)
        tt(tmp, li, li, ALU.mult)
        tt(den, den, tmp, ALU.add)
        rec(den, den)
        ts(tm2, abr, -1.0, None, ALU.add)
        tt(cfr, tm2, lrc, ALU.mult)
        tt(tmp, abi, li, ALU.mult)
        tt(cfr, cfr, tmp, ALU.add)
        tt(cfr, cfr, den, ALU.mult)
        tt(cfi, abi, lrc, ALU.mult)
        tt(tmp, tm2, li, ALU.mult)
        tt(cfi, cfi, tmp, ALU.subtract)
        tt(cfi, cfi, den, ALU.mult)
        braw = arena.take(4 * 256)
        a_s5 = arrival("s5_params_landed")
        bR, bI, cR, cI = (braw[:, 256 * n:256 * n + 256] for n in range(4))
        for n, nm in enumerate(("b_re", "b_im", "c_re", "c_im")):
            s5l = sp.dma(braw[:, 256 * n:256 * n + 256], t[nm], a_s5)
        glu = arena.take(512).rearrange("p (k c) -> p k c", k=2)
        s5l = sp.dma(glu, t["w_glu"].rearrange("(k p) c -> p k c", p=P), a_s5)
        bb = arena.take(512)
        bt = arena.take(512)
        tb = arena.take(256)
        r3 = lambda a: a.rearrange("p (j c) -> p j c", j=8)
        bc = lambda a: a.unsqueeze(2).broadcast_to([P, 8, 32])
        tt(r3(bb[:, 0:256]), r3(bR), bc(cfr), ALU.mult, [s5l])
        tt(r3(tb), r3(bI), bc(cfi), ALU.mult)
        tt(bb[:, 0:256], bb[:, 0:256], tb, ALU.subtract)
        tt(r3(bb[:, 256:512]), r3(bI), bc(cfr), ALU.mult)
        tt(r3(tb), r3(bR), bc(cfi), ALU.mult)
        tt(bb[:, 256:512], bb[:, 256:512], tb, ALU.add)
        m = ts(cI, cI, -1.0, None, ALU.mult)
        for q in range(4):
            mt = tr(bank(4)[:, P * q:P * q + P], bb[:, P * q:P * q + P], [m])
        m_bt = vcopy(bt, bank(4), [mt])
        s5_y = arena.take(2 * S)
        yS = v2(s5_y)
        cos_t, sin_t, zr, zi, t1, t2, br_, bi_ = (arena.take(S) for _ in range(8))
        fence()
        for j in range(8):
            f, r0 = j // 4, 32 * (j % 4)
            c0 = vset(cos_t[:, 0:1], 1.0)
            vset(sin_t[:, 0:1], 0.0)
            cn, s_n = cs[:, j:j + 1], sn[:, j:j + 1]
            n = 1
            while n < S:
                if n > 1:
                    tt(tmp[:, 0:1], cos_t[:, n - 1:n], cs[:, j:j + 1], ALU.mult)
                    tt(tm2[:, 0:1], sin_t[:, n - 1:n], sn[:, j:j + 1], ALU.mult)
                    tt(kk[:, 0:1], tmp[:, 0:1], tm2[:, 0:1], ALU.subtract)
                    tt(tmp[:, 0:1], sin_t[:, n - 1:n], cs[:, j:j + 1], ALU.mult)
                    tt(tm2[:, 0:1], cos_t[:, n - 1:n], sn[:, j:j + 1], ALU.mult)
                    tt(kk[:, 1:2], tmp[:, 0:1], tm2[:, 0:1], ALU.add)
                    cn, s_n = kk[:, 0:1], kk[:, 1:2]
                ts(t1[:, 0:n], sin_t[:, 0:n], s_n, None, ALU.mult)
                stt(cos_t[:, n:2 * n], cos_t[:, 0:n], cn, t1[:, 0:n], ALU.mult, ALU.subtract)
                ts(t1[:, 0:n], cos_t[:, 0:n], s_n, None, ALU.mult)
                stt(sin_t[:, n:2 * n], sin_t[:, 0:n], cn, t1[:, 0:n], ALU.mult, ALU.add)
                n *= 2
            for n in range(2):
                cols = slice(512 * n, 512 * n + 512)
                rhs = uT[r0:r0 + 32, f, cols]
                before = now()
                mm(bank(4), [(bt[r0:r0 + 32, P * f:P * f + P], rhs)], before)
                mk = mm(bank(5), [(bt[r0:r0 + 32, 256 + P * f:256 + P * f + P], rhs)])
                acopy(br_[:, cols], bank(4), [mk])
                acopy(bi_[:, cols], bank(5))
            tt(t1, cos_t, br_, ALU.mult, now())
            tt(t2, sin_t, bi_, ALU.mult)
            tt(t1, t1, t2, ALU.add)
            tt(t2, cos_t, bi_, ALU.mult)
            tt(zi, sin_t, br_, ALU.mult)
            tt(t2, t2, zi, ALU.subtract)
            mg = mag[:, j:j + 1].broadcast_to([P, S])
            scan(zr, mg, t1, 0.0, ALU.mult, ALU.add)
            scan(zi, mg, t2, 0.0, ALU.mult, ALU.add)
            tt(t1, cos_t, zr, ALU.mult)
            tt(t2, sin_t, zi, ALU.mult)
            tt(br_, t1, t2, ALU.subtract)
            tt(t1, sin_t, zr, ALU.mult)
            tt(t2, cos_t, zi, ALU.mult)
            m = tt(bi_, t1, t2, ALU.add)
            for n in range(2):
                cols = slice(512 * n, 512 * n + 512)
                o = ps[r0:r0 + 32, 512 * (6 + n):512 * (7 + n)]
                mk = mm(o, [(cR[:, 32 * j:32 * j + 32], br_[:, cols]),
                            (cI[:, 32 * j:32 * j + 32], bi_[:, cols])], [m] + now())
            if j % 4 == 3:
                for n in range(2):
                    cols = slice(512 * n, 512 * n + 512)
                    m = stt(yS[:, f, cols], uT[:, f, cols], small["s5d"][:, f:f + 1], bank(6 + n),
                            ALU.mult, ALU.add, [mk])
        fence()
        g_, q_ = arena.take(2 * S), arena.take(2 * S)
        tt(g_, s5_y, s5_y, ALU.mult)
        ts(g_, g_, 0.044715, 1.0, ALU.mult, ALU.add)
        tt(g_, g_, s5_y, ALU.mult)
        ts(g_, g_, -2.0 * 0.7978845608028654, 80.0, ALU.mult, ALU.min)
        fn(g_, g_, ACT.Exp)
        ts(g_, g_, 1.0, None, ALU.add)
        rec(g_, g_)
        m = tt(g_, g_, s5_y, ALU.mult)
        gT = v2(g_)
        qT = v2(q_)
        for f in range(2):
            for n in range(2):
                b, freed = proj_banks.take()
                mk = mm(bank(b), [(glu[:, k, P * f:P * f + P], gT[:, k, 512 * n:512 * n + 512])
                                  for k in range(2)], [m, freed])
                proj_banks.free[b] = acopy(qT[:, f, 512 * n:512 * n + 512], bank(b), [mk])
        sigmoid_(q_, q_)
        tt(g_, g_, q_, ALU.mult)
        m = tt(q_, g_, g_, ALU.mult)
        for n in range(2):
            b, freed = proj_banks.take()
            mk = mm(bank(b), [(ones, qT[:, k, 512 * n:512 * n + 512]) for k in range(2)], [m, freed])
            rr = t1[:, 0:512]
            r = rstd_of(rr, bank(b), GW, [mk])
            proj_banks.free[b] = r
            for f in range(2):
                stt(yT[:, f, 512 * n:512 * n + 512], gT[:, f, 512 * n:512 * n + 512],
                    small["gmix"][:, f:f + 1], rr, ALU.mult, ALU.mult, [r])
        fence()
        arena.at = base_w

        hq, hz, hv = (arena.take(2 * S) for _ in range(3))
        proj_T(w_in, [(IN1["hq"], 256)], [v2(hq)[:, 0], v2(hq)[:, 1]])
        proj_T(w_in, [(IN1["hf"], 256)], [v2(hz)[:, 0], v2(hz)[:, 1]])
        hv3 = hv.rearrange("p (t c) -> p t c", t=NT)
        proj_N(w_in, [(IN1["hi"], 256)], lambda i, b: (hv3[:, i, :], b))
        hb, hk, hE = (arena.take(2 * S) for _ in range(3))
        Z = [arena.take(2 * S), hz]
        lb = stat[:, 128:130]
        lbp = stat[:, 130:132]
        tt(lb, small["lbl"], small["lbl"], ALU.subtract)
        fn(lbp, lb, ACT.Exp, [(dve.sem, dve.count)])
        rec(lb, lbp, [(act.sem, act.count)])
        tt(lbp, lbp, lb, ALU.mult)
        tt(lb, lbp, lbp, ALU.subtract)
        ts(lb, lb, 0.0, None, ALU.max)
        ts(lbp, lb, -1.0, 1.0, ALU.mult, ALU.add)
        stt(hE, hz, -1.0, hz, ALU.mult, ALU.max, now())
        fn(hE, hE, ACT.Exp, [(dve.sem, dve.count)], scale=-1.0)
        m = fn(hE, hE, ACT.Ln, bias=1.0)
        stt(hE, hz, 0.0, hE, ALU.min, ALU.subtract, [m])
        m = tt(hk, hE, hz, ALU.subtract)
        fn(hk, hk, ACT.Exp, [m])
        ts(hb, hz, -1.0, 60.0, ALU.mult, ALU.min)
        fn(hb, hb, ACT.Exp, [(dve.sem, dve.count)])
        m = (act.sem, act.count)
        for f in range(2):
            ts(v2(hb)[:, f], v2(hb)[:, f], lb[:, f:f + 1], None, ALU.mult, after=[m])
            ts(v2(hk)[:, f], v2(hk)[:, f], lbp[:, f:f + 1], None, ALU.mult)
        m = fn(hb, hb, ACT.Ln, [(dve.sem, dve.count)], bias=1.0)
        tt(hE, hE, hb, ALU.add, [m])
        for f in range(2):
            scan(v2(hb)[:, f], scanmask, v2(hE)[:, f], 0.0, ALU.mult, ALU.add)
        b3 = hb.rearrange("p (n c) -> p n c", c=P)
        E3 = hE.rearrange("p (n c) -> p n c", c=P)
        qb = Z[0]
        dec = stat[:, 132:148]
        m = fn(hE, hb, ACT.Exp, [(dve.sem, dve.count)])
        m = fn(dec, b3[:, :, P - 1:P].rearrange("p n c -> p (n c)"), ACT.Exp)
        tt(qb, hq, hE, ALU.mult, [m])
        tt(E3, b3, b3[:, :, P - 1:P].broadcast_to([P, 16, P]), ALU.subtract)
        m = fn(hE, hE, ACT.Exp, [(dve.sem, dve.count)], scale=-1.0)
        kb = hz
        m = tt(kb, hk, hE, ALU.mult, [m])
        kN = arena.take(2 * S)
        kN3 = kN.rearrange("p (t c) -> p t c", t=NT)
        kb3 = v2(kb)
        for c in range(NT):
            b, freed = proj_banks.take()
            for f in range(2):
                mt = tr(bank(b)[:, P * f:P * f + P], kb3[:, f, P * c:P * c + P], [m, freed])
            proj_banks.free[b] = e = evac(kN3[:, c, :], bank(b, 256), [mt])
        kb_read = mt
        U4 = ps[:, 2048:3072].rearrange("p (c f v) -> p c f v", c=8, f=2)
        before = now()
        for c in range(NT - 1):
            for h in range(4):
                mk = mm(ps[64 * (h % 2):64 * (h % 2) + 64, 2048 + 128 * c + 64 * (h // 2):
                           2048 + 128 * c + 64 * (h // 2) + 64],
                        [(kN3[:, c, 64 * h:64 * h + 64], hv3[:, c, 64 * h:64 * h + 64])], before)
        Sh = arena.take(1024).rearrange("p (c f v) -> p c f v", c=8, f=2)
        vset(Sh[:, 0], 0.0)
        dec2 = dec.rearrange("p (f c) -> p f c", f=2)
        for c in range(NT - 1):
            for f in range(2):
                m_state = stt(Sh[:, c + 1, f, :], Sh[:, c, f, :], dec2[:, f, c:c + 1], U4[:, c, f, :],
                              ALU.mult, ALU.add, [mk])
        acc = arena.take(8 * 512)
        acc5 = acc.rearrange("p (r c f t) -> p r c f t", r=2, c=8, f=2)
        vset(acc, 0.0)
        sbanks = Banks([0, 1, 2, 3])
        o_n = kN
        o3 = o_n.rearrange("p (t c) -> p t c", t=NT)
        inter = Banks([6, 7])
        o_int = arena.take(2 * S)
        oi3 = o_int.rearrange("p (t c) -> p t c", t=NT)
        qb3 = v2(qb)
        oi5 = o_int.rearrange("p (t f r c) -> p t f r c", t=NT, f=2, r=2)
        for c0 in range(0, NT, 4):
            for r in range(2):
                b, freed = inter.take()
                r0 = 64 * r
                for c in range(c0, c0 + 4):
                    for f in range(2):
                        mk = mm(bank(b)[:, 128 * (c - c0) + 64 * f:128 * (c - c0) + 64 * f + 64],
                                [(qb3[r0:r0 + 64, f, P * c:P * c + P], Sh[r0:r0 + 64, c, f, :])],
                                [m_state, freed, m])
                inter.free[b] = evac(oi5[:, c0:c0 + 4, :, r, :],
                                     bank(b).rearrange("p (t f c) -> p t f c", t=4, f=2), [mk])
        z_read = [mk, kb_read]
        hk3, hq3 = v2(hk), v2(hq)
        for level in range(LEVELS + 1):
            if level < LEVELS:
                H = 1 << level
                Zl = Z[(level + 1) % 2]
                nb_ = 2 * S // (2 * H)
                bl = hb.rearrange("p (n c) -> p n c", c=2 * H)
                El = hE.rearrange("p (n c) -> p n c", c=2 * H)
                Zv = Zl.rearrange("p (n c) -> p n c", c=2 * H)
                kv = hk.rearrange("p (n c) -> p n c", c=2 * H)
                qv = hq.rearrange("p (n c) -> p n c", c=2 * H)
                m = tt(El, bl, bl[:, :, H - 1:H].broadcast_to([P, nb_, 2 * H]), ALU.subtract,
                       [(act.sem, act.count)])
                fn(El[:, :, 0:H], El[:, :, 0:H], ACT.Exp, [m], scale=-1.0)
                m = fn(El[:, :, H:2 * H], El[:, :, H:2 * H], ACT.Exp)
                tt(Zv[:, :, 0:H], El[:, :, 0:H], kv[:, :, 0:H], ALU.mult, [m, z_read[(level + 1) % 2]])
                m = tt(Zv[:, :, H:2 * H], El[:, :, H:2 * H], qv[:, :, H:2 * H], ALU.mult)
                left = right = v2(Zl)
            else:
                left, right = hk3, hq3
            for c0 in range(0, NT, 2):
                for r in range(2):
                    b, freed = sbanks.take()
                    r0 = 64 * r
                    for q in range(4):
                        c, f = c0 + q // 2, q % 2
                        mk = mm(bank(b)[:, P * q:P * q + P],
                                [(left[r0:r0 + 64, f, P * c:P * c + P],
                                  right[r0:r0 + 64, f, P * c:P * c + P])], [m, freed])
                    msk = level_mask[:, level:level + 1, :].broadcast_to([P, 4, P])
                    dst = acc5[:, r, c0:c0 + 2].rearrange("p c f t -> p (c f) t")
                    sbanks.free[b] = m_acc = dve.do(
                        lambda e, dst=dst, b=b, msk=msk: e.copy_predicated(
                            dst, msk, bank(b).rearrange("p (h t) -> p h t", h=4)), [mk])
            z_read[(level + 1) % 2] = mk
        for c in range(NT):
            b, freed = inter.take()
            for h in range(4):
                mk = mm(bank(b)[:, 64 * h:64 * h + 64],
                        [(acc5[:, h % 2, c, h // 2, :], hv3[:, c, 64 * h:64 * h + 64])], [m_acc, freed])
            inter.free[b] = tt(o3[:, c, :], oi3[:, c, :], bank(b, 256), ALU.add,
                               [mk, (act.sem, act.count)])
        fence()
        hgt = hb
        hg3 = hgt.rearrange("p (t c) -> p t c", t=NT)
        proj_N(w_in, [(IN1["hg"], 256)], lambda i, b: (hg3[:, i, :], b))
        sigmoid_(hE, hgt)
        tt(hgt, hgt, hE, ALU.mult)
        head_norm_gate(o_n, hE, hgt, 2, None)
        fence()
        arena.at = base_w

        gates = arena.take(NT * 12)
        g3 = gates.rearrange("p (t c) -> p t c", t=NT)
        proj_N(w_in, [(IN1["ff"], 4), (IN1["mi"], 8)], lambda i, b: (g3[:, i, :], b))
        rows = arena.take(7 * S, 4)
        fF, wI, mM, lF, tR, sR, zR = (rows[:, S * n:S * n + S] for n in range(7))
        gb = small["gate_b"]

        def gate_rows(dst, c0, bias):
            for n in range(2):
                b, freed = proj_banks.take()
                for q in range(4):
                    mt = tr(bank(b)[0:4, P * q:P * q + P], g3[:, 4 * n + q, c0:c0 + 4], [freed] + now())
                proj_banks.free[b] = ts(dst[:, 512 * n:512 * n + 512], bank(b)[0:4], bias, None,
                                        ALU.add, after=[mt])

        def log_sigmoid_rows(dst, src):
            stt(sR, src, -1.0, src, ALU.mult, ALU.max, now())
            fn(sR, sR, ACT.Exp, [(dve.sem, dve.count)], scale=-1.0)
            m = fn(sR, sR, ACT.Ln, bias=1.0)
            return stt(dst, src, 0.0, sR, ALU.min, ALU.subtract, [m])

        onesrow = zR
        vset(onesrow, 1.0)
        gate_rows(tR, 0, gb[:, 0:1])
        log_sigmoid_rows(tR, tR)
        scan(fF, onesrow, tR, 0.0, ALU.mult, ALU.add)
        ts(fF, fF, -8.0, None, ALU.mult)
        gate_rows(tR, 8, gb[:, 2:3])
        log_sigmoid_rows(tR, tR)
        scan(lF, onesrow, tR, 0.0, ALU.mult, ALU.add)
        gate_rows(tR, 4, gb[:, 1:2])
        tt(wI, tR, lF, ALU.subtract)
        ts(sR, wI, 0.0, None, ALU.mult)
        scan(mM, sR, wI, 0.0, ALU.add, ALU.max)
        ts(tR, mM, -1.0, None, ALU.mult)
        tt(sR, mM, lF, ALU.add)
        m = fn(sR, sR, ACT.Exp, [(dve.sem, dve.count)], scale=-1.0)
        wN = arena.take(32).rearrange("p (t h) -> p t h", t=NT)
        eN = arena.take(32).rearrange("p (t h) -> p t h", t=NT)
        before = now()
        for src, o in ((wI, wN), (sR, eN)):
            b, freed = proj_banks.take()
            for i in range(NT):
                mt = tr(bank(b)[:, 4 * i:4 * i + 4], src[:, P * i:P * i + P], before + [freed])
            proj_banks.free[b] = vcopy(o.rearrange("p t h -> p (t h)"), bank(b, 32), [mt])
        base_g = arena.at

        class Attention:

            def __init__(self):
                self.Pm = [arena.take(S) for _ in range(2)]
                self.PT = [arena.take(S) for _ in range(2)]
                self.mneg, self.z = arena.take(64), arena.take(64)
                self.s_free, self.p_free, self.pt_free = [None] * 2, [None] * 2, [None] * 2
                self.t_ring = Banks([4, 5])
                self.n = 0

            def run(self, units, finish, ready):
                Lane.turns = False
                self.run_(units, finish, ready)
                Lane.turns = True

            def run_(self, units, finish, ready):
                pending = None
                o_free = [None, None]
                for u_ in list(units) + [None]:
                    cur = None
                    if u_ is not None:
                        cur = self.scores(u_, ready)
                    if pending is not None:
                        self.values(pending, o_free, finish)
                    pending = cur

            def scores(self, u_, ready):
                p = self.n % 2
                slot = self.n % 64
                self.n += 1
                w = u_["width"]
                so = 1024 * p
                first = [self.s_free[p]] + ready
                for c0 in range(0, w, 512):
                    c1 = min(w, c0 + 512)
                    pairs = [(u_["q"], u_["k"](c0, c1))]
                    o = ps[:, so + c0:so + c1]
                    extra = u_["bias"](c0, c1)
                    total = 1 + len(extra)
                    mk = pe.do(lambda e, o=o, a=pairs[0], z=total == 1: e.matmul(
                        o, a[0], a[1], start=True, stop=z), first)
                    for n, (lo, hi, l, r) in enumerate(extra):
                        oo = ps[:, so + lo:so + hi]
                        mk = pe.do(lambda e, oo=oo, l=l, r=r, z=n == total - 2: e.matmul(
                            oo, l, r, start=False, stop=z))
                sc = ps[:, so:so + w]
                mn, zz = self.mneg[:, slot:slot + 1], self.z[:, slot:slot + 1]
                if u_.get("sink") is None:
                    red(mn, sc, ALU.max, [mk], negate=True)
                    m = ts(mn, mn, 0.125, None, ALU.mult)
                else:
                    red(mn, sc, ALU.max, [mk])
                    ts(mn, mn, 0.125, u_["sink"], ALU.mult, ALU.max)
                    m = ts(mn, mn, -1.0, None, ALU.mult)
                Pm = self.Pm[p]
                e_ = act.do(lambda e: e.activation(Pm[:, 0:w], sc, ACT.Exp, bias=mn, scale=0.125,
                                                   accum_out=zz), [m, mk, self.p_free[p]])
                self.s_free[p] = e_
                if u_.get("sink") is not None:
                    sk = stat[:, 200 + p:201 + p]
                    k_ = fn(sk, u_["sink"], ACT.Exp, [m], bias=mn)
                    tt(zz, zz, sk, ALU.add, [k_])
                    rec(zz, zz)
                else:
                    rec(zz, zz, [e_])
                return dict(u=u_, p=p, slot=slot, e=e_)

            def values(self, c, o_free, finish):
                u_, p = c["u"], c["p"]
                nbk = u_["width"] // P
                Pm, PT = self.Pm[p], self.PT[p]
                ev = []
                for b0 in range(0, nbk, 4):
                    n = min(4, nbk - b0)
                    b, freed = self.t_ring.take()
                    for q in range(n):
                        mt = tr(bank(b)[:, P * q:P * q + P], Pm[:, P * (b0 + q):P * (b0 + q) + P],
                                [c["e"], freed])
                    self.t_ring.free[b] = e_ = evac(PT[:, P * b0:P * (b0 + n)], bank(b, P * n),
                                                    [mt, self.pt_free[p]])
                    ev.append(e_)
                self.p_free[p] = mt
                ob = u_["tile"] % 2
                col = 512 * (6 + ob) + 64 * u_["head"]
                mk = mm(ps[:, col:col + 64], [(PT[:, P * n:P * n + P], u_["v"](n)) for n in range(nbk)],
                        ev + [o_free[ob]])
                self.pt_free[p] = mk
                if u_["last"]:
                    n = self_heads = u_["heads"]
                    lo = c["slot"] - n + 1
                    o_free[ob] = finish(u_["tile"], ps[:, 512 * (6 + ob):512 * (6 + ob) + 64 * n],
                                        self.z[:, lo:lo + n], [mk])

        fq, fk, fv = (arena.take(2 * S) for _ in range(3))
        fv3 = fv.rearrange("p (t c) -> p t c", t=NT)
        proj_T(w_in, [(IN1["fq"], 256)], [v2(fq)[:, 0], v2(fq)[:, 1]])
        proj_T(w_in, [(IN1["fk"], 256)], [v2(fk)[:, 0], v2(fk)[:, 1]])
        proj_N(w_in, [(IN1["fv"], 256)], lambda i, b: (fv3[:, i, :], b))
        o_f = arena.take(2 * S)
        of3 = o_f.rearrange("p (t c) -> p t c", t=NT)
        att = Attention()
        fq3, fk3 = v2(fq), v2(fk)
        fence()

        def fox_unit(i, h):
            r0, f = 64 * (h % 2), h // 2
            w = P * (i + 1)

            def bias(c0, c1):
                got = [(c0, c1, onehot[:, h, :], fF[:, c0:c1])]
                if c1 == w:
                    got.append((w - P, w, ident_b, causal_n))
                return got

            return dict(q=fq3[r0:r0 + 64, f, P * i:P * i + P],
                        k=lambda c0, c1: fk3[r0:r0 + 64, f, c0:c1], width=w, bias=bias,
                        v=lambda n: fv3[:, n, 64 * h:64 * h + 64], tile=i, head=h, heads=4,
                        last=h == 3)

        def fox_finish(i, o, rz, after):
            return tt(of3[:, i, :].rearrange("p (h c) -> p h c", h=4),
                      o.rearrange("p (h c) -> p h c", h=4), rz.unsqueeze(2).broadcast_to([P, 4, 64]),
                      ALU.mult, after)

        att.run([fox_unit(i, h) for i in range(NT) for h in range(4)], fox_finish, [])
        fence()
        head_norm_gate(o_f, fq, None, 4, None)
        fence()
        arena.at = base_g

        mq, mk_, cq, ck, mtmp = (arena.take(2 * S) for _ in range(5))
        mva = arena.take(8 * 4 * 65)
        mva4 = mva.rearrange("p (t h c) -> p t h c", t=NT, h=4)
        proj_T(w_in, [(IN1["mq"], 256)], [v2(mq)[:, 0], v2(mq)[:, 1]])
        proj_T(w_in, [(IN1["mk"], 256)], [v2(mk_)[:, 0], v2(mk_)[:, 1]])
        vset(mva4[:, :, :, 64:65], 1.0)
        proj_N(w_in, [(IN1["mv"], 256)], lambda i, b: (mva4[:, i, :, 0:64],
                                                      b.rearrange("p (h c) -> p h c", h=4)))
        fence()
        cw = small["convw"]
        for n, (src, dst) in enumerate(((mq, cq), (mk_, ck))):
            for f in range(2):
                a, o = v2(src)[:, f], v2(dst)[:, f]
                ct = 2 * n + f
                ts(o, a, cw[:, 4 * ct + 3:4 * ct + 4], None, ALU.mult)
                for lag in (1, 2, 3):
                    stt(o[:, lag:S], a[:, 0:S - lag], cw[:, 4 * ct + 3 - lag:4 * ct + 4 - lag],
                        o[:, lag:S], ALU.mult, ALU.add)
            sigmoid_(src, dst)
            if n == 0:
                tt(dst, dst, src, ALU.mult)
            else:
                stt(dst, dst, 0.125, src, ALU.mult, ALU.mult)
        o_m = mq
        om3 = o_m.rearrange("p (t c) -> p t c", t=NT)
        cq3, ck3 = v2(cq), v2(ck)
        nm = arena.take(4 * S).rearrange("p (h s) -> p h s", h=4)
        before = now()
        for h in range(4):
            for n in range(2):
                b, freed = proj_banks.take()
                cols = slice(512 * n, 512 * n + 512)
                mk1 = mm(bank(b), [(onehot[:, h, :], tR[:, cols])], before + [freed])
                proj_banks.free[b] = acopy(nm[:, h, cols], bank(b), [mk1])
        fence()
        Wt = [mk_[:, 0:S], mk_[:, S:2 * S]]
        Pt = [mtmp[:, 0:S], mtmp[:, S:2 * S]]
        s_free, w_free, pt_free, o_free = [None] * 2, [None] * 2, [None] * 2, [None] * 2
        dn = stat[:, 256:288]
        pending = None
        units = [(i, h) for i in range(NT) for h in range(4)]
        for n, un in enumerate(units + [None]):
            cur = None
            if un is not None:
                i, h = un
                p = n % 2
                r0, f = 64 * (h % 2), h // 2
                first = [s_free[p]]
                for j in range(i + 1):
                    mks = mm(ps[:, 1024 * p + P * j:1024 * p + P * j + P],
                             [(ck3[r0:r0 + 64, f, P * j:P * j + P], cq3[r0:r0 + 64, f, P * i:P * i + P])],
                             first)
                    src, wd_ = nm[:, h, P * i:P * i + P], Wt[p][:, P * j:P * j + P]
                    md = None
                    if j == i:
                        md = tt(wd_, src, causal_t, ALU.add, [w_free[p]])
                        src = wd_
                    mw = fn(wd_, src, ACT.Exp, [w_free[p], md], bias=wN[:, j, h:h + 1])
                w_ = P * (i + 1)
                mt = tt(Pt[p][:, 0:w_], ps[:, 1024 * p:1024 * p + w_], Wt[p][:, 0:w_], ALU.mult,
                        [mks, mw, pt_free[p]])
                s_free[p] = w_free[p] = mt
                cur = (i, h, p, mt)
            if pending is not None:
                i, h, p, mt = pending
                ob = i % 2
                col = 512 * (6 + ob) + 65 * h
                mkv = mm(ps[:, col:col + 65], [(Pt[p][:, P * j:P * j + P], mva4[:, j, h, :])
                                               for j in range(i + 1)], [mt, o_free[ob]])
                pt_free[p] = mkv
                if h == 3:
                    o4 = ps[:, 512 * (6 + ob):512 * (6 + ob) + 260].rearrange("p (h c) -> p h c", h=4)
                    d_ = dn[:, 4 * i:4 * i + 4]
                    d3 = d_.unsqueeze(2)
                    vcopy(d3, o4[:, :, 64:65], [mkv])
                    stt(d_, d_, -1.0, d_, ALU.mult, ALU.max)
                    tt(d_, d_, eN[:, i, :], ALU.max)
                    rec(d_, d_)
                    o_free[ob] = tt(om3[:, i, :].rearrange("p (h c) -> p h c", h=4), o4[:, :, 0:64],
                                    d3.broadcast_to([P, 4, 64]), ALU.mult)
            pending = cur
        fence()
        mo = cq
        mo3 = mo.rearrange("p (t c) -> p t c", t=NT)
        proj_N(w_in, [(IN1["mo"], 256)], lambda i, b: (mo3[:, i, :], b))
        sigmoid_(mo, mo)
        head_norm_gate(o_m, mtmp, mo, 6, None)
        fence()
        arena.at = base_w

        def post_norm_residual(F3, gain_src, tag):
            gb_ = arena.take(D)
            a_g = arrival("gain_" + tag)
            gl = sp.dma(gb_, gain_src.partition_broadcast(P), a_g)
            sq = arena.take(D)
            ss = stat[:, 300:308]
            for i in range(NT):
                m = act.do(lambda e, i=i: e.activation(sq, F3[:, i, :], ACT.Square,
                                                       accum_out=ss[:, i:i + 1]), [gl])
            r = rstd_of(ss, ss, D, [m])
            for i in range(NT):
                stt(F3[:, i, :], F3[:, i, :], ss[:, i:i + 1], gb_, ALU.mult, ALU.mult, [r, gl])
                m = tt(X[:, i, :], X[:, i, :], F3[:, i, :], ALU.add)
            return m

        def proj_out_N(w, srcT, kt, dst, tag):
            for c in range(4):
                slot, wv, landed = wslots.load(
                    lambda b: b[:, 0:kt * 256].rearrange("p (k c) -> p k c", k=kt),
                    [(lambda v: v, w.rearrange("(k p) c -> p k c", p=P)[:, :, 256 * c:256 * c + 256])])
                for i in range(NT):
                    b, freed = proj_banks.take()
                    mk = mm(bank(b, 256), [(srcT[:, k, P * i:P * i + P], wv[:, k, :]) for k in range(kt)],
                            [landed, freed])
                    proj_banks.free[b] = e = evac(dst[:, i, 256 * c:256 * c + 256], bank(b, 256), [mk])
                wslots.free[slot] = mk
            return e

        F1 = aTW.rearrange("p (t d) -> p t d", t=NT)
        proj_out_N(t["w_out"], yT, KD, F1, "wo")
        fence()
        ready = [sp.dma(X[:, i, :], xin[i], a_x[i]) for i in range(NT)]
        for l in (act, dve):
            l.held = l.held + ready
        post_norm_residual(F1, t["g1post"], "mix")
        fence()
        arena.at = base_w
        scratch = arena.take(3 * D)
        norm_to_T(small["g2pre"], [None] * NT, scratch)
        fence()
        arena.at = base_w

        NF = FF // P
        hT = arena.take(NF * S).rearrange("p (f s) -> p f s", f=NF)
        tmp4 = [arena.take(512) for _ in range(4)]
        fb = Banks([0, 1, 2, 3, 4, 5, 6, 7])
        tfree = [None] * 4

        def swiglu(gate_b, up_b, o, after, k):
            tp = tmp4[k % 4]
            m = fn(tp, bank(gate_b), ACT.Exp, after + [tfree[k % 4]], scale=-1.0)
            ts(tp, tp, 1.0, None, ALU.add, after=[m])
            rec(tp, tp)
            tt(tp, tp, bank(gate_b), ALU.mult)
            m = tt(o, tp, bank(up_b), ALU.mult)
            tfree[k % 4] = m
            fb.free[gate_b] = fb.free[up_b] = m
            return m

        kcount = [0]
        Lane.turns = False
        for f in range(NF):
            gsl = wslots.load(lambda b: b[:, 0:2048].rearrange("p (w k c) -> p w k c", w=2, k=KD),
                              [(lambda v, n=n: v[:, n], w.rearrange("(k p) c -> p k c", p=P)
                                [:, :, P * f:P * f + P]) for n, w in enumerate((t["w_fg"], t["w_fu"]))])
            slot, wv, landed = gsl
            for n in range(2):
                cols = slice(512 * n, 512 * n + 512)
                bg, f1 = fb.take()
                mm(bank(bg), [(wv[:, 0, k, :], aT[:, k, cols]) for k in range(KD)], [landed, f1])
                bu, f2 = fb.take()
                mk = mm(bank(bu), [(wv[:, 1, k, :], aT[:, k, cols]) for k in range(KD)], [f2])
                swiglu(bg, bu, hT[:, f, cols], [mk], kcount[0])
                kcount[0] += 1
            wslots.free[slot] = mk
        fence()
        wd = t["w_fd"].rearrange("(f p) c -> p f c", p=P)
        dfree = [None] * NT
        for n in range(2):
            f = 0
            while f < NF:
                nf = min(4, NF - f)
                slot, wv, landed = wslots.load(
                    lambda b: b[:, 0:nf * 512].rearrange("p (k c) -> p k c", k=nf),
                    [(lambda v: v, wd[:, f:f + nf, 512 * n:512 * n + 512])])
                for i in range(NT):
                    for q in range(nf):
                        mk = pe.do(lambda e, i=i, q=q, f=f, wv=wv: e.matmul(
                            bank(i), hT[:, f + q, P * i:P * i + P], wv[:, q, :],
                            start=(f + q == 0), stop=(f + q == NF - 1)),
                            [landed, dfree[i] if f + q == 0 else None])
                wslots.free[slot] = mk
                f += nf
            for i in range(NT):
                dfree[i] = evac(F1[:, i, 512 * n:512 * n + 512], bank(i), [mk])
        fence()
        arena.at = base_w
        Lane.turns = True
        post_norm_residual(F1, t["g2post"], "ffn")
        fence()
        arena.at = base_w

        scratch = arena.take(3 * D)
        norm_to_T(small["gffn"], [None] * NT, scratch)
        fence()
        arena.at = base_w
        w2 = t["w_in_2"]

        OA = arena.take(NT * 512).rearrange("p (t c) -> p t c", t=NT)
        qa = arena.take(4 * S).rearrange("p (a s) -> p a s", a=4)
        gN = arena.take(NT * 24)
        gN3 = gN.rearrange("p (t c) -> p t c", t=NT)
        BL = arena.take(S // 2).bitcast(BF16)
        a_bl = arrival("bias_rows_landed")
        bl_landed = sp.dma(BL[32:P, :], t["c_bl"][32:P, :], a_bl)
        base_2 = arena.at

        def heads_proj(c, dst):
            for i in range(0, 4, 2):
                proj_T(w2, [(c + 64 * h, 64) for h in (i, i + 4, i + 1, i + 5)],
                       [dst[:, i], dst[:, i + 1]])

        heads_proj(IN2["q"], qa)
        proj_N(w2, [(IN2["g"], 24)], lambda i, b: (gN3[:, i, :], b))
        sigmoid_(gN, gN)

        kcT = arena.take(64)
        vcN = arena.take(128).rearrange("p (g c) -> p g c", g=2)
        base_c = arena.at
        kvc = arena.take(2 * S)
        kv2 = v2(kvc)
        proj_T(w2, [(IN2["kc"], 256)], [kv2[:, 0], kv2[:, 1]])
        w1 = arena.take(32 * 256).rearrange("p (l c) -> p l c", l=32)
        w2s = arena.take(2 * 2 * 64).rearrange("p (n k c) -> p n k c", n=2, k=2)
        a_w1 = arrival("cmp_w1_landed")
        a_w2 = arrival("cmp_w2_landed")
        for n, nm_ in enumerate(("cmp_w2_k", "cmp_w2_v")):
            w2_landed = sp.dma(w2s[:, n], t[nm_].rearrange("(k p) c -> p k c", p=P), a_w2)
        AB = [arena.take(S) for _ in range(2)]
        hid = arena.take(2 * 2 * 64).rearrange("p (m g c) -> p m g c", m=2, g=2)
        vset(kcT, 0.0)
        vset(vcN, 0.0)
        for n, (wn, pos) in enumerate((("cmp_w1_k", "pos_k"), ("cmp_w1_v", "pos_v"))):
            before = now()
            src = t[wn].rearrange("(l d) c -> d l c", d=64)
            sp.dma(w1[0:64], src, a_w1, before)
            w1_landed = sp.dma(w1[64:128], src, a_w1)
            kv3 = kv2[:, n].rearrange("p (c l) -> p c l", l=16)
            for half in range(2):
                pv = small[pos][:, 16 * half:16 * half + 16].unsqueeze(1).broadcast_to([P, 64, 16])
                m = tt(AB[half].rearrange("p (c l) -> p c l", l=16), kv3, pv, ALU.add,
                       before if half == 0 else ())
            for mt_ in range(2):
                for g in range(2):
                    r0 = 64 * g
                    pairs = []
                    for l in range(32):
                        a3 = AB[l // 16].rearrange("p (c l) -> p c l", l=16)
                        c0 = l // 16
                        pairs.append((w1[r0:r0 + 64, l, P * mt_:P * mt_ + P],
                                      a3[r0:r0 + 64, c0:c0 + NC, l % 16]))
                    b, freed = proj_banks.take()
                    mk = mm(bank(b, NC), pairs, [m, w1_landed, freed])
                    tp = stat[:, 400:400 + NC]
                    m1 = fn(tp, bank(b, NC), ACT.Exp, [mk, (dve.sem, dve.count)], scale=-1.0)
                    ts(tp, tp, 1.0, None, ALU.add, after=[m1])
                    rec(tp, tp)
                    mh = tt(hid[:, mt_, g, 0:NC], tp, bank(b, NC), ALU.mult)
                    proj_banks.free[b] = mh
            b, freed = proj_banks.take()
            if n == 0:
                for g in range(2):
                    r0 = 64 * g
                    mk = mm(bank(b)[r0:r0 + 64, 0:NC], [(w2s[:, 0, k, :], hid[:, k, g, 0:NC])
                                                       for k in range(2)], [mh, w2_landed, freed])
                proj_banks.free[b] = vcopy(kcT[:, 0:NC], bank(b, NC), [mk])
            else:
                for g in range(2):
                    for r0 in (0, 64):
                        mk = mm(bank(b)[r0:r0 + NC, 64 * g:64 * g + 64],
                                [(hid[:, k, g, 0:NC], w2s[:, 1, k, :]) for k in range(2)],
                                [mh, w2_landed, freed])
                vcopy(vcN[0:NC].rearrange("p g c -> p (g c)"), bank(b)[0:NC, 0:128], [mk])
                proj_banks.free[b] = vcopy(vcN[64:64 + NC].rearrange("p g c -> p (g c)"),
                                           bank(b)[64:64 + NC, 0:128])
        fence()
        arena.at = base_c
        cslots = Slots("cmp_bias_landed", 512 + 64, 2, sp)
        pc = [arena.take(512) for _ in range(2)]
        pTc = arena.take(512)
        sc_ = arena.take(64)
        top = arena.take(16)
        pen = arena.take(32)
        cm = arena.take(16)
        g24 = gN.rearrange("p (t h b) -> p t h b", t=NT, h=8)
        for i in range(NT):
            slot, cv, landed = cslots.load(lambda b: b[:, 0:512 + 64], [
                (lambda v: v, t["c_cmp"].rearrange("(t p) c -> t p c", p=P)[i])])
            before = now()
            for h in range(8):
                r0 = 64 * (h // 4)
                mk = mm(bank(h // 4)[:, 64 * (h % 4):64 * (h % 4) + 64],
                        [(qa[r0:r0 + 64, h % 4, P * i:P * i + P], kcT[r0:r0 + 64, :])], before)
            p_ = pc[i % 2]
            p3 = p_.rearrange("p (h c) -> p h c", h=8)
            mx, zz = cm[:, 0:8], cm[:, 8:16]
            for g in range(2):
                half = slice(256 * g, 256 * g + 256)
                stt(p_[:, half], bank(g, 256), 0.125, cv[:, half], ALU.mult, ALU.add, [mk, landed])
            red(mx, p3, ALU.max)
            ts(mx, mx, -1e29, None, ALU.max)
            m = tt(p3, p3, mx.unsqueeze(2).broadcast_to([P, 8, 64]), ALU.subtract)
            m = fn(p_, p_, ACT.Exp, [m])
            red(zz, p3, ALU.add, [m])
            ts(zz, zz, 1e-30, None, ALU.max)
            rec(zz, zz)
            m = tt(p3, p3, zz.unsqueeze(2).broadcast_to([P, 8, 64]), ALU.mult)
            for q in range(4):
                mt = tr(bank(2)[:, P * q:P * q + P], p_[:, P * q:P * q + P], [m])
            m = vcopy(pTc, bank(2), [mt])
            for g in range(2):
                mk = mm(bank(3)[:, 16 * g:16 * g + 16],
                        [(pTc[:, P * q:P * q + P], ov) for q in (2 * g, 2 * g + 1)], [m])
            for h in range(8):
                r0 = 64 * (h % 2)
                mo_ = mm(bank(5 + h % 2)[:, 64 * (h // 2):64 * (h // 2) + 64],
                         [(pTc[r0:r0 + 64, P * (h // 2):P * (h // 2) + P],
                           vcN[r0:r0 + 64, h // 4, :])], [m])
            keep, add = cv[:, 512:544], cv[:, 544:576]
            tt(sc_[:, 0:32], bank(3, 32), keep, ALU.mult, [mk])
            tt(sc_[:, 0:32], sc_[:, 0:32], add, ALU.add)
            for g in range(2):
                dve.do(lambda e, g=g: e.max(top[:, 8 * g:8 * g + 8], sc_[:, 16 * g:16 * g + 16]))
                dve.do(lambda e, g=g: e.match_replace(sc_[:, 32 + 16 * g:48 + 16 * g],
                                                      top[:, 8 * g:8 * g + 8],
                                                      sc_[:, 16 * g:16 * g + 16], -3e38))
            m = ts(pen, sc_[:, 32:64], -1e38, NEG, ALU.is_gt, ALU.mult)
            mt = tr(bank(4)[0:32, 0:P], pen, [m])
            vcopy(BL[0:32, P * i:P * i + P], bank(4)[0:32, 0:P], [mt])
            for r in range(2):
                gate = g24[:, i, :, 0:1].rearrange("p (f r) b -> p f r b", r=2)[:, :, r, :]
                cslots.free[slot] = tt(OA[:, i, :].rearrange("p (f r c) -> p f r c", f=4, r=2)[:, :, r, :],
                                       bank(5 + r, 256).rearrange("p (f c) -> p f c", f=4),
                                       gate.broadcast_to([P, 4, 64]), ALU.mult, [mo_])
        fence()
        arena.at = base_2

        kx = arena.take(2 * S)
        vx = arena.take(NT * 256)
        kx2 = v2(kx)
        vx3 = vx.rearrange("p (t c) -> p t c", t=NT)
        proj_T(w2, [(IN2["ks"], 128), (IN2["kw"], 128)], [kx2[:, 0], kx2[:, 1]])
        proj_N(w2, [(IN2["vs"], 128), (IN2["vw"], 128)], lambda i, b: (vx3[:, i, :], b))
        BR = arena.take(8 * S // 2).bitcast(BF16)
        BR3 = BR.rearrange("p (h s) -> p h s", h=8)
        br_landed = sp.dma(BR, t["c_br"], a_bl)
        att = Attention()
        coef = arena.take(8)
        prod = arena.take(512)
        fence()

        def unit_2(i, h, q, kT, V, vcol, w, k_lo, bias, sink=None):
            g = h // 4
            r0 = 64 * g
            return dict(q=q[r0:r0 + 64, h % 4, P * i:P * i + P],
                        k=lambda c0, c1: kT[r0:r0 + 64, k_lo + c0:k_lo + c1], width=w, bias=bias,
                        v=lambda n: V[:, k_lo // P + n, vcol + 64 * g:vcol + 64 * g + 64],
                        tile=i, head=h, heads=8, last=h == 7, sink=sink)

        def gated_finish(branch):
            def finish(i, o, rz, after):
                tt(coef.unsqueeze(2), rz.unsqueeze(2), g24[:, i, :, branch:branch + 1], ALU.mult)
                m = tt(prod.rearrange("p (h c) -> p h c", h=8), o.rearrange("p (h c) -> p h c", h=8),
                       coef.unsqueeze(2).broadcast_to([P, 8, 64]), ALU.mult, after)
                tt(OA[:, i, :], OA[:, i, :], prod, ALU.add)
                return m
            return finish

        def slc_unit(i, h):
            w = P * (i + 1)

            def bias(c0, c1):
                got = [(c0, c1, BL[:, P * i:P * i + P], BR3[:, h, c0:c1])]
                if c1 == w:
                    got.append((w - P, w, ident_b, causal_n))
                return got
            return unit_2(i, h, qa, kx2[:, 0], vx3, 0, w, 0, bias)

        def band_unit(i, h, q, kT, V, vcol, nprev, mask, rows_r, sink=None):
            nb1 = min(i, nprev) + 1
            skip = P * (nprev + 1 - nb1)
            rs = P * (2 - nprev) + skip

            def bias(c0, c1):
                return [(c0, c1, win_l, rows_r[:, h, rs + c0:rs + c1]),
                        (c0, c1, ident_b, mask[:, skip + c0:skip + c1])]
            return unit_2(i, h, q, kT, V, vcol, P * nb1, P * (i + 1 - nb1), bias, sink)

        att.run([slc_unit(i, h) for i in range(NT) for h in range(8)], gated_finish(1), [])
        att.run([band_unit(i, h, qa, kx2[:, 1], vx3, 128, 2, win_mask, win_r)
                 for i in range(NT) for h in range(8)], gated_finish(2), [])
        fence()
        arena.at = base_2

        OB = arena.take(NT * 512).rearrange("p (t c) -> p t c", t=NT)
        base_o = arena.at
        kb_ = arena.take(S)
        vb_ = arena.take(NT * 128)
        vb3 = vb_.rearrange("p (t c) -> p t c", t=NT)
        heads_proj(IN2["qb"], qa)
        proj_T(w2, [(IN2["kb"], 128)], [kb_])
        proj_N(w2, [(IN2["vb"], 128)], lambda i, b: (vb3[:, i, :], b))
        att = Attention()
        fence()

        def swa_finish(i, o, rz, after):
            return tt(OB[:, i, :].rearrange("p (h c) -> p h c", h=8),
                      o.rearrange("p (h c) -> p h c", h=8), rz.unsqueeze(2).broadcast_to([P, 8, 64]),
                      ALU.mult, after)

        att.run([band_unit(i, h, qa, kb_, vb3, 0, 1, swa_mask, swa_r, small["sinks"][:, h:h + 1])
                 for i in range(NT) for h in range(8)], swa_finish, [])
        fence()

        arena.at = base_o
        OAT = arena.take(4 * S).rearrange("p (k s) -> p k s", k=4)
        OBT = arena.take(4 * S).rearrange("p (k s) -> p k s", k=4)
        for src, dst in ((OA, OAT), (OB, OBT)):
            for k in range(4):
                for n in range(2):
                    b, freed = proj_banks.take()
                    for q in range(4):
                        mt = tr(bank(b)[:, P * q:P * q + P], src[:, 4 * n + q, P * k:P * k + P], [freed])
                    proj_banks.free[b] = evac(dst[:, k, 512 * n:512 * n + 512], bank(b), [mt])
        fence()
        keep_at = arena.at
        arena.at = base_w
        mixT = arena.take(8 * S).rearrange("p (k s) -> p k s", k=8)
        arena.at = keep_at
        assert base_w + 8 * S <= base_2
        pslots = Slots("wab_landed", 1024, 2, act)
        keep_at = arena.at
        arena.at = base_2
        tmp4 = [arena.take(512) for _ in range(4)]
        arena.at = keep_at
        tfree = [None] * 4
        m8b = Banks([0, 1, 2, 3, 4, 5, 6, 7])
        k8 = 0
        r_wa = t["w_a"].rearrange("(k p) c -> p k c", p=P)
        r_wb = t["w_b"].rearrange("(k p) c -> p k c", p=P)
        for c in range(8):
            slot, wv, landed = w_load(w2, [(IN2["ga"] + P * c, P), (IN2["gb"] + P * c, P)])
            s2, wab, landed2 = pslots.load(
                lambda b: b.rearrange("p (n k c) -> p n k c", n=2, k=4),
                [(lambda v, n=n: v[:, n], w[:, :, P * c:P * c + P]) for n, w in enumerate((r_wa, r_wb))])
            for n in range(2):
                cols = slice(512 * n, 512 * n + 512)
                parts = []
                for br2, oT in enumerate((OAT, OBT)):
                    b1, f1 = m8b.take()
                    mg_ = mm(bank(b1), [(wv[:, k, P * br2:P * br2 + P], aT[:, k, cols])
                                        for k in range(KD)], [landed, f1])
                    b2, f2 = m8b.take()
                    mp_ = mm(bank(b2), [(wab[:, br2, k, :], oT[:, k, cols]) for k in range(4)],
                             [landed2, f2])
                    tp = tmp4[k8 % 4]
                    m = fn(tp, bank(b1), ACT.Exp, [mg_, tfree[k8 % 4]], scale=-1.0)
                    m8b.free[b1] = m
                    ts(tp, tp, 1.0, None, ALU.add, after=[m])
                    rec(tp, tp)
                    m8b.free[b2] = tt(tp, tp, bank(b2), ALU.mult, [mp_])
                    parts.append((tp, k8 % 4))
                    k8 += 1
                m = tt(mixT[:, c, cols], parts[0][0], parts[1][0], ALU.add)
                tfree[parts[0][1]] = tfree[parts[1][1]] = m
            wslots.free[slot] = mp_
            pslots.free[s2] = mp_
        fence()
        for c in range(4):
            slot, wv, landed = w_load(t["w_o"], [(256 * c, 256)])
            for i in range(NT):
                b, freed = proj_banks.take()
                mk = mm(bank(b, 256), [(mixT[:, k, P * i:P * i + P], wv[:, k, :]) for k in range(KD)],
                        [landed, freed])
                xs = X[:, i, 256 * c:256 * c + 256]
                proj_banks.free[b] = tt(xs, xs, bank(b, 256), ALU.add, [mk])
            wslots.free[slot] = mk
        fence()
        arena.at = base_w
        scratch = arena.take(3 * D)
        norm_to_T(small["gmoe"], [None] * NT, scratch)
        fence()
        arena.at = base_w

        lg = arena.take(NT * 36)
        lg3 = lg.rearrange("p (t c) -> p t c", t=NT)
        bias36 = arena.take(36)
        a_b36 = arrival("router_bias_landed")
        b36 = sp.dma(bias36, t["b_router"].partition_broadcast(P), a_b36)
        proj_N(t["w_router"], [(0, 36)], lambda i, b: (lg3[:, i, :], b))
        tt(lg3, lg3, bias36.unsqueeze(1).broadcast_to([P, NT, 36]), ALU.add, now())
        rt = arena.take(1024)
        gm = rt[:, 0:8]
        oh = rt[:, 32:64].rearrange("p (t c) -> p t c", t=NT)
        eq = rt[:, 64:128]
        ein = rt[:, 128:192].rearrange("p (t c) -> p t c", t=NT)
        m1 = rt[:, 192:256].rearrange("p (t c) -> p t c", t=NT)
        m2 = rt[:, 256:320].rearrange("p (t c) -> p t c", t=NT)
        v1, v2_, pg, p1, p2, ix = (rt[:, 320 + 8 * n:328 + 8 * n] for n in range(6))
        we = rt[:, 384:448].rearrange("p (t c) -> p t c", t=NT)
        tm = rt[:, 448:512].rearrange("p (t c) -> p t c", t=NT)
        W32 = arena.take(256).rearrange("p (t g e) -> p t g e", t=NT, g=NG)
        bc3 = lambda a, n: a.unsqueeze(2).broadcast_to([P, NT, n])

        def first_max(vals, n, value, hot, io):
            red(value, vals, ALU.max)
            tt(hot, vals, bc3(value, n), ALU.is_equal)
            ts(hot, hot, -64.0, 64.0, ALU.mult, ALU.add)
            tt(hot, hot, io.unsqueeze(1).broadcast_to([P, NT, n]), ALU.add)
            red(ix, hot, ALU.min)
            return tt(hot, hot, bc3(ix, n), ALU.is_equal)

        gl3 = lg3[:, :, 0:4]
        first_max(gl3, 4, gm, oh, iota4)
        t4 = eq[:, 0:32].rearrange("p (t c) -> p t c", t=NT)
        m = tt(t4, gl3, bc3(gm, 4), ALU.subtract)
        m = fn(t4, t4, ACT.Exp, [m])
        red(pg, t4, ALU.add, [m])
        rec(pg, pg)
        for g in range(NG):
            le = lg3[:, :, 4 + EG * g:4 + EG * g + EG]
            sel = oh[:, :, g:g + 1].broadcast_to([P, NT, EG])
            if g == 0:
                tt(ein, le, sel, ALU.mult)
            else:
                tt(tm, le, sel, ALU.mult)
                tt(ein, ein, tm, ALU.add)
        first_max(ein, 8, v1, m1, iota8)
        stt(tm, m1, NEG, ein, ALU.mult, ALU.add)
        first_max(tm, 8, v2_, m2, iota8)
        tt(p2, v2_, v1, ALU.subtract)
        m = fn(p2, p2, ACT.Exp, [(dve.sem, dve.count)])
        ts(p1, p2, 1.0, None, ALU.add, after=[m])
        rec(p1, p1)
        tt(p1, p1, pg, ALU.mult)
        tt(p2, p2, p1, ALU.mult)
        tt(m1, m1, bc3(p1, 8), ALU.mult)
        tt(m2, m2, bc3(p2, 8), ALU.mult)
        tt(we, m1, m2, ALU.add)
        for g in range(NG):
            tt(W32[:, :, g, :], we, oh[:, :, g:g + 1].broadcast_to([P, NT, EG]), ALU.mult)
        W32f = W32.rearrange("p t g e -> p t (g e)")
        fence()
        eslots = Slots("expert_landed", 6144, 2, sp)
        eh = [arena.take(2 * S).rearrange("p (m s) -> p m s", m=2) for _ in range(2)]
        tmp4 = [arena.take(512) for _ in range(4)]
        tfree = [None] * 4
        fb = Banks([0, 1, 2, 3])
        db = Banks([4, 5, 6, 7])
        eh_free = [None, None]
        k9 = 0

        def expert_up(e):
            nonlocal k9
            wge = t["w_ge"][e].rearrange("(k p) c -> p k c", p=P)
            wue = t["w_ue"][e].rearrange("(k p) c -> p k c", p=P)
            wde = t["w_de"][e].rearrange("(k p) c -> p k c", p=P)
            slot, wv, landed = eslots.load(lambda b: b, [
                (lambda v: v[:, 0:2048].rearrange("p (k c) -> p k c", k=KD), wge),
                (lambda v: v[:, 2048:4096].rearrange("p (k c) -> p k c", k=KD), wue),
                (lambda v: v[:, 4096:6144].rearrange("p (k c) -> p k c", k=2), wde)])
            wg = wv[:, 0:2048].rearrange("p (k c) -> p k c", k=KD)
            wu = wv[:, 2048:4096].rearrange("p (k c) -> p k c", k=KD)
            for mt_ in range(2):
                for n in range(2):
                    cols = slice(512 * n, 512 * n + 512)
                    bg, f1 = fb.take()
                    mm(bank(bg), [(wg[:, k, P * mt_:P * mt_ + P], aT[:, k, cols]) for k in range(KD)],
                       [landed, f1])
                    bu, f2 = fb.take()
                    mk = mm(bank(bu), [(wu[:, k, P * mt_:P * mt_ + P], aT[:, k, cols])
                                       for k in range(KD)], [f2])
                    m = swiglu2(bg, bu, eh[e % 2][:, mt_, cols], [mk, eh_free[e % 2]])
            return slot, wv, m

        def swiglu2(bg, bu, o, after):
            nonlocal k9
            tp = tmp4[k9 % 4]
            m = fn(tp, bank(bg), ACT.Exp, after + [tfree[k9 % 4]], scale=-1.0)
            ts(tp, tp, 1.0, None, ALU.add, after=[m])
            rec(tp, tp)
            tt(tp, tp, bank(bg), ALU.mult)
            m = tt(o, tp, bank(bu), ALU.mult, after)
            tfree[k9 % 4] = m
            fb.free[bg] = fb.free[bu] = m
            k9 += 1
            return m

        def expert_down(e, slot, wv, ready_):
            wd_ = wv[:, 4096:6144].rearrange("p (k c) -> p k c", k=2)
            for i in range(NT):
                for n in range(2):
                    b, freed = db.take()
                    mk = mm(bank(b), [(eh[e % 2][:, k, P * i:P * i + P], wd_[:, k, 512 * n:512 * n + 512])
                                      for k in range(2)], [ready_, freed])
                    xs = X[:, i, 512 * n:512 * n + 512]
                    db.free[b] = stt(xs, bank(b), W32f[:, i, e:e + 1], xs, ALU.mult, ALU.add, [mk])
            eslots.free[slot] = mk
            eh_free[e % 2] = mk

        pending = None
        Lane.turns = False
        for e in range(NE + 1):
            cur = (e, *expert_up(e)) if e < NE else None
            if pending is not None:
                expert_down(*pending)
            pending = cur
        fence()
        arena.at = base_w

        Lane.turns = True
        gfin = arena.take(D)
        a_gf = arrival("final_gain_landed")
        gl = sp.dma(gfin, t["g_final"].partition_broadcast(P), a_gf)
        sq = arena.take(D)
        ss = stat[:, 0:8]
        for i in range(NT):
            m = act.do(lambda e, i=i: e.activation(sq, X[:, i, :], ACT.Square,
                                                   accum_out=ss[:, i:i + 1]))
        r = rstd_of(ss, ss, D, [m])
        a_out = arrival("out_written")
        outv = out.rearrange("(t p) d -> t p d", p=P)
        for i in range(NT):
            m = stt(X[:, i, :], X[:, i, :], ss[:, i:i + 1], gfin, ALU.mult, ALU.mult, [r, gl])
            stored = sp.dma(outv[i], X[:, i, :], a_out, [m])

        block = ctx.enter_context(nc.Block())

        @block.sync
        def _(eng):
            sp.emit(eng)
            eng.wait_ge(*stored)

        @block.tensor
        def _(eng):
            pe.emit(eng)

        @block.vector
        def _(eng):
            dve.emit(eng)

        @block.scalar
        def _(eng):
            act.emit(eng)

        if pool.steps:
            @block.gpsimd
            def _(eng):
                pool.emit(eng)


def shape_constants():
    bf = np.dtype("bfloat16")
    f32 = np.float32
    r = np.arange(P)
    c = np.zeros((P, 1280 + 512 + 16 + 8), f32)
    c[:, 0:128] = np.eye(P)
    c[:, 128:256] = 1.0
    c[:, 256:1280] = (np.arange(S) % P != 0)[None, :]
    for h in range(4):
        c[h, 1280 + 128 * h:1280 + 128 * h + 128] = 1.0
    ov = np.zeros((64, 16))
    for b in range(NC):
        for j in range(16):
            ov[b, j] = max(min(16 * b + 32, 64 * j + 64) - max(16 * b, 64 * j), 0) / 32
    c[0:64, 1792:1808] = ov
    c[64:128, 1792:1808] = ov
    c[:, 1808:1816] = np.arange(8)[None, :]

    slopes = (2.0 ** (-8.0 * np.arange(1, 17) / 16)).astype(f32)
    swa, nsa = slopes[:8], slopes[8:]

    def parts(a):
        a = np.asarray(a, np.float64)
        got = []
        for _ in range(3):
            q = a.astype(bf)
            got.append(q)
            a = a - q.astype(np.float64)
        return got

    b = np.zeros((P, 4224 + 8 * 384), bf)
    b[:, 0:128] = np.eye(P)
    b[:, 128:256] = np.where(r[None, :] > r[:, None], NEG, 0)
    b[:, 256:384] = np.where(r[:, None] > r[None, :], NEG, 0)
    kw = np.arange(384) - 256
    dist = r[:, None] - kw[None, :]
    b[:, 384:768] = np.where((dist >= 0) & (dist < 256), 0, NEG)
    b[:, 768:1024] = np.where((dist >= 0) & (dist < 128), 0, NEG)[:, 128:]
    for n in range(3):
        b[n, 1024:1152] = r
        b[3 + n, 1024:1152] = 1.0
    for lo, sl in ((1152, nsa), (4224, swa)):
        for h in range(8):
            for n, q in enumerate(parts(-8.0 * sl[h])):
                b[n, lo + 384 * h:lo + 384 * h + 384] = q
            for n, q in enumerate(parts(8.0 * sl[h].astype(np.float64) * kw)):
                b[3 + n, lo + 384 * h:lo + 384 * h + 384] = q

    mask = np.zeros((P, 8, P), bf)
    for l in range(LEVELS):
        same = (r[:, None] >> (l + 1)) == (r[None, :] >> (l + 1))
        mask[:, l] = same & (((r[None, :] >> l) & 1) == 1) & (((r[:, None] >> l) & 1) == 0)
    mask[:, 7] = np.eye(P)

    tok = np.arange(S)
    bl = np.zeros((P, S), bf)
    for n in range(3):
        bl[32 + n] = tok // 256 * 256
        bl[35 + n] = tok % 256
        bl[38 + n] = 1.0
    br = np.zeros((P, 8, S), bf)
    for h in range(8):
        for j in range(16):
            br[16 * (h // 4) + j, h, 64 * j:64 * j + 64] = 1.0
        for n, q in enumerate(parts(-8.0 * nsa[h])):
            br[32 + n, h] = q
            br[35 + n, h] = q
        for n, q in enumerate(parts(8.0 * nsa[h].astype(np.float64) * tok)):
            br[38 + n, h] = q

    cmp_ = np.full((S, 8, 64), NEG, f32)
    d = tok[:, None] - (np.arange(NC) * 16 + 31)[None, :]
    for h in range(8):
        cmp_[:, h, :NC] = np.where(d >= 0, -(nsa[h] * d.astype(f32)), f32(NEG))
    j = np.arange(16)[None, :]
    cur = tok[:, None] // 64
    forced = (j == 0) | (j == cur) | (j == cur - 1)
    valid = j * 64 <= tok[:, None]
    keep = (valid & ~forced).astype(f32)
    add = np.where(forced, 1e9, np.where(valid, 0, NEG)).astype(f32)
    table = np.concatenate([cmp_.reshape(S, 512), keep, keep, add, add], axis=1)
    return dict(c_f32=c, c_bf16=b, c_mask=mask.reshape(P, -1), c_bl=bl, c_br=br.reshape(P, -1),
                c_cmp=table)


def kernel(**inputs):
    import concourse.bacc as bacc
    from concourse.bass_utils import run_bass_kernel_spmd

    a = {k: np.asarray(v) for k, v in inputs.items()}
    f32 = np.float32

    def cols(v):
        return np.ascontiguousarray(v.reshape(-1, P).T)

    def states(v):
        return v.reshape(8, P).T

    def blocks(v):
        o = np.zeros((P, 8, 32), f32)
        w = v.reshape(8, 2, 64, 16)
        for g in range(2):
            o[64 * g:64 * g + 64, :, 16 * g:16 * g + 16] = w[:, g].transpose(1, 0, 2)
        return o.reshape(P, 256)

    x = {
        "x": a["x"][0], "w_in": a["w_in"][0],
        "g1pre": cols(a["ln_mix_pre"][0]), "g2pre": cols(a["ln_ffn_pre"][0]),
        "gmix": cols(a["mix_gain"][0]), "gffn": cols(a["norm_mix_g_2"][0]),
        "gmoe": cols(a["norm_ffn_g_2"][0]),
        "g1post": a["ln_mix_post"][0], "g2post": a["ln_ffn_post"][0], "g_final": a["norm_final_g_2"],
        "lam": np.concatenate([states(a["s5_lambda_re"][0]), states(a["s5_lambda_im"][0])], axis=1),
        "s5d": cols(a["s5_d"][0]),
        "ldt": states(np.repeat(a["s5_log_dt"][0][:, None], 64, axis=1)),
        "lbl": cols(a["hgrn_lb_logits"][0]),
        "convw": np.concatenate([a["mlstm_conv_w"][0][:, P * n:P * n + P].T for n in range(4)], axis=1),
        "gate_b": a["gate_bias"][0].reshape(3, 4).T,
        "sinks": np.broadcast_to(a["sinks_2"][0][None, :], (P, 8)),
        "pos_k": np.concatenate([a["cmp_pos_k_2"][0].T] * 2, axis=0),
        "pos_v": np.concatenate([a["cmp_pos_v_2"][0].T] * 2, axis=0),
        "b_re": blocks(a["s5_b_re"][0]), "b_im": blocks(a["s5_b_im"][0]),
        "c_re": blocks(a["s5_c_re"][0].transpose(0, 2, 1)),
        "c_im": blocks(a["s5_c_im"][0].transpose(0, 2, 1)),
        "w_glu": a["s5_w_glu"][0], "w_out": a["w_out"][0],
        "w_fg": a["w_ffn_gate"][0], "w_fu": a["w_ffn_up"][0], "w_fd": a["w_ffn_down"][0],
        "w_in_2": a["w_in_2"][0],
        "cmp_w1_k": a["cmp_w1_k_2"][0], "cmp_w1_v": a["cmp_w1_v_2"][0],
        "cmp_w2_k": a["cmp_w2_k_2"][0], "cmp_w2_v": a["cmp_w2_v_2"][0],
        "w_a": a["w_a_2"][0], "w_b": a["w_b_2"][0], "w_o": a["w_o_2"][0],
        "w_router": np.concatenate([a["w_group_2"][0], a["w_expert_2"][0]], axis=1),
        "b_router": np.concatenate([a["b_group_2"][0], a["b_expert_2"][0]]),
        "w_ge": a["w_gate_e_2"][0], "w_ue": a["w_up_e_2"][0], "w_de": a["w_down_e_2"][0],
    }
    x.update(shape_constants())
    nc = bacc.Bacc("TRN2", target_bir_lowering=False, num_devices=1)
    arrays, handles = {}, {}
    for name, v in x.items():
        v = np.ascontiguousarray(v)
        arrays["in_" + name] = v
        handles[name] = nc.dram_tensor("in_" + name, v.shape, mybir.dt.from_np(v.dtype),
                                       kind="ExternalInput").ap()
    out = nc.dram_tensor("out", (S, D), F32, kind="ExternalOutput").ap()
    build(nc, handles, out)
    r = run_bass_kernel_spmd(nc, [arrays], core_ids=[0])
    return r.results[0]["out"].reshape(1, S, D)
```

```python
import numpy as np
import concourse.bass as bass
from concourse import mybir
from concourse.alu_op_type import AluOpType as ALU

F32 = mybir.dt.float32
BF16 = mybir.dt.bfloat16
ACT = mybir.ActivationFunctionType
AX = mybir.AxisListType.X

P = 128
S = 1024
D = 1024
NT = S // P
KD = D // P
GW = 256
FF = 2816
EPS = 1e-6
NEG = -1e30
TWO_PI = 6.283185307179586
ROUND = 12582912.0

IN1 = dict(s5=0, hq=256, hf=512, hi=768, hg=1024, fq=1280, fk=1536, fv=1792, ff=2048,
           mq=2052, mk=2308, mv=2564, mo=2820, mi=3076, mf=3080)
IN2 = dict(q=0, kc=512, vc=640, ks=768, vs=896, kw=1024, vw=1152, g=1280, qb=1304, kb=1816,
           vb=1944, ga=2072, gb=3096)
NC = 63
NE, EG, NG, EF = 32, 8, 4, 256
NOV = (2 * S - 1) // P
NBLK = NE + NOV
LEVELS = 7


class Lane:

    turns = True
    partner = None

    def __init__(self, sem, chained):
        self.sem, self.chained, self.count, self.steps, self.held = sem, chained, 0, [], []

    def do(self, step, after=(), chain=True):
        waits = self.held + [m for m in after if m is not None]
        self.held = []
        if self.chained and chain and self.count:
            waits.append((self.sem, self.count))
        if self.partner is not None and Lane.turns and self.partner.count:
            waits.append((self.partner.sem, self.partner.count))
        self.count += 1
        self.steps.append((waits, step, self.sem, 1))
        return (self.sem, self.count)

    def dma(self, out, in_, arrival, after=()):
        waits = self.held + [m for m in after if m is not None]
        self.held = []
        arrival.count += 16
        self.steps.append((waits, lambda e: e.dma_start(out, in_), arrival.sem, 16))
        return (arrival.sem, arrival.count)

    def emit(self, eng):
        passed = {}
        for waits, step, sem, by in self.steps:
            for s, v in waits:
                if passed.get(s.name, 0) < v:
                    eng.wait_ge(s, v)
                    passed[s.name] = v
            step(eng).then_inc(sem, by)


class Arrival:

    def __init__(self, sem):
        self.sem, self.count = sem, 0


class Region:

    def __init__(self, whole, lo, hi):
        self.whole, self.at, self.hi, self.peak = whole, lo, hi, lo

    def take(self, words, parts=P):
        lo = self.at
        self.at += words
        self.peak = max(self.peak, self.at)
        assert self.at <= self.hi, (self.at, self.hi)
        return self.whole[0:parts, lo:lo + words]


def build(nc, t, out):
    from contextlib import ExitStack
    ctx = ExitStack()
    with ctx:
        def sem(name):
            return ctx.enter_context(nc.semaphore(name))

        WORDS = 52600
        sb = ctx.enter_context(nc.sbuf_tensor("arena", [P, WORDS], F32))
        ps = ctx.enter_context(nc.psum_tensor("banks", [P, 4096], F32))
        arena = Region(sb, 0, WORDS)

        pe, act, dve, pool, sp = (Lane(sem("pe_done"), False), Lane(sem("act_done"), True),
                                  Lane(sem("dve_done"), True), Lane(sem("pool_done"), True),
                                  Lane(sem("sp_done"), False))
        lanes = [pe, act, dve, pool, sp]
        act.partner, dve.partner = dve, act
        arrivals = []

        def arrival(name):
            a = Arrival(sem(name))
            arrivals.append(a)
            return a

        def now():
            return [(l.sem, l.count) for l in lanes if l.count] + \
                   [(a.sem, a.count) for a in arrivals if a.count]

        def fence():
            marks = now()
            for l in (pe, act, dve, pool):
                l.held = list(marks)

        def tt(o, a, b, op, after=(), chain=True):
            return dve.do(lambda e: e.tensor_tensor(o, a, b, op), after, chain)

        def ts(o, a, s1, s2, op0, op1=None, after=(), chain=True):
            if op1 is None:
                return dve.do(lambda e: e.tensor_scalar(o, a, s1, None, op0), after, chain)
            return dve.do(lambda e: e.tensor_scalar(o, a, s1, s2, op0, op1), after, chain)

        def stt(o, a, s, b, op0, op1, after=(), chain=True):
            return dve.do(lambda e: e.scalar_tensor_tensor(o, a, s, b, op0, op1), after, chain)

        def scan(o, a, b, init, op0, op1, after=()):
            return dve.do(lambda e: e.tensor_tensor_scan(o, a, b, init, op0, op1), after)

        def vcopy(o, a, after=(), chain=True):
            return dve.do(lambda e: e.tensor_copy(o, a), after, chain)

        def red(o, a, op, after=(), negate=False):
            return dve.do(lambda e: e.tensor_reduce(o, a, AX, op, negate=negate), after)

        def rec(o, a, after=()):
            return dve.do(lambda e: e.reciprocal(o, a), after)

        def vset(o, v, after=()):
            return dve.do(lambda e: e.memset(o, v), after)

        def fn(o, a, f, after=(), chain=True, **k):
            return act.do(lambda e: e.activation(o, a, f, **k), after, chain)

        def indirect(o, o_rows, i, i_rows, arrival_, after):
            wrap = lambda r: None if r is None else bass.IndirectOffsetOnAxis(ap=r, axis=0)
            pool_steps = [m for m in after if m is not None]
            arrival_.count += 16
            if i_rows is None:
                step = lambda e: e.indirect_dma_start(out=o, out_offset=wrap(o_rows), in_=i,
                                                      in_offset=None)
            else:
                step = lambda e: e.indirect_dma_start(out=o, out_offset=None, in_=i,
                                                      in_offset=wrap(i_rows))
            pool.steps.append((pool.held + pool_steps, step, arrival_.sem, 16))
            pool.held = []
            return (arrival_.sem, arrival_.count)

        def acopy(o, a, after=(), chain=True):
            return act.do(lambda e: e.activation(o, a, ACT.Copy), after, chain)

        def mm(out_, pairs, after=()):
            mark = None
            for n, (l, r) in enumerate(pairs):
                first, last = n == 0, n == len(pairs) - 1
                mark = pe.do(lambda e, l=l, r=r, f=first, z=last: e.matmul(out_, l, r, start=f, stop=z),
                             after if first else ())
            return mark

        def tr(out_, in_, after=()):
            n = in_.shape[0]
            lo = in_.start_partition if isinstance(in_.start_partition, int) else in_.start_partition()
            return pe.do(lambda e: e.transpose(out_, in_, ident[lo:lo + n, lo:lo + n]), after)

        def bank(n, width=512):
            return ps[:, 512 * n:512 * n + width]

        class Banks:

            def __init__(self, banks):
                self.banks, self.n, self.free = banks, 0, {b: None for b in banks}

            def take(self):
                b = self.banks[self.n % len(self.banks)]
                self.n += 1
                return b, self.free[b]

        class Slots:

            def __init__(self, name, words, n, lane):
                self.bufs = [arena.take(words) for _ in range(n)]
                self.arr = [arrival(f"{name}{i}") for i in range(n)]
                self.n, self.free, self.lane = 0, [now() for _ in range(n)], lane

            def load(self, shape, sources, parts=P):
                i = self.n % len(self.bufs)
                self.n += 1
                v = shape(self.bufs[i])
                mark = None
                for pick, src in sources:
                    f = self.free[i]
                    mark = self.lane.dma(pick(v), src, self.arr[i], f if isinstance(f, list) else [f])
                return i, v, mark

        hn = nc.dram_tensor("norm_rows", (S, D), F32, kind="Internal").ap()
        slot_map = nc.dram_tensor("slot_map", (NBLK * P, 1), F32, kind="Internal").ap()
        yb = nc.dram_tensor("expert_rows", (NBLK * P, D), F32, kind="Internal").ap()
        a_rows = [arrival(f"norm_rows{n}_written") for n in range(2)]
        a_const = arrival("const_landed")
        cf = arena.take(t["c_f32"].shape[1])
        sp.dma(cf, t["c_f32"], a_const)
        ident = cf[:, 0:128]
        ones = cf[:, 128:256]
        scanmask = cf[:, 256:1280]
        at = 1280
        onehot = cf[0:4, at:at + 512].rearrange("p (h c) -> p h c", h=4)
        at += 512
        ov = cf[:, at:at + 16]
        at += 16
        iota8 = cf[:, at:at + 8]
        at += 8
        iota4 = iota8[:, 0:4]
        iota16 = cf[:, at:at + 16]
        steps128 = cf[:, at + 16:at + 16 + NOV]
        e128 = cf[:, at + 32:at + 64]
        tokid = cf[:, at + 64:at + 72]
        nb = t["c_bf16"].shape[1] // 2
        cb = arena.take(nb).bitcast(BF16)
        sp.dma(cb, t["c_bf16"], a_const)
        ident_b = cb[:, 0:128]
        causal_n = cb[:, 128:256]
        causal_t = cb[:, 256:384]
        win_mask = cb[:, 384:768]
        swa_mask = cb[:, 768:1024]
        ones_b = cb[:, 7296:7424]
        before_b = cb[:, 7424:7552]
        win_l = cb[0:6, 1024:1152]
        win_r = cb[0:6, 1152:1152 + 8 * 384].rearrange("p (h c) -> p h c", h=8)
        swa_r = cb[0:6, 4224:4224 + 8 * 384].rearrange("p (h c) -> p h c", h=8)
        m8 = arena.take(512).bitcast(BF16)
        sp.dma(m8, t["c_mask"], a_const)
        level_mask = m8.bitcast(mybir.dt.uint16).rearrange("p (l c) -> p l c", l=8)
        small = {}
        for name in ("g1pre", "g2pre", "gmix", "gffn", "gmoe", "lam", "s5d", "ldt", "lbl", "convw",
                     "gate_b", "sinks", "pos_k", "pos_v"):
            a = t[name]
            v = arena.take(a.shape[1], a.shape[0])
            sp.dma(v, a, a_const)
            small[name] = v
        consts = (a_const.sem, a_const.count)
        for l in (pe, act, dve, pool):
            l.held = [consts]

        XW = arena.take(NT * D)
        X = XW.rearrange("p (t d) -> p t d", t=NT)
        aTW = arena.take(KD * S)
        aT = aTW.rearrange("p (k s) -> p k s", k=KD)
        stat = arena.take(1024)
        base = arena.at

        def rstd_of(dst, src, n, after=()):
            ts(dst, src, 1.0 / n, EPS, ALU.mult, ALU.add, after)
            fn(dst, dst, ACT.Ln, [(dve.sem, dve.count)])
            return fn(dst, dst, ACT.Exp, scale=-0.5)

        def norm_to_T(gain, ready, scratch, rows_out=None):
            ring = Banks([0, 1, 2, 3])
            ss, rs = stat[:, 0:NT], stat[:, NT:2 * NT]
            for i in range(NT):
                m = act.do(lambda e, i=i: e.activation(scratch[:, 0:D], X[:, i, :], ACT.Square,
                                                       accum_out=ss[:, i:i + 1]), [ready[i]])
            r = rstd_of(rs, ss, D, [m])
            for i in range(NT):
                xs = scratch[:, D * (1 + i % 2):D * (2 + i % 2)]
                m = ts(xs, X[:, i, :], rs[:, i:i + 1], None, ALU.mult,
                       after=[r, norm_to_T.read[i % 2], norm_to_T.also[i % 2]])
                for half in range(2):
                    b, freed = ring.take()
                    for q in range(4):
                        k = 4 * half + q
                        mt = tr(bank(b)[:, P * q:P * q + P], xs[:, P * k:P * k + P], [m, freed])
                    g = gain[:, 4 * half:4 * half + 4].unsqueeze(2).broadcast_to([P, 4, P])
                    ring.free[b] = tt(aT[:, 4 * half:4 * half + 4, P * i:P * i + P],
                                      bank(b).rearrange("p (q c) -> p q c", q=4), g, ALU.mult, [mt])
                if rows_out is not None:
                    w_ = sp.dma(rows_out[P * i:P * i + P, :], xs, a_rows[i % 2], [m])
                norm_to_T.read[i % 2] = mt
                if rows_out is not None:
                    norm_to_T.also[i % 2] = w_
            norm_to_T.read = [None, None]
            return ring.free[b]

        norm_to_T.read = [None, None]
        norm_to_T.also = [None, None]

        a_x = [arrival(f"x{i}_landed") for i in range(NT)]
        xin = t["x"].rearrange("(t p) d -> t p d", p=P)
        ready = [sp.dma(X[:, i, :], xin[i], a_x[i]) for i in range(NT)]
        sp.held = []
        scratch = arena.take(3 * D)
        a_ready = norm_to_T(small["g1pre"], ready, scratch)
        fence()
        arena.at = base
        yT = XW.rearrange("p (k s) -> p k s", k=KD)

        wslots = Slots("w_landed", 2048, 2, sp)
        base_w = arena.at
        proj_banks = Banks([0, 1, 2, 3])
        turn = [0]

        def evac(o, i, after, chain=True):
            turn[0] += 1
            return acopy(o, i, after, chain) if turn[0] % 2 else vcopy(o, i, after, chain)

        def w_load(w, cols):
            src = w.rearrange("(k p) c -> p k c", p=P)
            picks, at_ = [], 0
            for c, n in cols:
                picks.append((lambda v, a=at_, n=n: v[:, :, a:a + n], src[:, :, c:c + n]))
                at_ += n
            return wslots.load(lambda b: b[:, 0:KD * at_].rearrange("p (k c) -> p k c", k=KD), picks)

        def proj_T(w, cols, dsts):
            slot, wv, landed = w_load(w, cols)
            for m, dst in enumerate(dsts):
                for n in range(2):
                    b, freed = proj_banks.take()
                    mk = mm(bank(b), [(wv[:, k, P * m:P * m + P], aT[:, k, 512 * n:512 * n + 512])
                                      for k in range(KD)], [landed, freed])
                    proj_banks.free[b] = e = evac(dst[:, 512 * n:512 * n + 512], bank(b), [mk])
            wslots.free[slot] = mk
            return e

        def proj_N(w, cols, put):
            width = sum(n for _, n in cols)
            slot, wv, landed = w_load(w, cols)
            for i in range(NT):
                b, freed = proj_banks.take()
                mk = mm(bank(b, width), [(aT[:, k, P * i:P * i + P], wv[:, k, :]) for k in range(KD)],
                        [landed, freed])
                proj_banks.free[b] = e = evac(put(i, bank(b, width))[0], put(i, bank(b, width))[1], [mk])
            wslots.free[slot] = mk
            return e

        def v2(w, a="a"):
            return w.rearrange("p (a s) -> p a s", a=2)

        def sigmoid_(o, i, tmp=None):
            return fn(o, i, ACT.Sigmoid, now())

        def head_norm_gate(o, sq, gate, col, extra):
            ss = stat[:, 64:96]
            m = tt(sq, o, o, ALU.mult, now())
            red(ss, sq.rearrange("p (n c) -> p n c", c=64), ALU.add)
            r = rstd_of(ss, ss, 64)
            ov_ = o.rearrange("p (n c) -> p n c", c=64)
            m = tt(ov_, ov_, ss.unsqueeze(2).broadcast_to([P, 32, 64]), ALU.mult, [r])
            if gate is not None:
                m = tt(o, o, gate, ALU.mult)
            o3 = o.rearrange("p (t c) -> p t c", t=NT)
            for f in range(2):
                for n in range(2):
                    b, freed = proj_banks.take()
                    for q in range(4):
                        mt = tr(bank(b)[:, P * q:P * q + P], o3[:, 4 * n + q, P * f:P * f + P], [m, freed])
                    proj_banks.free[b] = ts(yT[:, col + f, 512 * n:512 * n + 512], bank(b),
                                            small["gmix"][:, col + f:col + f + 1], None, ALU.mult,
                                            after=[mt])

        w_in = t["w_in"]

        u = arena.take(2 * S)
        uT = v2(u)
        proj_T(w_in, [(IN1["s5"], 256)], [uT[:, 0], uT[:, 1]])
        lam = small["lam"]
        lr, li = lam[:, 0:8], lam[:, 8:16]
        w8 = arena.take(8 * 16)
        sl = lambda n: w8[:, 8 * n:8 * n + 8]
        dt_, mag, cs, sn, th, kk, den, cfr, cfi, tmp, abr, abi, lrc, tm2 = (sl(n) for n in range(14))
        fn(dt_, small["ldt"], ACT.Exp)
        ts(lrc, lr, -1e-4, None, ALU.min)
        tt(tmp, lrc, dt_, ALU.mult, [(act.sem, act.count)])
        fn(mag, tmp, ACT.Exp, [(dve.sem, dve.count)])
        tt(th, li, dt_, ALU.mult)
        ts(kk, th, 1.0 / TWO_PI, ROUND, ALU.mult, ALU.add)
        ts(kk, kk, ROUND, None, ALU.subtract)
        for part in (6.28125, 0.0019350051879882812, 3.019916e-07):
            stt(th, kk, -part, th, ALU.mult, ALU.add)
        ts(th, th, 3.1415925, -3.1415925, ALU.min, ALU.max)
        stt(tmp, th, -1.0, th, ALU.mult, ALU.max)
        ts(tmp, tmp, -1.0, TWO_PI / 4, ALU.mult, ALU.add)
        fn(sn, th, ACT.Sin, [(dve.sem, dve.count)])
        m = fn(cs, tmp, ACT.Sin)
        tt(abr, mag, cs, ALU.mult, [m])
        tt(abi, mag, sn, ALU.mult)
        tt(den, lrc, lrc, ALU.mult)
        tt(tmp, li, li, ALU.mult)
        tt(den, den, tmp, ALU.add)
        rec(den, den)
        ts(tm2, abr, -1.0, None, ALU.add)
        tt(cfr, tm2, lrc, ALU.mult)
        tt(tmp, abi, li, ALU.mult)
        tt(cfr, cfr, tmp, ALU.add)
        tt(cfr, cfr, den, ALU.mult)
        tt(cfi, abi, lrc, ALU.mult)
        tt(tmp, tm2, li, ALU.mult)
        tt(cfi, cfi, tmp, ALU.subtract)
        tt(cfi, cfi, den, ALU.mult)
        braw = arena.take(4 * 256)
        a_s5 = arrival("s5_params_landed")
        bR, bI, cR, cI = (braw[:, 256 * n:256 * n + 256] for n in range(4))
        for n, nm in enumerate(("b_re", "b_im", "c_re", "c_im")):
            s5l = sp.dma(braw[:, 256 * n:256 * n + 256], t[nm], a_s5, now())
        glu = arena.take(512).rearrange("p (k c) -> p k c", k=2)
        s5l = sp.dma(glu, t["w_glu"].rearrange("(k p) c -> p k c", p=P), a_s5, now())
        bb = arena.take(512)
        bt = arena.take(512)
        tb = arena.take(256)
        r3 = lambda a: a.rearrange("p (j c) -> p j c", j=8)
        bc = lambda a: a.unsqueeze(2).broadcast_to([P, 8, 32])
        tt(r3(bb[:, 0:256]), r3(bR), bc(cfr), ALU.mult, [s5l])
        tt(r3(tb), r3(bI), bc(cfi), ALU.mult)
        tt(bb[:, 0:256], bb[:, 0:256], tb, ALU.subtract)
        tt(r3(bb[:, 256:512]), r3(bI), bc(cfr), ALU.mult)
        tt(r3(tb), r3(bR), bc(cfi), ALU.mult)
        tt(bb[:, 256:512], bb[:, 256:512], tb, ALU.add)
        m = ts(cI, cI, -1.0, None, ALU.mult)
        for q in range(4):
            mt = tr(bank(4)[:, P * q:P * q + P], bb[:, P * q:P * q + P], [m])
        m_bt = vcopy(bt, bank(4), [mt])
        s5_y = arena.take(2 * S)
        yS = v2(s5_y)
        cos_t, sin_t, zr, zi, t1, t2, br_, bi_ = (arena.take(S) for _ in range(8))
        fence()
        for j in range(8):
            f, r0 = j // 4, 32 * (j % 4)
            c0 = vset(cos_t[:, 0:1], 1.0)
            vset(sin_t[:, 0:1], 0.0)
            cn, s_n = cs[:, j:j + 1], sn[:, j:j + 1]
            n = 1
            while n < S:
                if n > 1:
                    tt(tmp[:, 0:1], cos_t[:, n - 1:n], cs[:, j:j + 1], ALU.mult)
                    tt(tm2[:, 0:1], sin_t[:, n - 1:n], sn[:, j:j + 1], ALU.mult)
                    tt(kk[:, 0:1], tmp[:, 0:1], tm2[:, 0:1], ALU.subtract)
                    tt(tmp[:, 0:1], sin_t[:, n - 1:n], cs[:, j:j + 1], ALU.mult)
                    tt(tm2[:, 0:1], cos_t[:, n - 1:n], sn[:, j:j + 1], ALU.mult)
                    tt(kk[:, 1:2], tmp[:, 0:1], tm2[:, 0:1], ALU.add)
                    cn, s_n = kk[:, 0:1], kk[:, 1:2]
                ts(t1[:, 0:n], sin_t[:, 0:n], s_n, None, ALU.mult)
                stt(cos_t[:, n:2 * n], cos_t[:, 0:n], cn, t1[:, 0:n], ALU.mult, ALU.subtract)
                ts(t1[:, 0:n], cos_t[:, 0:n], s_n, None, ALU.mult)
                stt(sin_t[:, n:2 * n], sin_t[:, 0:n], cn, t1[:, 0:n], ALU.mult, ALU.add)
                n *= 2
            for n in range(2):
                cols = slice(512 * n, 512 * n + 512)
                rhs = uT[r0:r0 + 32, f, cols]
                before = now()
                mm(bank(4), [(bt[r0:r0 + 32, P * f:P * f + P], rhs)], before)
                mk = mm(bank(5), [(bt[r0:r0 + 32, 256 + P * f:256 + P * f + P], rhs)])
                acopy(br_[:, cols], bank(4), [mk])
                acopy(bi_[:, cols], bank(5))
            tt(t1, cos_t, br_, ALU.mult, now())
            tt(t2, sin_t, bi_, ALU.mult)
            tt(t1, t1, t2, ALU.add)
            tt(t2, cos_t, bi_, ALU.mult)
            tt(zi, sin_t, br_, ALU.mult)
            tt(t2, t2, zi, ALU.subtract)
            mg = mag[:, j:j + 1].broadcast_to([P, S])
            scan(zr, mg, t1, 0.0, ALU.mult, ALU.add)
            scan(zi, mg, t2, 0.0, ALU.mult, ALU.add)
            tt(t1, cos_t, zr, ALU.mult)
            tt(t2, sin_t, zi, ALU.mult)
            tt(br_, t1, t2, ALU.subtract)
            tt(t1, sin_t, zr, ALU.mult)
            tt(t2, cos_t, zi, ALU.mult)
            m = tt(bi_, t1, t2, ALU.add)
            for n in range(2):
                cols = slice(512 * n, 512 * n + 512)
                o = ps[r0:r0 + 32, 512 * (6 + n):512 * (7 + n)]
                mk = mm(o, [(cR[:, 32 * j:32 * j + 32], br_[:, cols]),
                            (cI[:, 32 * j:32 * j + 32], bi_[:, cols])], [m] + now())
            if j % 4 == 3:
                for n in range(2):
                    cols = slice(512 * n, 512 * n + 512)
                    m = stt(yS[:, f, cols], uT[:, f, cols], small["s5d"][:, f:f + 1], bank(6 + n),
                            ALU.mult, ALU.add, [mk])
        fence()
        g_, q_ = arena.take(2 * S), arena.take(2 * S)
        tt(g_, s5_y, s5_y, ALU.mult)
        ts(g_, g_, 0.044715, 1.0, ALU.mult, ALU.add)
        tt(g_, g_, s5_y, ALU.mult)
        fn(g_, g_, ACT.Sigmoid, scale=2.0 * 0.7978845608028654)
        m = tt(g_, g_, s5_y, ALU.mult)
        gT = v2(g_)
        qT = v2(q_)
        for f in range(2):
            for n in range(2):
                b, freed = proj_banks.take()
                mk = mm(bank(b), [(glu[:, k, P * f:P * f + P], gT[:, k, 512 * n:512 * n + 512])
                                  for k in range(2)], [m, freed])
                proj_banks.free[b] = acopy(qT[:, f, 512 * n:512 * n + 512], bank(b), [mk])
        sigmoid_(q_, q_)
        tt(g_, g_, q_, ALU.mult)
        m = tt(q_, g_, g_, ALU.mult)
        for n in range(2):
            b, freed = proj_banks.take()
            mk = mm(bank(b), [(ones, qT[:, k, 512 * n:512 * n + 512]) for k in range(2)], [m, freed])
            rr = t1[:, 0:512]
            r = rstd_of(rr, bank(b), GW, [mk])
            proj_banks.free[b] = r
            for f in range(2):
                stt(yT[:, f, 512 * n:512 * n + 512], gT[:, f, 512 * n:512 * n + 512],
                    small["gmix"][:, f:f + 1], rr, ALU.mult, ALU.mult, [r])
        fence()
        arena.at = base_w

        hq, hz, hv = (arena.take(2 * S) for _ in range(3))
        proj_T(w_in, [(IN1["hq"], 256)], [v2(hq)[:, 0], v2(hq)[:, 1]])
        proj_T(w_in, [(IN1["hf"], 256)], [v2(hz)[:, 0], v2(hz)[:, 1]])
        hv3 = hv.rearrange("p (t c) -> p t c", t=NT)
        proj_N(w_in, [(IN1["hi"], 256)], lambda i, b: (hv3[:, i, :], b))
        hb, hk, hE = (arena.take(2 * S) for _ in range(3))
        Z = [arena.take(2 * S), hz]
        lb = stat[:, 128:130]
        lbp = stat[:, 130:132]
        tt(lb, small["lbl"], small["lbl"], ALU.subtract)
        fn(lbp, lb, ACT.Exp, [(dve.sem, dve.count)])
        rec(lb, lbp, [(act.sem, act.count)])
        tt(lbp, lbp, lb, ALU.mult)
        tt(lb, lbp, lbp, ALU.subtract)
        ts(lb, lb, 0.0, None, ALU.max)
        ts(lbp, lb, -1.0, 1.0, ALU.mult, ALU.add)
        stt(hE, hz, -1.0, hz, ALU.mult, ALU.max, now())
        fn(hE, hE, ACT.Exp, [(dve.sem, dve.count)], scale=-1.0)
        m = fn(hE, hE, ACT.Ln, bias=1.0)
        stt(hE, hz, 0.0, hE, ALU.min, ALU.subtract, [m])
        m = tt(hk, hE, hz, ALU.subtract)
        fn(hk, hk, ACT.Exp, [m])
        ts(hb, hz, -1.0, 60.0, ALU.mult, ALU.min)
        fn(hb, hb, ACT.Exp, [(dve.sem, dve.count)])
        m = (act.sem, act.count)
        for f in range(2):
            ts(v2(hb)[:, f], v2(hb)[:, f], lb[:, f:f + 1], None, ALU.mult, after=[m])
            ts(v2(hk)[:, f], v2(hk)[:, f], lbp[:, f:f + 1], None, ALU.mult)
        m = fn(hb, hb, ACT.Ln, [(dve.sem, dve.count)], bias=1.0)
        tt(hE, hE, hb, ALU.add, [m])
        for f in range(2):
            scan(v2(hb)[:, f], scanmask, v2(hE)[:, f], 0.0, ALU.mult, ALU.add)
        b3 = hb.rearrange("p (n c) -> p n c", c=P)
        E3 = hE.rearrange("p (n c) -> p n c", c=P)
        qb = Z[0]
        dec = stat[:, 132:148]
        m = fn(hE, hb, ACT.Exp, [(dve.sem, dve.count)])
        m = fn(dec, b3[:, :, P - 1:P].rearrange("p n c -> p (n c)"), ACT.Exp)
        tt(qb, hq, hE, ALU.mult, [m])
        tt(E3, b3, b3[:, :, P - 1:P].broadcast_to([P, 16, P]), ALU.subtract)
        m = fn(hE, hE, ACT.Exp, [(dve.sem, dve.count)], scale=-1.0)
        kb = hz
        m = tt(kb, hk, hE, ALU.mult, [m])
        kN = arena.take(2 * S)
        kN3 = kN.rearrange("p (t c) -> p t c", t=NT)
        kb3 = v2(kb)
        for c in range(NT):
            b, freed = proj_banks.take()
            for f in range(2):
                mt = tr(bank(b)[:, P * f:P * f + P], kb3[:, f, P * c:P * c + P], [m, freed])
            proj_banks.free[b] = e = evac(kN3[:, c, :], bank(b, 256), [mt])
        kb_read = mt
        U4 = ps[:, 2048:3072].rearrange("p (c f v) -> p c f v", c=8, f=2)
        before = now()
        for c in range(NT - 1):
            for h in range(4):
                mk = mm(ps[64 * (h % 2):64 * (h % 2) + 64, 2048 + 128 * c + 64 * (h // 2):
                           2048 + 128 * c + 64 * (h // 2) + 64],
                        [(kN3[:, c, 64 * h:64 * h + 64], hv3[:, c, 64 * h:64 * h + 64])], before)
        Sh = arena.take(1024).rearrange("p (c f v) -> p c f v", c=8, f=2)
        vset(Sh[:, 0], 0.0)
        dec2 = dec.rearrange("p (f c) -> p f c", f=2)
        for c in range(NT - 1):
            for f in range(2):
                m_state = stt(Sh[:, c + 1, f, :], Sh[:, c, f, :], dec2[:, f, c:c + 1], U4[:, c, f, :],
                              ALU.mult, ALU.add, [mk])
        acc = arena.take(8 * 512)
        acc5 = acc.rearrange("p (r c f t) -> p r c f t", r=2, c=8, f=2)
        vset(acc, 0.0)
        sbanks = Banks([0, 1, 2, 3])
        o_n = kN
        o3 = o_n.rearrange("p (t c) -> p t c", t=NT)
        inter = Banks([6, 7])
        o_int = arena.take(2 * S)
        oi3 = o_int.rearrange("p (t c) -> p t c", t=NT)
        qb3 = v2(qb)
        oi5 = o_int.rearrange("p (t f r c) -> p t f r c", t=NT, f=2, r=2)
        for c0 in range(0, NT, 4):
            for r in range(2):
                b, freed = inter.take()
                r0 = 64 * r
                for c in range(c0, c0 + 4):
                    for f in range(2):
                        mk = mm(bank(b)[:, 128 * (c - c0) + 64 * f:128 * (c - c0) + 64 * f + 64],
                                [(qb3[r0:r0 + 64, f, P * c:P * c + P], Sh[r0:r0 + 64, c, f, :])],
                                [m_state, freed, m])
                inter.free[b] = evac(oi5[:, c0:c0 + 4, :, r, :],
                                     bank(b).rearrange("p (t f c) -> p t f c", t=4, f=2), [mk])
        z_read = [mk, kb_read]
        hk3, hq3 = v2(hk), v2(hq)
        for level in range(LEVELS + 1):
            if level < LEVELS:
                H = 1 << level
                Zl = Z[(level + 1) % 2]
                nb_ = 2 * S // (2 * H)
                bl = hb.rearrange("p (n c) -> p n c", c=2 * H)
                El = hE.rearrange("p (n c) -> p n c", c=2 * H)
                Zv = Zl.rearrange("p (n c) -> p n c", c=2 * H)
                kv = hk.rearrange("p (n c) -> p n c", c=2 * H)
                qv = hq.rearrange("p (n c) -> p n c", c=2 * H)
                m = tt(El, bl, bl[:, :, H - 1:H].broadcast_to([P, nb_, 2 * H]), ALU.subtract,
                       [(act.sem, act.count)])
                fn(El[:, :, 0:H], El[:, :, 0:H], ACT.Exp, [m], scale=-1.0)
                m = fn(El[:, :, H:2 * H], El[:, :, H:2 * H], ACT.Exp)
                tt(Zv[:, :, 0:H], El[:, :, 0:H], kv[:, :, 0:H], ALU.mult, [m, z_read[(level + 1) % 2]])
                m = tt(Zv[:, :, H:2 * H], El[:, :, H:2 * H], qv[:, :, H:2 * H], ALU.mult)
                left = right = v2(Zl)
            else:
                left, right = hk3, hq3
            for c0 in range(0, NT, 2):
                for r in range(2):
                    b, freed = sbanks.take()
                    r0 = 64 * r
                    for q in range(4):
                        c, f = c0 + q // 2, q % 2
                        mk = mm(bank(b)[:, P * q:P * q + P],
                                [(left[r0:r0 + 64, f, P * c:P * c + P],
                                  right[r0:r0 + 64, f, P * c:P * c + P])], [m, freed])
                    msk = level_mask[:, level:level + 1, :].broadcast_to([P, 4, P])
                    dst = acc5[:, r, c0:c0 + 2].rearrange("p c f t -> p (c f) t")
                    sbanks.free[b] = m_acc = dve.do(
                        lambda e, dst=dst, b=b, msk=msk: e.copy_predicated(
                            dst, msk, bank(b).rearrange("p (h t) -> p h t", h=4)), [mk])
            z_read[(level + 1) % 2] = mk
        for c in range(NT):
            b, freed = inter.take()
            for h in range(4):
                mk = mm(bank(b)[:, 64 * h:64 * h + 64],
                        [(acc5[:, h % 2, c, h // 2, :], hv3[:, c, 64 * h:64 * h + 64])], [m_acc, freed])
            inter.free[b] = tt(o3[:, c, :], oi3[:, c, :], bank(b, 256), ALU.add,
                               [mk, (act.sem, act.count)])
        fence()
        hgt = hb
        hg3 = hgt.rearrange("p (t c) -> p t c", t=NT)
        proj_N(w_in, [(IN1["hg"], 256)], lambda i, b: (hg3[:, i, :], b))
        sigmoid_(hE, hgt)
        tt(hgt, hgt, hE, ALU.mult)
        head_norm_gate(o_n, hE, hgt, 2, None)
        fence()
        arena.at = base_w

        gates = arena.take(NT * 12)
        g3 = gates.rearrange("p (t c) -> p t c", t=NT)
        proj_N(w_in, [(IN1["ff"], 4), (IN1["mi"], 8)], lambda i, b: (g3[:, i, :], b))
        rows = arena.take(7 * S, 4)
        fF, wI, mM, lF, tR, sR, zR = (rows[:, S * n:S * n + S] for n in range(7))
        gb = small["gate_b"]

        def gate_rows(dst, c0, bias):
            for n in range(2):
                b, freed = proj_banks.take()
                for q in range(4):
                    mt = tr(bank(b)[0:4, P * q:P * q + P], g3[:, 4 * n + q, c0:c0 + 4], [freed] + now())
                proj_banks.free[b] = ts(dst[:, 512 * n:512 * n + 512], bank(b)[0:4], bias, None,
                                        ALU.add, after=[mt])

        def log_sigmoid_rows(dst, src):
            stt(sR, src, -1.0, src, ALU.mult, ALU.max, now())
            fn(sR, sR, ACT.Exp, [(dve.sem, dve.count)], scale=-1.0)
            m = fn(sR, sR, ACT.Ln, bias=1.0)
            return stt(dst, src, 0.0, sR, ALU.min, ALU.subtract, [m])

        onesrow = zR
        vset(onesrow, 1.0)
        gate_rows(tR, 0, gb[:, 0:1])
        log_sigmoid_rows(tR, tR)
        scan(fF, onesrow, tR, 0.0, ALU.mult, ALU.add)
        ts(fF, fF, -8.0, None, ALU.mult)
        gate_rows(tR, 8, gb[:, 2:3])
        log_sigmoid_rows(tR, tR)
        scan(lF, onesrow, tR, 0.0, ALU.mult, ALU.add)
        gate_rows(tR, 4, gb[:, 1:2])
        tt(wI, tR, lF, ALU.subtract)
        ts(sR, wI, 0.0, None, ALU.mult)
        scan(mM, sR, wI, 0.0, ALU.add, ALU.max)
        ts(tR, mM, -1.0, None, ALU.mult)
        tt(sR, mM, lF, ALU.add)
        m = fn(sR, sR, ACT.Exp, [(dve.sem, dve.count)], scale=-1.0)
        wN = arena.take(32).rearrange("p (t h) -> p t h", t=NT)
        eN = arena.take(32).rearrange("p (t h) -> p t h", t=NT)
        before = now()
        for src, o in ((wI, wN), (sR, eN)):
            b, freed = proj_banks.take()
            for i in range(NT):
                mt = tr(bank(b)[:, 4 * i:4 * i + 4], src[:, P * i:P * i + P], before + [freed])
            proj_banks.free[b] = vcopy(o.rearrange("p t h -> p (t h)"), bank(b, 32), [mt])
        base_g = arena.at

        def span(n):
            return next(c for c in (128, 256, 512, 1024) if n <= c)

        class Attention:

            def __init__(self):
                self.Pm = [arena.take(S) for _ in range(2)]
                self.PT = [arena.take(S) for _ in range(2)]
                self.mneg, self.z, self.sk = arena.take(64), arena.take(64), arena.take(64)
                self.s_free, self.p_free, self.pt_free = [None] * 2, [None] * 2, [None] * 2
                self.t_ring = Banks([4, 5])
                self.n = 0
                self.o_free = [None, None]

            def run(self, tiles, finish, aside=None):
                Lane.turns = False
                batches = []
                for u_ in tiles:
                    st = span(u_["width"])
                    nh = min(1024 // st, u_["rows_of"])
                    for h in range(0, u_["heads"], nh):
                        batches.append((u_, st, list(range(h, h + nh)), h + nh == u_["heads"]))
                scored = turned = None
                for bt_ in batches + [None, None]:
                    cur = None if bt_ is None else self.scores(*bt_)
                    if turned is not None:
                        self.values(turned, finish)
                    turned = None if scored is None else self.turn(scored)
                    scored = cur
                    if aside is not None:
                        aside()
                Lane.turns = True

            def scores(self, u_, st, heads, last):
                p = self.n % 2
                self.n += 1
                w, i, nh = u_["width"], u_["tile"], len(heads)
                so = 1024 * p
                for m_, h in enumerate(heads):
                    for c0 in range(0, w, 512):
                        c1 = min(w, c0 + 512)
                        base_c = so + st * m_
                        extra = u_["bias"](h, c0, c1)
                        group = [(c0, c1, u_["q"](h), u_["k"](h, c0, c1))] + extra
                        for n, (lo, hi, l, r) in enumerate(group):
                            o = ps[:, base_c + lo:base_c + hi]
                            mk = pe.do(lambda e, o=o, l=l, r=r, a=n == 0, z=n == len(group) - 1:
                                       e.matmul(o, l, r, start=a, stop=z), [self.s_free[p]])
                slot = 8 * (i % 4) + heads[0]
                mn, zz = self.mneg[:, slot:slot + nh], self.z[:, slot:slot + nh]
                sc = ps[:, so:so + st * nh].rearrange("p (h c) -> p h c", c=st)[:, :, 0:w]
                if u_.get("sinks") is None:
                    red(mn, sc, ALU.max, [mk], negate=True)
                    m = ts(mn, mn, 0.125, None, ALU.mult)
                else:
                    sk, sink = self.sk[:, slot:slot + nh], u_["sinks"][:, heads[0]:heads[0] + nh]
                    red(mn, sc, ALU.max, [mk])
                    stt(mn, mn, 0.125, sink, ALU.mult, ALU.max)
                    m = ts(mn, mn, -1.0, None, ALU.mult)
                    m_sk = tt(sk, sink, mn, ALU.add)
                Pm = self.Pm[p]
                for m_ in range(nh):
                    e_ = act.do(lambda e, m_=m_: e.activation(
                        Pm[:, w * m_:w * m_ + w], sc[:, m_, :], ACT.Exp, bias=mn[:, m_:m_ + 1],
                        scale=0.125, accum_out=zz[:, m_:m_ + 1]), [m, mk, self.p_free[p]], chain=False)
                self.s_free[p] = e_
                if u_.get("sinks") is not None:
                    k_ = fn(sk, sk, ACT.Exp, [m_sk])
                    self.s_free[p] = e_
                    tt(zz, zz, sk, ALU.add, [k_])
                    rec(zz, zz)
                else:
                    rec(zz, zz, [e_])
                return dict(u=u_, p=p, e=e_, heads=heads, last=last)

            def turn(self, c):
                u_, p, heads = c["u"], c["p"], c["heads"]
                per = u_["width"] // P
                nbk = per * len(heads)
                Pm, PT = self.Pm[p], self.PT[p]
                ev = []
                for b0 in range(0, nbk, 4):
                    n = min(4, nbk - b0)
                    b, freed = self.t_ring.take()
                    for q in range(n):
                        mt = tr(bank(b)[:, P * q:P * q + P], Pm[:, P * (b0 + q):P * (b0 + q) + P],
                                [c["e"], freed])
                    self.t_ring.free[b] = e_ = evac(PT[:, P * b0:P * (b0 + n)], bank(b, P * n),
                                                    [mt, self.pt_free[p]], chain=False)
                    ev += [e_] * n
                self.p_free[p] = mt
                return dict(c, ev=ev)

            def values(self, c, finish):
                u_, p, heads, ev, PT = c["u"], c["p"], c["heads"], c["ev"], self.PT[c["p"]]
                per = u_["width"] // P
                ob = u_["tile"] % 2
                for m_, h in enumerate(heads):
                    col = 512 * (6 + ob) + 64 * h
                    for n in range(per):
                        j = per * m_ + n
                        mk = pe.do(lambda e, j=j, n=n, h=h, col=col: e.matmul(
                            ps[:, col:col + 64], PT[:, P * j:P * j + P], u_["v"](h, n),
                            start=(n == 0), stop=(n == per - 1)), [ev[j], self.o_free[ob]])
                self.pt_free[p] = mk
                if c["last"]:
                    n = u_["heads"]
                    lo = 8 * (u_["tile"] % 4)
                    self.o_free[ob] = finish(u_["tile"], ps[:, 512 * (6 + ob):512 * (6 + ob) + 64 * n],
                                             self.z[:, lo:lo + n], [mk])

        fq, fk, fv = (arena.take(2 * S) for _ in range(3))
        fv3 = fv.rearrange("p (t c) -> p t c", t=NT)
        for c, dst in ((IN1["fq"], fq), (IN1["fk"], fk)):
            proj_T(w_in, [(c + 64 * h, 64) for h in (0, 2, 1, 3)], [v2(dst)[:, 0], v2(dst)[:, 1]])
        proj_N(w_in, [(IN1["fv"], 256)], lambda i, b: (fv3[:, i, :], b))
        o_f = arena.take(2 * S)
        of3 = o_f.rearrange("p (t c) -> p t c", t=NT)
        att = Attention()
        fq3, fk3 = v2(fq), v2(fk)
        fence()

        def fox_tile(i):
            w = P * (i + 1)
            part = lambda h: slice(64 * (h // 2), 64 * (h // 2) + 64)

            def bias(h, c0, c1):
                got = [(c0, c1, onehot[:, h, :], fF[:, c0:c1])]
                if c1 == w:
                    got.append((w - P, w, ident_b, causal_n))
                return got

            return dict(q=lambda h: fq3[part(h), h % 2, P * i:P * i + P],
                        k=lambda h, c0, c1: fk3[part(h), h % 2, c0:c1], width=w, bias=bias,
                        v=lambda h, n: fv3[:, n, 64 * h:64 * h + 64], tile=i, heads=4, rows_of=2)

        def fox_finish(i, o, rz, after):
            return tt(of3[:, i, :].rearrange("p (h c) -> p h c", h=4),
                      o.rearrange("p (h c) -> p h c", h=4), rz.unsqueeze(2).broadcast_to([P, 4, 64]),
                      ALU.mult, after)

        att.run([fox_tile(i) for i in range(NT)], fox_finish)
        fence()
        head_norm_gate(o_f, fq, None, 4, None)
        fence()
        arena.at = base_g

        mq, mk_, cq, ck, mtmp = (arena.take(2 * S) for _ in range(5))
        mva = arena.take(8 * 4 * 65)
        mva4 = mva.rearrange("p (t h c) -> p t h c", t=NT, h=4)
        proj_T(w_in, [(IN1["mq"], 256)], [v2(mq)[:, 0], v2(mq)[:, 1]])
        proj_T(w_in, [(IN1["mk"], 256)], [v2(mk_)[:, 0], v2(mk_)[:, 1]])
        vset(mva4[:, :, :, 64:65], 1.0)
        proj_N(w_in, [(IN1["mv"], 256)], lambda i, b: (mva4[:, i, :, 0:64],
                                                      b.rearrange("p (h c) -> p h c", h=4)))
        fence()
        cw = small["convw"]
        for n, (src, dst) in enumerate(((mq, cq), (mk_, ck))):
            for f in range(2):
                a, o = v2(src)[:, f], v2(dst)[:, f]
                ct = 2 * n + f
                ts(o, a, cw[:, 4 * ct + 3:4 * ct + 4], None, ALU.mult)
                for lag in (1, 2, 3):
                    stt(o[:, lag:S], a[:, 0:S - lag], cw[:, 4 * ct + 3 - lag:4 * ct + 4 - lag],
                        o[:, lag:S], ALU.mult, ALU.add)
            sigmoid_(src, dst)
            if n == 0:
                tt(dst, dst, src, ALU.mult)
            else:
                stt(dst, dst, 0.125, src, ALU.mult, ALU.mult)
        o_m = mq
        om3 = o_m.rearrange("p (t c) -> p t c", t=NT)
        cq3, ck3 = v2(cq), v2(ck)
        nm = arena.take(4 * S).rearrange("p (h s) -> p h s", h=4)
        before = now()
        for h in range(4):
            for n in range(2):
                b, freed = proj_banks.take()
                cols = slice(512 * n, 512 * n + 512)
                mk1 = mm(bank(b), [(onehot[:, h, :], tR[:, cols])], before + [freed])
                proj_banks.free[b] = acopy(nm[:, h, cols], bank(b), [mk1])
        fence()
        Wt = [mk_[:, 0:S], mk_[:, S:2 * S]]
        Pt = [mtmp[:, 0:S], mtmp[:, S:2 * S]]
        s_free, w_free, pt_free, o_free = [None] * 2, [None] * 2, [None] * 2, [None] * 2
        dn = stat[:, 256:288]
        pending = None
        units = [(i, h) for i in range(NT) for h in range(4)]
        for n, un in enumerate(units + [None]):
            cur = None
            if un is not None:
                i, h = un
                p = n % 2
                r0, f = 64 * (h % 2), h // 2
                first = [s_free[p]]
                for j in range(i + 1):
                    mks = mm(ps[:, 1024 * p + P * j:1024 * p + P * j + P],
                             [(ck3[r0:r0 + 64, f, P * j:P * j + P], cq3[r0:r0 + 64, f, P * i:P * i + P])],
                             first)
                    src, wd_ = nm[:, h, P * i:P * i + P], Wt[p][:, P * j:P * j + P]
                    md = None
                    if j == i:
                        md = tt(wd_, src, causal_t, ALU.add, [w_free[p]])
                        src = wd_
                    mw = fn(wd_, src, ACT.Exp, [w_free[p], md], bias=wN[:, j, h:h + 1])
                w_ = P * (i + 1)
                mt = tt(Pt[p][:, 0:w_], ps[:, 1024 * p:1024 * p + w_], Wt[p][:, 0:w_], ALU.mult,
                        [mks, mw, pt_free[p]])
                s_free[p] = w_free[p] = mt
                cur = (i, h, p, mt)
            if pending is not None:
                i, h, p, mt = pending
                ob = i % 2
                col = 512 * (6 + ob) + 65 * h
                mkv = mm(ps[:, col:col + 65], [(Pt[p][:, P * j:P * j + P], mva4[:, j, h, :])
                                               for j in range(i + 1)], [mt, o_free[ob]])
                pt_free[p] = mkv
                if h == 3:
                    o4 = ps[:, 512 * (6 + ob):512 * (6 + ob) + 260].rearrange("p (h c) -> p h c", h=4)
                    d_ = dn[:, 4 * i:4 * i + 4]
                    d3 = d_.unsqueeze(2)
                    vcopy(d3, o4[:, :, 64:65], [mkv])
                    stt(d_, d_, -1.0, d_, ALU.mult, ALU.max)
                    tt(d_, d_, eN[:, i, :], ALU.max)
                    rec(d_, d_)
                    o_free[ob] = tt(om3[:, i, :].rearrange("p (h c) -> p h c", h=4), o4[:, :, 0:64],
                                    d3.broadcast_to([P, 4, 64]), ALU.mult)
            pending = cur
        fence()
        mo = cq
        mo3 = mo.rearrange("p (t c) -> p t c", t=NT)
        proj_N(w_in, [(IN1["mo"], 256)], lambda i, b: (mo3[:, i, :], b))
        sigmoid_(mo, mo)
        head_norm_gate(o_m, mtmp, mo, 6, None)
        fence()
        arena.at = base_w

        def post_norm_residual(F3, gain_src, tag):
            gb_ = arena.take(D)
            a_g = arrival("gain_" + tag)
            gl = sp.dma(gb_, gain_src.partition_broadcast(P), a_g, now())
            sq = arena.take(D)
            ss = stat[:, 300:308]
            for i in range(NT):
                m = act.do(lambda e, i=i: e.activation(sq, F3[:, i, :], ACT.Square,
                                                       accum_out=ss[:, i:i + 1]), [gl])
            r = rstd_of(ss, ss, D, [m])
            for i in range(NT):
                stt(F3[:, i, :], F3[:, i, :], ss[:, i:i + 1], gb_, ALU.mult, ALU.mult, [r, gl])
                m = tt(X[:, i, :], X[:, i, :], F3[:, i, :], ALU.add)
            return m

        def proj_out_N(w, srcT, kt, dst, tag):
            for c in range(4):
                slot, wv, landed = wslots.load(
                    lambda b: b[:, 0:kt * 256].rearrange("p (k c) -> p k c", k=kt),
                    [(lambda v: v, w.rearrange("(k p) c -> p k c", p=P)[:, :, 256 * c:256 * c + 256])])
                for i in range(NT):
                    b, freed = proj_banks.take()
                    mk = mm(bank(b, 256), [(srcT[:, k, P * i:P * i + P], wv[:, k, :]) for k in range(kt)],
                            [landed, freed])
                    proj_banks.free[b] = e = evac(dst[:, i, 256 * c:256 * c + 256], bank(b, 256), [mk])
                wslots.free[slot] = mk
            return e

        F1 = aTW.rearrange("p (t d) -> p t d", t=NT)
        proj_out_N(t["w_out"], yT, KD, F1, "wo")
        fence()
        ready = [sp.dma(X[:, i, :], xin[i], a_x[i], now()) for i in range(NT)]
        for l in (act, dve):
            l.held = l.held + ready
        post_norm_residual(F1, t["g1post"], "mix")
        fence()
        arena.at = base_w
        scratch = arena.take(3 * D)
        norm_to_T(small["g2pre"], [None] * NT, scratch)
        fence()
        arena.at = base_w

        NF = FF // P
        hT = arena.take(NF * S).rearrange("p (f s) -> p f s", f=NF)
        tmp4 = [arena.take(512) for _ in range(4)]
        fb = Banks([0, 1, 2, 3, 4, 5, 6, 7])
        tfree = [None] * 4

        def swiglu(gate_b, up_b, o, after, k):
            tp = tmp4[k % 4]
            m = fn(tp, bank(gate_b), ACT.Silu, after + [tfree[k % 4]], chain=False)
            m = tt(o, tp, bank(up_b), ALU.mult, [m], chain=False)
            tfree[k % 4] = m
            fb.free[gate_b] = fb.free[up_b] = m
            return m

        kcount = [0]
        Lane.turns = False
        for f in range(NF):
            gsl = wslots.load(lambda b: b[:, 0:2048].rearrange("p (w k c) -> p w k c", w=2, k=KD),
                              [(lambda v, n=n: v[:, n], w.rearrange("(k p) c -> p k c", p=P)
                                [:, :, P * f:P * f + P]) for n, w in enumerate((t["w_fg"], t["w_fu"]))])
            slot, wv, landed = gsl
            for n in range(2):
                cols = slice(512 * n, 512 * n + 512)
                bg, f1 = fb.take()
                mm(bank(bg), [(wv[:, 0, k, :], aT[:, k, cols]) for k in range(KD)], [landed, f1])
                bu, f2 = fb.take()
                mk = mm(bank(bu), [(wv[:, 1, k, :], aT[:, k, cols]) for k in range(KD)], [f2])
                swiglu(bg, bu, hT[:, f, cols], [mk], kcount[0])
                kcount[0] += 1
            wslots.free[slot] = mk
        fence()
        wd = t["w_fd"].rearrange("(f p) c -> p f c", p=P)
        dfree = [None] * NT
        for n in range(2):
            f = 0
            while f < NF:
                nf = min(4, NF - f)
                slot, wv, landed = wslots.load(
                    lambda b: b[:, 0:nf * 512].rearrange("p (k c) -> p k c", k=nf),
                    [(lambda v: v, wd[:, f:f + nf, 512 * n:512 * n + 512])])
                for i in range(NT):
                    for q in range(nf):
                        mk = pe.do(lambda e, i=i, q=q, f=f, wv=wv: e.matmul(
                            bank(i), hT[:, f + q, P * i:P * i + P], wv[:, q, :],
                            start=(f + q == 0), stop=(f + q == NF - 1)),
                            [landed, dfree[i] if f + q == 0 else None])
                wslots.free[slot] = mk
                f += nf
            for i in range(NT):
                dfree[i] = evac(F1[:, i, 512 * n:512 * n + 512], bank(i), [mk])
        fence()
        arena.at = base_w
        Lane.turns = True
        post_norm_residual(F1, t["g2post"], "ffn")
        fence()
        arena.at = base_w

        scratch = arena.take(3 * D)
        norm_to_T(small["gffn"], [None] * NT, scratch)
        fence()
        arena.at = base_w
        w2 = t["w_in_2"]

        OA = arena.take(NT * 512).rearrange("p (t c) -> p t c", t=NT)
        qa = arena.take(4 * S).rearrange("p (a s) -> p a s", a=4)
        gN = arena.take(NT * 24)
        gN3 = gN.rearrange("p (t c) -> p t c", t=NT)
        BL = arena.take(S // 2).bitcast(BF16)
        a_bl = arrival("bias_rows_landed")
        bl_landed = sp.dma(BL[32:P, :], t["c_bl"][32:P, :], a_bl, now())
        base_2 = arena.at

        def heads_proj(c, dst):
            for i in range(0, 4, 2):
                proj_T(w2, [(c + 64 * h, 64) for h in (i, i + 4, i + 1, i + 5)],
                       [dst[:, i], dst[:, i + 1]])

        heads_proj(IN2["q"], qa)
        proj_N(w2, [(IN2["g"], 24)], lambda i, b: (gN3[:, i, :], b))
        sigmoid_(gN, gN)

        kcT = arena.take(64)
        vcN = arena.take(128).rearrange("p (g c) -> p g c", g=2)
        base_c = arena.at
        kvc = arena.take(2 * S)
        kv2 = v2(kvc)
        proj_T(w2, [(IN2["kc"], 256)], [kv2[:, 0], kv2[:, 1]])
        w1 = arena.take(32 * 256).rearrange("p (l c) -> p l c", l=32)
        w2s = arena.take(2 * 2 * 64).rearrange("p (n k c) -> p n k c", n=2, k=2)
        a_w1 = arrival("cmp_w1_landed")
        a_w2 = arrival("cmp_w2_landed")
        for n, nm_ in enumerate(("cmp_w2_k", "cmp_w2_v")):
            w2_landed = sp.dma(w2s[:, n], t[nm_].rearrange("(k p) c -> p k c", p=P), a_w2, now())
        AB = [arena.take(S) for _ in range(2)]
        hid = arena.take(2 * 2 * 64).rearrange("p (m g c) -> p m g c", m=2, g=2)
        vset(kcT, 0.0)
        vset(vcN, 0.0)
        for n, (wn, pos) in enumerate((("cmp_w1_k", "pos_k"), ("cmp_w1_v", "pos_v"))):
            before = now()
            src = t[wn].rearrange("(l d) c -> d l c", d=64)
            sp.dma(w1[0:64], src, a_w1, before)
            w1_landed = sp.dma(w1[64:128], src, a_w1)
            kv3 = kv2[:, n].rearrange("p (c l) -> p c l", l=16)
            for half in range(2):
                pv = small[pos][:, 16 * half:16 * half + 16].unsqueeze(1).broadcast_to([P, 64, 16])
                m = tt(AB[half].rearrange("p (c l) -> p c l", l=16), kv3, pv, ALU.add,
                       before if half == 0 else ())
            for mt_ in range(2):
                for g in range(2):
                    r0 = 64 * g
                    pairs = []
                    for l in range(32):
                        a3 = AB[l // 16].rearrange("p (c l) -> p c l", l=16)
                        c0 = l // 16
                        pairs.append((w1[r0:r0 + 64, l, P * mt_:P * mt_ + P],
                                      a3[r0:r0 + 64, c0:c0 + NC, l % 16]))
                    b, freed = proj_banks.take()
                    mk = mm(bank(b, NC), pairs, [m, w1_landed, freed])
                    mh = fn(hid[:, mt_, g, 0:NC], bank(b, NC), ACT.Silu, [mk, (dve.sem, dve.count)])
                    proj_banks.free[b] = mh
            b, freed = proj_banks.take()
            if n == 0:
                for g in range(2):
                    r0 = 64 * g
                    mk = mm(bank(b)[r0:r0 + 64, 0:NC], [(w2s[:, 0, k, :], hid[:, k, g, 0:NC])
                                                       for k in range(2)], [mh, w2_landed, freed])
                proj_banks.free[b] = vcopy(kcT[:, 0:NC], bank(b, NC), [mk])
            else:
                for g in range(2):
                    for r0 in (0, 64):
                        mk = mm(bank(b)[r0:r0 + NC, 64 * g:64 * g + 64],
                                [(hid[:, k, g, 0:NC], w2s[:, 1, k, :]) for k in range(2)],
                                [mh, w2_landed, freed])
                vcopy(vcN[0:NC].rearrange("p g c -> p (g c)"), bank(b)[0:NC, 0:128], [mk])
                proj_banks.free[b] = vcopy(vcN[64:64 + NC].rearrange("p g c -> p (g c)"),
                                           bank(b)[64:64 + NC, 0:128])
        fence()
        arena.at = base_c
        cslots = Slots("cmp_bias_landed", 512 + 64, 2, sp)
        pc = [arena.take(512) for _ in range(2)]
        pTc = arena.take(512)
        sc_ = arena.take(64)
        top = arena.take(16)
        pen = arena.take(32)
        cm = arena.take(16)
        g24 = gN.rearrange("p (t h b) -> p t h b", t=NT, h=8)
        for i in range(NT):
            slot, cv, landed = cslots.load(lambda b: b[:, 0:512 + 64], [
                (lambda v: v, t["c_cmp"].rearrange("(t p) c -> t p c", p=P)[i])])
            before = now()
            for h in range(8):
                r0 = 64 * (h // 4)
                mk = mm(bank(h // 4)[:, 64 * (h % 4):64 * (h % 4) + 64],
                        [(qa[r0:r0 + 64, h % 4, P * i:P * i + P], kcT[r0:r0 + 64, :])], before)
            p_ = pc[i % 2]
            p3 = p_.rearrange("p (h c) -> p h c", h=8)
            mx, zz = cm[:, 0:8], cm[:, 8:16]
            for g in range(2):
                half = slice(256 * g, 256 * g + 256)
                stt(p_[:, half], bank(g, 256), 0.125, cv[:, half], ALU.mult, ALU.add, [mk, landed])
            red(mx, p3, ALU.max)
            ts(mx, mx, -1e29, None, ALU.max)
            m = tt(p3, p3, mx.unsqueeze(2).broadcast_to([P, 8, 64]), ALU.subtract)
            m = fn(p_, p_, ACT.Exp, [m])
            red(zz, p3, ALU.add, [m])
            ts(zz, zz, 1e-30, None, ALU.max)
            rec(zz, zz)
            m = tt(p3, p3, zz.unsqueeze(2).broadcast_to([P, 8, 64]), ALU.mult)
            for q in range(4):
                mt = tr(bank(2)[:, P * q:P * q + P], p_[:, P * q:P * q + P], [m])
            m = vcopy(pTc, bank(2), [mt])
            for g in range(2):
                mk = mm(bank(3)[:, 16 * g:16 * g + 16],
                        [(pTc[:, P * q:P * q + P], ov) for q in (2 * g, 2 * g + 1)], [m])
            for h in range(8):
                r0 = 64 * (h % 2)
                mo_ = mm(bank(5 + h % 2)[:, 64 * (h // 2):64 * (h // 2) + 64],
                         [(pTc[r0:r0 + 64, P * (h // 2):P * (h // 2) + P],
                           vcN[r0:r0 + 64, h // 4, :])], [m])
            keep, add = cv[:, 512:544], cv[:, 544:576]
            tt(sc_[:, 0:32], bank(3, 32), keep, ALU.mult, [mk])
            tt(sc_[:, 0:32], sc_[:, 0:32], add, ALU.add)
            for g in range(2):
                dve.do(lambda e, g=g: e.max(top[:, 8 * g:8 * g + 8], sc_[:, 16 * g:16 * g + 16]))
                dve.do(lambda e, g=g: e.match_replace(sc_[:, 32 + 16 * g:48 + 16 * g],
                                                      top[:, 8 * g:8 * g + 8],
                                                      sc_[:, 16 * g:16 * g + 16], -3e38))
            m = ts(pen, sc_[:, 32:64], -1e38, NEG, ALU.is_gt, ALU.mult)
            mt = tr(bank(4)[0:32, 0:P], pen, [m])
            vcopy(BL[0:32, P * i:P * i + P], bank(4)[0:32, 0:P], [mt])
            for r in range(2):
                gate = g24[:, i, :, 0:1].rearrange("p (f r) b -> p f r b", r=2)[:, :, r, :]
                cslots.free[slot] = tt(OA[:, i, :].rearrange("p (f r c) -> p f r c", f=4, r=2)[:, :, r, :],
                                       bank(5 + r, 256).rearrange("p (f c) -> p f c", f=4),
                                       gate.broadcast_to([P, 4, 64]), ALU.mult, [mo_])
        fence()
        arena.at = base_2

        kx = arena.take(2 * S)
        vx = arena.take(NT * 256)
        kx2 = v2(kx)
        vx3 = vx.rearrange("p (t c) -> p t c", t=NT)
        proj_T(w2, [(IN2["ks"], 128), (IN2["kw"], 128)], [kx2[:, 0], kx2[:, 1]])
        proj_N(w2, [(IN2["vs"], 128), (IN2["vw"], 128)], lambda i, b: (vx3[:, i, :], b))
        BR = arena.take(8 * S // 2).bitcast(BF16)
        BR3 = BR.rearrange("p (h s) -> p h s", h=8)
        br_landed = sp.dma(BR, t["c_br"], a_bl, now())
        att = Attention()
        coef = arena.take(8)
        prod = arena.take(512)
        fence()

        def tile_2(i, q, kT, V, vcol, w, k_lo, bias, sinks=None):
            part = lambda h: slice(64 * (h // 4), 64 * (h // 4) + 64)
            return dict(q=lambda h: q[part(h), h % 4, P * i:P * i + P],
                        k=lambda h, c0, c1: kT[part(h), k_lo + c0:k_lo + c1], width=w, bias=bias,
                        v=lambda h, n: V[:, k_lo // P + n,
                                         vcol + 64 * (h // 4):vcol + 64 * (h // 4) + 64],
                        tile=i, heads=8, rows_of=4, sinks=sinks)

        def gated_finish(branch):
            def finish(i, o, rz, after):
                tt(coef.unsqueeze(2), rz.unsqueeze(2), g24[:, i, :, branch:branch + 1], ALU.mult)
                m = tt(prod.rearrange("p (h c) -> p h c", h=8), o.rearrange("p (h c) -> p h c", h=8),
                       coef.unsqueeze(2).broadcast_to([P, 8, 64]), ALU.mult, after)
                tt(OA[:, i, :], OA[:, i, :], prod, ALU.add)
                return m
            return finish

        def slc_tile(i):
            w = P * (i + 1)

            def bias(h, c0, c1):
                got = [(c0, c1, BL[:, P * i:P * i + P], BR3[:, h, c0:c1])]
                if c1 == w:
                    got.append((w - P, w, ident_b, causal_n))
                return got
            return tile_2(i, qa, kx2[:, 0], vx3, 0, w, 0, bias)

        def band_tile(i, q, kT, V, vcol, nprev, mask, rows_r, sinks=None):
            nb1 = min(i, nprev) + 1
            skip = P * (nprev + 1 - nb1)
            rs = P * (2 - nprev) + skip

            def bias(h, c0, c1):
                return [(c0, c1, win_l, rows_r[:, h, rs + c0:rs + c1]),
                        (c0, c1, ident_b, mask[:, skip + c0:skip + c1])]
            return tile_2(i, q, kT, V, vcol, P * nb1, P * (i + 1 - nb1), bias, sinks)

        att.run([slc_tile(i) for i in range(NT)], gated_finish(1))
        att.run([band_tile(i, qa, kx2[:, 1], vx3, 128, 2, win_mask, win_r) for i in range(NT)],
                gated_finish(2))
        fence()
        arena.at = base_2

        OB = arena.take(NT * 512).rearrange("p (t c) -> p t c", t=NT)
        base_o = arena.at
        kb_ = arena.take(S)
        vb_ = arena.take(NT * 128)
        vb3 = vb_.rearrange("p (t c) -> p t c", t=NT)
        heads_proj(IN2["qb"], qa)
        proj_T(w2, [(IN2["kb"], 128)], [kb_])
        proj_N(w2, [(IN2["vb"], 128)], lambda i, b: (vb3[:, i, :], b))
        att = Attention()
        fence()

        def swa_finish(i, o, rz, after):
            return tt(OB[:, i, :].rearrange("p (h c) -> p h c", h=8),
                      o.rearrange("p (h c) -> p h c", h=8), rz.unsqueeze(2).broadcast_to([P, 8, 64]),
                      ALU.mult, after)

        att.run([band_tile(i, qa, kb_, vb3, 0, 1, swa_mask, swa_r, small["sinks"])
                 for i in range(NT)], swa_finish)
        fence()

        arena.at = base_o
        OAT = arena.take(4 * S).rearrange("p (k s) -> p k s", k=4)
        OBT = arena.take(4 * S).rearrange("p (k s) -> p k s", k=4)
        for src, dst in ((OA, OAT), (OB, OBT)):
            for k in range(4):
                for n in range(2):
                    b, freed = proj_banks.take()
                    for q in range(4):
                        mt = tr(bank(b)[:, P * q:P * q + P], src[:, 4 * n + q, P * k:P * k + P], [freed])
                    proj_banks.free[b] = evac(dst[:, k, 512 * n:512 * n + 512], bank(b), [mt])
        fence()
        keep_at = arena.at
        arena.at = base_w
        mixT = arena.take(8 * S).rearrange("p (k s) -> p k s", k=8)
        arena.at = keep_at
        assert base_w + 8 * S <= base_2
        pslots = Slots("wab_landed", 1024, 2, act)
        keep_at = arena.at
        arena.at = base_2
        tmp4 = [arena.take(512) for _ in range(4)]
        arena.at = keep_at
        tfree = [None] * 4
        m8b = Banks([0, 1, 2, 3, 4, 5, 6, 7])
        k8 = 0
        r_wa = t["w_a"].rearrange("(k p) c -> p k c", p=P)
        r_wb = t["w_b"].rearrange("(k p) c -> p k c", p=P)
        for c in range(8):
            slot, wv, landed = w_load(w2, [(IN2["ga"] + P * c, P), (IN2["gb"] + P * c, P)])
            s2, wab, landed2 = pslots.load(
                lambda b: b.rearrange("p (n k c) -> p n k c", n=2, k=4),
                [(lambda v, n=n: v[:, n], w[:, :, P * c:P * c + P]) for n, w in enumerate((r_wa, r_wb))])
            for n in range(2):
                cols = slice(512 * n, 512 * n + 512)
                parts = []
                for br2, oT in enumerate((OAT, OBT)):
                    b1, f1 = m8b.take()
                    mg_ = mm(bank(b1), [(wv[:, k, P * br2:P * br2 + P], aT[:, k, cols])
                                        for k in range(KD)], [landed, f1])
                    b2, f2 = m8b.take()
                    mp_ = mm(bank(b2), [(wab[:, br2, k, :], oT[:, k, cols]) for k in range(4)],
                             [landed2, f2])
                    tp = tmp4[k8 % 4]
                    m = fn(tp, bank(b1), ACT.Sigmoid, [mg_, tfree[k8 % 4]])
                    m8b.free[b1] = m
                    m8b.free[b2] = tt(tp, tp, bank(b2), ALU.mult, [mp_, m])
                    parts.append((tp, k8 % 4))
                    k8 += 1
                m = tt(mixT[:, c, cols], parts[0][0], parts[1][0], ALU.add)
                tfree[parts[0][1]] = tfree[parts[1][1]] = m
            wslots.free[slot] = mp_
            pslots.free[s2] = mp_
        fence()
        for c in range(4):
            slot, wv, landed = w_load(t["w_o"], [(256 * c, 256)])
            for i in range(NT):
                b, freed = proj_banks.take()
                mk = mm(bank(b, 256), [(mixT[:, k, P * i:P * i + P], wv[:, k, :]) for k in range(KD)],
                        [landed, freed])
                xs = X[:, i, 256 * c:256 * c + 256]
                proj_banks.free[b] = tt(xs, xs, bank(b, 256), ALU.add, [mk])
            wslots.free[slot] = mk
        fence()
        arena.at = base_w
        scratch = arena.take(3 * D)
        norm_to_T(small["gmoe"], [None] * NT, scratch, hn)
        fence()
        arena.at = base_w

        eslots = Slots("expert_landed", 6144, 3, sp)
        lg = arena.take(NT * 36)
        lg3 = lg.rearrange("p (t c) -> p t c", t=NT)
        bias36 = arena.take(36)
        a_b36 = arrival("router_bias_landed")
        b36 = sp.dma(bias36, t["b_router"].partition_broadcast(P), a_b36, now())
        proj_N(t["w_router"], [(0, 36)], lambda i, b: (lg3[:, i, :], b))
        tt(lg3, lg3, bias36.unsqueeze(1).broadcast_to([P, NT, 36]), ALU.add, now())
        rt = arena.take(1024)
        gm = rt[:, 0:8]
        oh = rt[:, 32:64].rearrange("p (t c) -> p t c", t=NT)
        eq = rt[:, 64:128]
        ein = rt[:, 128:192].rearrange("p (t c) -> p t c", t=NT)
        m1 = rt[:, 192:256].rearrange("p (t c) -> p t c", t=NT)
        m2 = rt[:, 256:320].rearrange("p (t c) -> p t c", t=NT)
        v1, v2_, pg, p1, p2, ix = (rt[:, 320 + 8 * n:328 + 8 * n] for n in range(6))
        we = rt[:, 384:448].rearrange("p (t c) -> p t c", t=NT)
        tm = rt[:, 448:512].rearrange("p (t c) -> p t c", t=NT)
        bc3 = lambda a, n: a.unsqueeze(2).broadcast_to([P, NT, n])

        def first_max(vals, n, value, hot, io):
            red(value, vals, ALU.max)
            tt(hot, vals, bc3(value, n), ALU.is_equal)
            ts(hot, hot, -64.0, 64.0, ALU.mult, ALU.add)
            tt(hot, hot, io.unsqueeze(1).broadcast_to([P, NT, n]), ALU.add)
            red(ix, hot, ALU.min)
            return tt(hot, hot, bc3(ix, n), ALU.is_equal)

        gl3 = lg3[:, :, 0:4]
        first_max(gl3, 4, gm, oh, iota4)
        t4 = eq[:, 0:32].rearrange("p (t c) -> p t c", t=NT)
        m = tt(t4, gl3, bc3(gm, 4), ALU.subtract)
        m = fn(t4, t4, ACT.Exp, [m])
        red(pg, t4, ALU.add, [m])
        rec(pg, pg)
        for g in range(NG):
            le = lg3[:, :, 4 + EG * g:4 + EG * g + EG]
            sel = oh[:, :, g:g + 1].broadcast_to([P, NT, EG])
            if g == 0:
                tt(ein, le, sel, ALU.mult)
            else:
                tt(tm, le, sel, ALU.mult)
                tt(ein, ein, tm, ALU.add)
        first_max(ein, 8, v1, m1, iota8)
        stt(tm, m1, NEG, ein, ALU.mult, ALU.add)
        first_max(tm, 8, v2_, m2, iota8)
        tt(p2, v2_, v1, ALU.subtract)
        m = fn(p2, p2, ACT.Exp, [(dve.sem, dve.count)])
        ts(p1, p2, 1.0, None, ALU.add, after=[m])
        rec(p1, p1)
        tt(p1, p1, pg, ALU.mult)
        tt(p2, p2, p1, ALU.mult)
        one1 = rt[:, 512:768].rearrange("p (t g e) -> p t g e", t=NT, g=NG)
        one2 = rt[:, 768:1024].rearrange("p (t g e) -> p t g e", t=NT, g=NG)
        for g in range(NG):
            sel = oh[:, :, g:g + 1].broadcast_to([P, NT, EG])
            tt(one1[:, :, g, :], m1, sel, ALU.mult)
            tt(one2[:, :, g, :], m2, sel, ALU.mult)
        o1 = one1.rearrange("p t g e -> p t (g e)")
        o2 = one2.rearrange("p t g e -> p t (g e)")
        chosen = arena.take(128).bitcast(BF16).rearrange("p (t e) -> p t e", t=NT)
        m = tt(chosen, o1, o2, ALU.add)
        before = now()
        for i in range(NT):
            pairs = [(ones_b, chosen[:, j, :]) for j in range(i)] + [(before_b, chosen[:, i, :])]
            mk = mm(bank(0)[:, NE * i:NE * i + NE], pairs, before)
        mk = mm(bank(1, NE), [(ones_b, chosen[:, j, :]) for j in range(NT)], before)
        posw = arena.take(2 * 256)
        pos = posw[:, 0:256].rearrange("p (t e) -> p t e", t=NT)
        far = posw[:, 256:512].rearrange("p (t e) -> p t e", t=NT)
        ew = arena.take(5 * NE)
        cnt, more, upto, shift, one_row = (ew[:, NE * n:NE * n + NE] for n in range(5))
        grid = arena.take(NE * NOV)
        vcopy(posw[:, 0:256], bank(0, 256), [mk])
        vcopy(cnt, bank(1, NE))
        g1 = grid.rearrange("p (e b) -> p e b", e=NE)
        tt(g1, cnt.unsqueeze(2).broadcast_to([P, NE, NOV]),
           steps128.unsqueeze(1).broadcast_to([P, NE, NOV]), ALU.is_gt)
        red(more, g1, ALU.add)
        vset(one_row, 1.0)
        scan(upto, one_row, more, 0.0, ALU.mult, ALU.add)
        g2 = grid.rearrange("p (b e) -> p b e", b=NOV)
        ov_e = arena.take(NOV)
        tt(g2, upto.unsqueeze(1).broadcast_to([P, NOV, NE]),
           iota16[:, 0:NOV].unsqueeze(2).broadcast_to([P, NOV, NE]), ALU.is_le)
        red(ov_e, g2, ALU.add)
        ts(ov_e, ov_e, float(NE - 1), None, ALU.min)
        ov_i = arena.take(NOV).bitcast(mybir.dt.int32)
        m_ov = vcopy(ov_i, ov_e)
        tt(shift, upto, more, ALU.subtract)
        ts(shift, shift, 128.0, 128.0 * (NE - 1), ALU.mult, ALU.add)
        tt(shift, shift, e128, ALU.subtract)
        rows3 = lambda a: a.unsqueeze(1).broadcast_to([P, NT, NE])
        ts(far, pos, 128.0, None, ALU.is_ge)
        tt(far, far, rows3(shift), ALU.mult)
        tt(pos, pos, far, ALU.add)
        tt(pos, pos, rows3(e128), ALU.add)
        dstf = arena.take(16)
        tt(far, pos, o1, ALU.mult)
        red(dstf[:, 0:8], far, ALU.add)
        tt(far, pos, o2, ALU.mult)
        red(dstf[:, 8:16], far, ALU.add)
        dsti = arena.take(16).bitcast(mybir.dt.uint32)
        m_dst = vcopy(dsti, dstf)
        zslot = grid[0:NBLK, 0:P]
        m = vset(zslot, 0.0)
        a_map = arrival("slot_map_cleared")
        cleared = sp.dma(slot_map.rearrange("(b s) o -> b (s o)", s=P), zslot, a_map, [m])
        a_sc = arrival("tokens_scattered")
        for k in range(2):
            for i in range(NT):
                scattered = indirect(slot_map, dsti[:, 8 * k + i:8 * k + i + 1], tokid[:, i:i + 1],
                                     None, a_sc, [cleared, m_dst])
        smap = arena.take(P)
        a_sm = arrival("slot_map_loaded")
        got = sp.dma(smap[0:NBLK, :], slot_map.rearrange("(b s) o -> b (s o)", s=P), a_sm, [scattered])
        mt = tr(bank(2)[:, 0:NBLK], smap[0:NBLK, :], [got] + now())
        idx = arena.take(NBLK).bitcast(mybir.dt.uint32)
        m_idx = vcopy(idx, bank(2, NBLK), [mt])
        fence()
        Lane.turns = False
        xg = [aTW[:, D * n:D * n + D] for n in range(3)]
        xgT = [aTW[:, D * (3 + n):D * (4 + n)].rearrange("p (k s) -> p k s", k=KD) for n in range(2)]
        yo = [aTW[:, D * (5 + n):D * (6 + n)] for n in range(3)]
        a_xg = [arrival(f"rows{n}_gathered") for n in range(3)]
        a_yo = [arrival(f"rows{n}_written") for n in range(3)]
        hid_ = [arena.take(256) for _ in range(2)]
        sg = [arena.take(256) for _ in range(2)]
        xg_free, xgT_free, yo_free, hid_free, sg_free = ([None] * 3, [None] * 2, [None] * 3,
                                                         [None] * 2, [None] * 2)
        tb_, ub_, db_ = Banks([0, 1]), Banks([2, 3]), Banks([4, 5, 6, 7])

        def expert_weights(b_):
            def shape(b):
                return b
            if b_ < NE:
                srcs = [(t["w_ge"][b_], 0, KD), (t["w_ue"][b_], 2048, KD), (t["w_de"][b_], 4096, 2)]
                return eslots.load(shape, [
                    (lambda v, lo=lo, k=k: v[:, lo:lo + 2048].rearrange("p (k c) -> p k c", k=k),
                     w.rearrange("(k p) c -> p k c", p=P)) for w, lo, k in srcs])
            i = eslots.n % len(eslots.bufs)
            eslots.n += 1
            v = eslots.bufs[i]
            arr = eslots.arr[i]
            number = {}
            free_ = eslots.free[i] if isinstance(eslots.free[i], list) else [eslots.free[i]]
            for n, (w, lo, k) in enumerate(((t["w_ge"], 0, KD), (t["w_ue"], 2048, KD),
                                            (t["w_de"], 4096, 2))):
                arr.count += 16

                def step(e, n=n, w=w, lo=lo, k=k):
                    if n == 0:
                        number["e"] = e.value_load(ov_i[0:1, b_ - NE:b_ - NE + 1], min_val=0,
                                                   max_val=NE - 1)
                    src = w[bass.ds(number["e"], 1)].rearrange("o (k p) c -> p (o k) c", p=P)
                    return e.dma_start(v[:, lo:lo + 2048].rearrange("p (k c) -> p k c", k=k), src)
                sp.steps.append((free_ + [m_ov], step,
                                 arr.sem, 16))
            return i, v, (arr.sem, arr.count)

        def block_up(b_):
            n3, n2 = b_ % 3, b_ % 2
            slot, wv, landed = expert_weights(b_)
            rows = indirect(xg[n3], None, hn, idx[:, b_:b_ + 1], a_xg[n3], [m_idx, xg_free[n3]])
            for half in range(2):
                b, freed = tb_.take()
                for q in range(4):
                    k = 4 * half + q
                    mt = tr(bank(b)[:, P * q:P * q + P], xg[n3][:, P * k:P * k + P], [rows, freed])
                g = small["gmoe"][:, 4 * half:4 * half + 4].unsqueeze(2).broadcast_to([P, 4, P])
                tb_.free[b] = e_ = tt(xgT[n2][:, 4 * half:4 * half + 4, :],
                                      bank(b).rearrange("p (q c) -> p q c", q=4), g, ALU.mult,
                                      [mt, xgT_free[n2]])
            xg_free[n3] = mt
            wg = wv[:, 0:2048].rearrange("p (k c) -> p k c", k=KD)
            wu = wv[:, 2048:4096].rearrange("p (k c) -> p k c", k=KD)
            b, freed = ub_.take()
            for n, w in enumerate((wg, wu)):
                for mt_ in range(2):
                    mk = mm(bank(b)[:, 256 * n + P * mt_:256 * n + P * mt_ + P],
                            [(w[:, k, P * mt_:P * mt_ + P], xgT[n2][:, k, :]) for k in range(KD)],
                            [e_, landed, freed])
            xgT_free[n2] = mk
            tp = sg[n2]
            m = fn(tp, bank(b, 256), ACT.Silu, [mk, sg_free[n2]], chain=False)
            m = tt(hid_[n2], tp, bank(b)[:, 256:512], ALU.mult, [m, hid_free[n2]], chain=False)
            sg_free[n2] = ub_.free[b] = m
            return b_, slot, wv, m

        def block_down(b_, slot, wv, ready_):
            n3, n2 = b_ % 3, b_ % 2
            wd_ = wv[:, 4096:6144].rearrange("p (k c) -> p k c", k=2)
            ev = []
            for n in range(2):
                b, freed = db_.take()
                mk = mm(bank(b), [(hid_[n2][:, P * k:P * k + P], wd_[:, k, 512 * n:512 * n + 512])
                                  for k in range(2)], [ready_, freed])
                db_.free[b] = acopy(yo[n3][:, 512 * n:512 * n + 512], bank(b), [mk, yo_free[n3]])
                ev.append(db_.free[b])
            eslots.free[slot] = mk
            hid_free[n2] = mk
            yo_free[n3] = act.dma(yb[P * b_:P * b_ + P, :], yo[n3], a_yo[n3], ev)

        pending = None
        for b_ in range(NBLK + 1):
            cur = block_up(b_) if b_ < NBLK else None
            if pending is not None:
                block_down(*pending)
            pending = cur
        yg = [aTW[:, D * n:D * n + D] for n in range(4)]
        a_yg = [arrival(f"results{n}_gathered") for n in range(4)]
        yg_free = [None] * 4
        pw = [p1, p2]
        allw = [(a.sem, a.count) for a in a_yo] + [(pe.sem, pe.count), (dve.sem, dve.count)]
        for i in range(NT):
            for k in range(2):
                n = (2 * i + k) % 4
                rows = indirect(yg[n], None, yb, dsti[:, 8 * k + i:8 * k + i + 1], a_yg[n],
                                allw + [yg_free[n]])
                yg_free[n] = stt(X[:, i, :], yg[n], pw[k][:, i:i + 1], X[:, i, :], ALU.mult, ALU.add,
                                 [rows])
        fence()
        arena.at = base_w

        gfin = arena.take(D)
        a_gf = arrival("final_gain_landed")
        gl = sp.dma(gfin, t["g_final"].partition_broadcast(P), a_gf, now())
        sq = arena.take(D)
        ss = stat[:, 0:8]
        for i in range(NT):
            m = act.do(lambda e, i=i: e.activation(sq, X[:, i, :], ACT.Square,
                                                   accum_out=ss[:, i:i + 1]))
        r = rstd_of(ss, ss, D, [m])
        a_out = arrival("out_written")
        outv = out.rearrange("(t p) d -> t p d", p=P)
        for i in range(NT):
            m = stt(X[:, i, :], X[:, i, :], ss[:, i:i + 1], gfin, ALU.mult, ALU.mult, [r, gl])
            stored = sp.dma(outv[i], X[:, i, :], a_out, [m])

        block = ctx.enter_context(nc.Block())

        @block.sync
        def _(eng):
            sp.emit(eng)
            eng.wait_ge(*stored)

        @block.tensor
        def _(eng):
            pe.emit(eng)

        @block.vector
        def _(eng):
            dve.emit(eng)

        @block.scalar
        def _(eng):
            act.emit(eng)

        if pool.steps:
            @block.gpsimd
            def _(eng):
                pool.emit(eng)


def shape_constants():
    bf = np.dtype("bfloat16")
    f32 = np.float32
    r = np.arange(P)
    c = np.zeros((P, 1280 + 512 + 16 + 8 + 72), f32)
    c[:, 1816:1832] = np.arange(16)[None, :]
    c[:, 1832:1832 + NOV] = 128.0 * np.arange(1, NOV + 1)[None, :]
    c[:, 1848:1880] = 128.0 * np.arange(32)[None, :]
    c[:, 1880:1888] = r[:, None] + 128 * np.arange(8)[None, :]
    c[:, 0:128] = np.eye(P)
    c[:, 128:256] = 1.0
    c[:, 256:1280] = (np.arange(S) % P != 0)[None, :]
    for h in range(4):
        c[h, 1280 + 128 * h:1280 + 128 * h + 128] = 1.0
    ov = np.zeros((64, 16))
    for b in range(NC):
        for j in range(16):
            ov[b, j] = max(min(16 * b + 32, 64 * j + 64) - max(16 * b, 64 * j), 0) / 32
    c[0:64, 1792:1808] = ov
    c[64:128, 1792:1808] = ov
    c[:, 1808:1816] = np.arange(8)[None, :]

    slopes = (2.0 ** (-8.0 * np.arange(1, 17) / 16)).astype(f32)
    swa, nsa = slopes[:8], slopes[8:]

    def parts(a):
        a = np.asarray(a, np.float64)
        got = []
        for _ in range(3):
            q = a.astype(bf)
            got.append(q)
            a = a - q.astype(np.float64)
        return got

    b = np.zeros((P, 4224 + 8 * 384 + 256), bf)
    b[:, 7296:7424] = 1.0
    b[:, 7424:7552] = r[:, None] < r[None, :]
    b[:, 0:128] = np.eye(P)
    b[:, 128:256] = np.where(r[None, :] > r[:, None], NEG, 0)
    b[:, 256:384] = np.where(r[:, None] > r[None, :], NEG, 0)
    kw = np.arange(384) - 256
    dist = r[:, None] - kw[None, :]
    b[:, 384:768] = np.where((dist >= 0) & (dist < 256), 0, NEG)
    b[:, 768:1024] = np.where((dist >= 0) & (dist < 128), 0, NEG)[:, 128:]
    for n in range(3):
        b[n, 1024:1152] = r
        b[3 + n, 1024:1152] = 1.0
    for lo, sl in ((1152, nsa), (4224, swa)):
        for h in range(8):
            for n, q in enumerate(parts(-8.0 * sl[h])):
                b[n, lo + 384 * h:lo + 384 * h + 384] = q
            for n, q in enumerate(parts(8.0 * sl[h].astype(np.float64) * kw)):
                b[3 + n, lo + 384 * h:lo + 384 * h + 384] = q

    mask = np.zeros((P, 8, P), bf)
    for l in range(LEVELS):
        same = (r[:, None] >> (l + 1)) == (r[None, :] >> (l + 1))
        mask[:, l] = same & (((r[None, :] >> l) & 1) == 1) & (((r[:, None] >> l) & 1) == 0)
    mask[:, 7] = np.eye(P)

    tok = np.arange(S)
    bl = np.zeros((P, S), bf)
    for n in range(3):
        bl[32 + n] = tok // 256 * 256
        bl[35 + n] = tok % 256
        bl[38 + n] = 1.0
    br = np.zeros((P, 8, S), bf)
    for h in range(8):
        for j in range(16):
            br[16 * (h // 4) + j, h, 64 * j:64 * j + 64] = 1.0
        for n, q in enumerate(parts(-8.0 * nsa[h])):
            br[32 + n, h] = q
            br[35 + n, h] = q
        for n, q in enumerate(parts(8.0 * nsa[h].astype(np.float64) * tok)):
            br[38 + n, h] = q

    cmp_ = np.full((S, 8, 64), NEG, f32)
    d = tok[:, None] - (np.arange(NC) * 16 + 31)[None, :]
    for h in range(8):
        cmp_[:, h, :NC] = np.where(d >= 0, -(nsa[h] * d.astype(f32)), f32(NEG))
    j = np.arange(16)[None, :]
    cur = tok[:, None] // 64
    forced = (j == 0) | (j == cur) | (j == cur - 1)
    valid = j * 64 <= tok[:, None]
    keep = (valid & ~forced).astype(f32)
    add = np.where(forced, 1e9, np.where(valid, 0, NEG)).astype(f32)
    table = np.concatenate([cmp_.reshape(S, 512), keep, keep, add, add], axis=1)
    return dict(c_f32=c, c_bf16=b, c_mask=mask.reshape(P, -1), c_bl=bl, c_br=br.reshape(P, -1),
                c_cmp=table)


def kernel(**inputs):
    import concourse.bacc as bacc
    from concourse.bass_utils import run_bass_kernel_spmd

    a = {k: np.asarray(v) for k, v in inputs.items()}
    f32 = np.float32

    def cols(v):
        return np.ascontiguousarray(v.reshape(-1, P).T)

    def states(v):
        return v.reshape(8, P).T

    def blocks(v):
        o = np.zeros((P, 8, 32), f32)
        w = v.reshape(8, 2, 64, 16)
        for g in range(2):
            o[64 * g:64 * g + 64, :, 16 * g:16 * g + 16] = w[:, g].transpose(1, 0, 2)
        return o.reshape(P, 256)

    x = {
        "x": a["x"][0], "w_in": a["w_in"][0],
        "g1pre": cols(a["ln_mix_pre"][0]), "g2pre": cols(a["ln_ffn_pre"][0]),
        "gmix": cols(a["mix_gain"][0]), "gffn": cols(a["norm_mix_g_2"][0]),
        "gmoe": cols(a["norm_ffn_g_2"][0]),
        "g1post": a["ln_mix_post"][0], "g2post": a["ln_ffn_post"][0], "g_final": a["norm_final_g_2"],
        "lam": np.concatenate([states(a["s5_lambda_re"][0]), states(a["s5_lambda_im"][0])], axis=1),
        "s5d": cols(a["s5_d"][0]),
        "ldt": states(np.repeat(a["s5_log_dt"][0][:, None], 64, axis=1)),
        "lbl": cols(a["hgrn_lb_logits"][0]),
        "convw": np.concatenate([a["mlstm_conv_w"][0][:, P * n:P * n + P].T for n in range(4)], axis=1),
        "gate_b": a["gate_bias"][0].reshape(3, 4).T,
        "sinks": np.broadcast_to(a["sinks_2"][0][None, :], (P, 8)),
        "pos_k": np.concatenate([a["cmp_pos_k_2"][0].T] * 2, axis=0),
        "pos_v": np.concatenate([a["cmp_pos_v_2"][0].T] * 2, axis=0),
        "b_re": blocks(a["s5_b_re"][0]), "b_im": blocks(a["s5_b_im"][0]),
        "c_re": blocks(a["s5_c_re"][0].transpose(0, 2, 1)),
        "c_im": blocks(a["s5_c_im"][0].transpose(0, 2, 1)),
        "w_glu": a["s5_w_glu"][0], "w_out": a["w_out"][0],
        "w_fg": a["w_ffn_gate"][0], "w_fu": a["w_ffn_up"][0], "w_fd": a["w_ffn_down"][0],
        "w_in_2": a["w_in_2"][0],
        "cmp_w1_k": a["cmp_w1_k_2"][0], "cmp_w1_v": a["cmp_w1_v_2"][0],
        "cmp_w2_k": a["cmp_w2_k_2"][0], "cmp_w2_v": a["cmp_w2_v_2"][0],
        "w_a": a["w_a_2"][0], "w_b": a["w_b_2"][0], "w_o": a["w_o_2"][0],
        "w_router": np.concatenate([a["w_group_2"][0], a["w_expert_2"][0]], axis=1),
        "b_router": np.concatenate([a["b_group_2"][0], a["b_expert_2"][0]]),
        "w_ge": a["w_gate_e_2"][0], "w_ue": a["w_up_e_2"][0], "w_de": a["w_down_e_2"][0],
    }
    x.update(shape_constants())
    nc = bacc.Bacc("TRN2", target_bir_lowering=False, num_devices=1)
    arrays, handles = {}, {}
    for name, v in x.items():
        v = np.ascontiguousarray(v)
        arrays["in_" + name] = v
        handles[name] = nc.dram_tensor("in_" + name, v.shape, mybir.dt.from_np(v.dtype),
                                       kind="ExternalInput").ap()
    out = nc.dram_tensor("out", (S, D), F32, kind="ExternalOutput").ap()
    build(nc, handles, out)
    r = run_bass_kernel_spmd(nc, [arrays], core_ids=[0])
    return r.results[0]["out"].reshape(1, S, D)
```

```python
import numpy as np
import concourse.bass as bass
from concourse import mybir
from concourse.alu_op_type import AluOpType as ALU

F32 = mybir.dt.float32
BF16 = mybir.dt.bfloat16
ACT = mybir.ActivationFunctionType
AX = mybir.AxisListType.X

P = 128
S = 1024
D = 1024
NT = S // P
KD = D // P
GW = 256
FF = 2816
EPS = 1e-6
NEG = -1e30
TWO_PI = 6.283185307179586
ROUND = 12582912.0

IN1 = dict(s5=0, hq=256, hf=512, hi=768, hg=1024, fq=1280, fk=1536, fv=1792, ff=2048,
           mq=2052, mk=2308, mv=2564, mo=2820, mi=3076, mf=3080)
IN2 = dict(q=0, kc=512, vc=640, ks=768, vs=896, kw=1024, vw=1152, g=1280, qb=1304, kb=1816,
           vb=1944, ga=2072, gb=3096)
NC = 63
NE, EG, NG, EF = 32, 8, 4, 256
NOV = (2 * S - 1) // P
NBLK = NE + NOV
NFIXED = NE + 1
GROUPS = [(NFIXED, NFIXED + 2), (NFIXED + 2, NFIXED + 6), (NFIXED + 6, NBLK)]
LEVELS = 7


class Lane:

    turns = True
    partner = None

    def __init__(self, sem, chained):
        self.sem, self.chained, self.count, self.steps, self.held = sem, chained, 0, [], []

    def do(self, step, after=(), chain=True):
        waits = self.held + [m for m in after if m is not None]
        self.held = []
        if self.chained and chain and self.count:
            waits.append((self.sem, self.count))
        if self.partner is not None and Lane.turns and self.partner.count:
            waits.append((self.partner.sem, self.partner.count))
        self.count += 1
        self.steps.append((waits, step, self.sem, 1))
        return (self.sem, self.count)

    def dma(self, out, in_, arrival, after=()):
        waits = self.held + [m for m in after if m is not None]
        self.held = []
        arrival.count += 16
        self.steps.append((waits, lambda e: e.dma_start(out, in_), arrival.sem, 16))
        return (arrival.sem, arrival.count)

    def begin_group(self):
        assert not self.held
        self.outer, self.steps = self.steps, []

    def end_group(self, over, ready, source, own):
        inner, self.steps = self.steps, self.outer
        self.steps.append((inner, over, ready, source, own))

    def emit(self, eng):
        self.number = None
        self.emit_steps(eng, self.steps, {}, {})

    def emit_steps(self, eng, steps, passed, signalled):
        for entry in steps:
            if isinstance(entry[0], list) and isinstance(entry[1], int):
                inner, over, ready, source, own = entry
                if self.number is None:
                    eng.wait_ge(*ready)
                    passed[ready[0].name] = max(passed.get(ready[0].name, 0), ready[1])
                    self.number = eng.value_load(source, min_val=0, max_val=NOV)
                adds = {}
                for _, _, sem, by in inner:
                    if sem.name in own:
                        continue
                    adds[sem.name] = (sem, adds.get(sem.name, (sem, 0))[1] + by)
                with eng.If(self.number > over):
                    self.emit_steps(eng, inner, dict(passed), {})
                with eng.If(self.number <= over):
                    for sem, by in adds.values():
                        if signalled.get(sem.name):
                            eng.wait_ge(sem, signalled[sem.name])
                    for sem, by in adds.values():
                        eng.sem_inc(sem, by)
                for sem, by in adds.values():
                    signalled[sem.name] = signalled.get(sem.name, 0) + by
                continue
            waits, step, sem, by = entry
            for s, v in waits:
                if passed.get(s.name, 0) < v:
                    eng.wait_ge(s, v)
                    passed[s.name] = v
            step(eng).then_inc(sem, by)
            signalled[sem.name] = signalled.get(sem.name, 0) + by


class Arrival:

    def __init__(self, sem):
        self.sem, self.count = sem, 0


class Region:

    def __init__(self, whole, lo, hi):
        self.whole, self.at, self.hi, self.peak = whole, lo, hi, lo

    def take(self, words, parts=P):
        lo = self.at
        self.at += words
        self.peak = max(self.peak, self.at)
        assert self.at <= self.hi, (self.at, self.hi)
        return self.whole[0:parts, lo:lo + words]


def build(nc, t, out):
    from contextlib import ExitStack
    ctx = ExitStack()
    with ctx:
        def sem(name):
            return ctx.enter_context(nc.semaphore(name))

        WORDS = 52600
        sb = ctx.enter_context(nc.sbuf_tensor("arena", [P, WORDS], F32))
        ps = ctx.enter_context(nc.psum_tensor("banks", [P, 4096], F32))
        arena = Region(sb, 0, WORDS)

        pe, act, dve, pool, sp = (Lane(sem("pe_done"), False), Lane(sem("act_done"), True),
                                  Lane(sem("dve_done"), True), Lane(sem("pool_done"), True),
                                  Lane(sem("sp_done"), False))
        lanes = [pe, act, dve, pool, sp]
        act.partner, dve.partner = dve, act
        arrivals = []

        def arrival(name):
            a = Arrival(sem(name))
            arrivals.append(a)
            return a

        def now():
            return [(l.sem, l.count) for l in lanes if l.count] + \
                   [(a.sem, a.count) for a in arrivals if a.count]

        def fence():
            marks = now()
            for l in (pe, act, dve, pool):
                l.held = list(marks)

        def tt(o, a, b, op, after=(), chain=True):
            return dve.do(lambda e: e.tensor_tensor(o, a, b, op), after, chain)

        def ts(o, a, s1, s2, op0, op1=None, after=(), chain=True):
            if op1 is None:
                return dve.do(lambda e: e.tensor_scalar(o, a, s1, None, op0), after, chain)
            return dve.do(lambda e: e.tensor_scalar(o, a, s1, s2, op0, op1), after, chain)

        def stt(o, a, s, b, op0, op1, after=(), chain=True):
            return dve.do(lambda e: e.scalar_tensor_tensor(o, a, s, b, op0, op1), after, chain)

        def scan(o, a, b, init, op0, op1, after=()):
            return dve.do(lambda e: e.tensor_tensor_scan(o, a, b, init, op0, op1), after)

        def vcopy(o, a, after=(), chain=True):
            return dve.do(lambda e: e.tensor_copy(o, a), after, chain)

        def red(o, a, op, after=(), negate=False):
            return dve.do(lambda e: e.tensor_reduce(o, a, AX, op, negate=negate), after)

        def rec(o, a, after=()):
            return dve.do(lambda e: e.reciprocal(o, a), after)

        def vset(o, v, after=()):
            return dve.do(lambda e: e.memset(o, v), after)

        def fn(o, a, f, after=(), chain=True, **k):
            return act.do(lambda e: e.activation(o, a, f, **k), after, chain)

        def indirect(o, o_rows, i, i_rows, arrival_, after):
            wrap = lambda r: None if r is None else bass.IndirectOffsetOnAxis(ap=r, axis=0)
            pool_steps = [m for m in after if m is not None]
            arrival_.count += 16
            if i_rows is None:
                step = lambda e: e.indirect_dma_start(out=o, out_offset=wrap(o_rows), in_=i,
                                                      in_offset=None)
            else:
                step = lambda e: e.indirect_dma_start(out=o, out_offset=None, in_=i,
                                                      in_offset=wrap(i_rows))
            pool.steps.append((pool.held + pool_steps, step, arrival_.sem, 16))
            pool.held = []
            return (arrival_.sem, arrival_.count)

        def acopy(o, a, after=(), chain=True):
            return act.do(lambda e: e.activation(o, a, ACT.Copy), after, chain)

        def mm(out_, pairs, after=()):
            mark = None
            for n, (l, r) in enumerate(pairs):
                first, last = n == 0, n == len(pairs) - 1
                mark = pe.do(lambda e, l=l, r=r, f=first, z=last: e.matmul(out_, l, r, start=f, stop=z),
                             after if first else ())
            return mark

        def tr(out_, in_, after=()):
            n = in_.shape[0]
            lo = in_.start_partition if isinstance(in_.start_partition, int) else in_.start_partition()
            return pe.do(lambda e: e.transpose(out_, in_, ident[lo:lo + n, lo:lo + n]), after)

        def bank(n, width=512):
            return ps[:, 512 * n:512 * n + width]

        class Banks:

            def __init__(self, banks):
                self.banks, self.n, self.free = banks, 0, {b: None for b in banks}

            def take(self):
                b = self.banks[self.n % len(self.banks)]
                self.n += 1
                return b, self.free[b]

        class Slots:

            def __init__(self, name, words, n, lane):
                self.bufs = [arena.take(words) for _ in range(n)]
                self.arr = [arrival(f"{name}{i}") for i in range(n)]
                self.n, self.free, self.lane = 0, [now() for _ in range(n)], lane

            def load(self, shape, sources, parts=P):
                i = self.n % len(self.bufs)
                self.n += 1
                v = shape(self.bufs[i])
                mark = None
                for pick, src in sources:
                    f = self.free[i]
                    mark = self.lane.dma(pick(v), src, self.arr[i], f if isinstance(f, list) else [f])
                return i, v, mark

        hn = nc.dram_tensor("norm_rows", (S, D), F32, kind="Internal").ap()
        slot_map = nc.dram_tensor("slot_map", (NBLK * P, 1), F32, kind="Internal").ap()
        yb = nc.dram_tensor("expert_rows", (NBLK * P, D), F32, kind="Internal").ap()
        a_rows = [arrival(f"norm_rows{n}_written") for n in range(2)]
        XW = arena.take(NT * D)
        X = XW.rearrange("p (t d) -> p t d", t=NT)
        a_x = [arrival(f"x{i}_landed") for i in range(NT)]
        xin = t["x"].rearrange("(t p) d -> t p d", p=P)
        ready = [sp.dma(X[:, i, :], xin[i], a_x[i]) for i in range(NT)]
        a_const = arrival("const_landed")
        cf = arena.take(t["c_f32"].shape[1])
        sp.dma(cf, t["c_f32"], a_const)
        ident = cf[:, 0:128]
        ones = cf[:, 128:256]
        scanmask = cf[:, 256:1280]
        at = 1280
        onehot = cf[0:4, at:at + 512].rearrange("p (h c) -> p h c", h=4)
        at += 512
        ov = cf[:, at:at + 16]
        at += 16
        iota8 = cf[:, at:at + 8]
        at += 8
        iota4 = iota8[:, 0:4]
        iota16 = cf[:, at:at + 16]
        steps128 = cf[:, at + 16:at + 16 + NOV]
        e128 = cf[:, at + 32:at + 64]
        tokid = cf[:, at + 64:at + 72]
        nb = t["c_bf16"].shape[1] // 2
        cb = arena.take(nb).bitcast(BF16)
        sp.dma(cb, t["c_bf16"], a_const)
        ident_b = cb[:, 0:128]
        causal_n = cb[:, 128:256]
        causal_t = cb[:, 256:384]
        win_mask = cb[:, 384:768]
        swa_mask = cb[:, 768:1024]
        ones_b = cb[:, 7296:7424]
        before_b = cb[:, 7424:7552]
        win_l = cb[0:6, 1024:1152]
        win_r = cb[0:6, 1152:1152 + 8 * 384].rearrange("p (h c) -> p h c", h=8)
        swa_r = cb[0:6, 4224:4224 + 8 * 384].rearrange("p (h c) -> p h c", h=8)
        m8 = arena.take(512).bitcast(BF16)
        sp.dma(m8, t["c_mask"], a_const)
        level_mask = m8.bitcast(mybir.dt.uint16).rearrange("p (l c) -> p l c", l=8)
        small = {}
        for name in ("g1pre", "g2pre", "gmix", "gffn", "gmoe", "lam", "s5d", "ldt", "lbl", "convw",
                     "gate_b", "sinks", "pos_k", "pos_v"):
            a = t[name]
            v = arena.take(a.shape[1], a.shape[0])
            sp.dma(v, a, a_const)
            small[name] = v
        consts = (a_const.sem, a_const.count)
        for l in (pe, act, dve, pool):
            l.held = [consts]

        aTW = arena.take(KD * S)
        aT = aTW.rearrange("p (k s) -> p k s", k=KD)
        stat = arena.take(1024)
        base = arena.at

        def rstd_of(dst, src, n, after=()):
            ts(dst, src, 1.0 / n, EPS, ALU.mult, ALU.add, after)
            fn(dst, dst, ACT.Ln, [(dve.sem, dve.count)])
            return fn(dst, dst, ACT.Exp, scale=-0.5)

        def norm_to_T(gain, ready, scratch, rows_out=None):
            ring = Banks([0, 1, 2, 3])
            ss, rs = stat[:, 0:NT], stat[:, NT:2 * NT]
            for i in range(NT):
                m = act.do(lambda e, i=i: e.activation(scratch[:, 0:D], X[:, i, :], ACT.Square,
                                                       accum_out=ss[:, i:i + 1]), [ready[i]])
            r = rstd_of(rs, ss, D, [m])
            for i in range(NT):
                xs = scratch[:, D * (1 + i % 2):D * (2 + i % 2)]
                m = fn(xs, X[:, i, :], ACT.Copy, [r, norm_to_T.read[i % 2], norm_to_T.also[i % 2]],
                       scale=rs[:, i:i + 1])
                for half in range(2):
                    b, freed = ring.take()
                    for q in range(4):
                        k = 4 * half + q
                        mt = tr(bank(b)[:, P * q:P * q + P], xs[:, P * k:P * k + P], [m, freed])
                    g = gain[:, 4 * half:4 * half + 4].unsqueeze(2).broadcast_to([P, 4, P])
                    ring.free[b] = tt(aT[:, 4 * half:4 * half + 4, P * i:P * i + P],
                                      bank(b).rearrange("p (q c) -> p q c", q=4), g, ALU.mult, [mt])
                if rows_out is not None:
                    w_ = sp.dma(rows_out[P * i:P * i + P, :], xs, a_rows[i % 2], [m])
                norm_to_T.read[i % 2] = mt
                if rows_out is not None:
                    norm_to_T.also[i % 2] = w_
            norm_to_T.read = [None, None]
            return ring.free[b]

        norm_to_T.read = [None, None]
        norm_to_T.also = [None, None]

        scratch = arena.take(3 * D)
        Lane.turns = False
        norm_to_T(small["g1pre"], ready, scratch)
        Lane.turns = True
        fence()
        arena.at = base
        yT = XW.rearrange("p (k s) -> p k s", k=KD)

        wslots = Slots("w_landed", 2048, 2, sp)
        base_w = arena.at
        proj_banks = Banks([0, 1, 2, 3])
        turn = [0]

        def evac(o, i, after, chain=True):
            turn[0] += 1
            return acopy(o, i, after, chain) if turn[0] % 2 else vcopy(o, i, after, chain)

        def w_load(w, cols):
            src = w.rearrange("(k p) c -> p k c", p=P)
            picks, at_ = [], 0
            for c, n in cols:
                picks.append((lambda v, a=at_, n=n: v[:, :, a:a + n], src[:, :, c:c + n]))
                at_ += n
            return wslots.load(lambda b: b[:, 0:KD * at_].rearrange("p (k c) -> p k c", k=KD), picks)

        aside_ = [None, 1]

        def aside(times):
            for _ in range(times * aside_[1]):
                if aside_[0] is not None and next(aside_[0], "end") == "end":
                    aside_[0] = None

        def proj_T(w, cols, dsts):
            slot, wv, landed = w_load(w, cols)
            for m, dst in enumerate(dsts):
                for n in range(2):
                    b, freed = proj_banks.take()
                    mk = mm(bank(b), [(wv[:, k, P * m:P * m + P], aT[:, k, 512 * n:512 * n + 512])
                                      for k in range(KD)], [landed, freed])
                    proj_banks.free[b] = e = evac(dst[:, 512 * n:512 * n + 512], bank(b), [mk],
                                                  chain=False)
                    aside(2)
            wslots.free[slot] = mk
            return e

        def proj_N(w, cols, put):
            width = sum(n for _, n in cols)
            slot, wv, landed = w_load(w, cols)
            for i in range(NT):
                b, freed = proj_banks.take()
                mk = mm(bank(b, width), [(aT[:, k, P * i:P * i + P], wv[:, k, :]) for k in range(KD)],
                        [landed, freed])
                proj_banks.free[b] = e = evac(put(i, bank(b, width))[0], put(i, bank(b, width))[1], [mk],
                                              chain=False)
                aside(1)
            wslots.free[slot] = mk
            return e

        def v2(w, a="a"):
            return w.rearrange("p (a s) -> p a s", a=2)

        def sigmoid_(o, i, tmp=None):
            return fn(o, i, ACT.Sigmoid, now())

        def head_norm_gate(o, sq, gate, col, extra):
            ss = stat[:, 64:96]
            m = tt(sq, o, o, ALU.mult, now())
            red(ss, sq.rearrange("p (n c) -> p n c", c=64), ALU.add)
            r = rstd_of(ss, ss, 64)
            ov_ = o.rearrange("p (n c) -> p n c", c=64)
            m = tt(ov_, ov_, ss.unsqueeze(2).broadcast_to([P, 32, 64]), ALU.mult, [r])
            if gate is not None:
                m = tt(o, o, gate, ALU.mult)
            o3 = o.rearrange("p (t c) -> p t c", t=NT)
            for f in range(2):
                for n in range(2):
                    b, freed = proj_banks.take()
                    for q in range(4):
                        mt = tr(bank(b)[:, P * q:P * q + P], o3[:, 4 * n + q, P * f:P * f + P], [m, freed])
                    proj_banks.free[b] = ts(yT[:, col + f, 512 * n:512 * n + 512], bank(b),
                                            small["gmix"][:, col + f:col + f + 1], None, ALU.mult,
                                            after=[mt])

        w_in = t["w_in"]

        hq, hz, hv = (arena.take(2 * S) for _ in range(3))
        proj_T(w_in, [(IN1["hq"], 256)], [v2(hq)[:, 0], v2(hq)[:, 1]])
        proj_T(w_in, [(IN1["hf"], 256)], [v2(hz)[:, 0], v2(hz)[:, 1]])
        hv3 = hv.rearrange("p (t c) -> p t c", t=NT)
        proj_N(w_in, [(IN1["hi"], 256)], lambda i, b: (hv3[:, i, :], b))
        hb, hk, hE = (arena.take(2 * S) for _ in range(3))
        Z = [arena.take(2 * S), hz]
        lb = stat[:, 128:130]
        lbp = stat[:, 130:132]
        tt(lb, small["lbl"], small["lbl"], ALU.subtract)
        fn(lbp, lb, ACT.Exp, [(dve.sem, dve.count)])
        rec(lb, lbp, [(act.sem, act.count)])
        tt(lbp, lbp, lb, ALU.mult)
        tt(lb, lbp, lbp, ALU.subtract)
        ts(lb, lb, 0.0, None, ALU.max)
        ts(lbp, lb, -1.0, 1.0, ALU.mult, ALU.add)
        stt(hE, hz, -1.0, hz, ALU.mult, ALU.max, now())
        fn(hE, hE, ACT.Exp, [(dve.sem, dve.count)], scale=-1.0)
        m = fn(hE, hE, ACT.Ln, bias=1.0)
        stt(hE, hz, 0.0, hE, ALU.min, ALU.subtract, [m])
        m = tt(hk, hE, hz, ALU.subtract)
        fn(hk, hk, ACT.Exp, [m])
        ts(hb, hz, -1.0, 60.0, ALU.mult, ALU.min)
        fn(hb, hb, ACT.Exp, [(dve.sem, dve.count)])
        m = (act.sem, act.count)
        for f in range(2):
            ts(v2(hb)[:, f], v2(hb)[:, f], lb[:, f:f + 1], None, ALU.mult, after=[m])
            ts(v2(hk)[:, f], v2(hk)[:, f], lbp[:, f:f + 1], None, ALU.mult)
        m = fn(hb, hb, ACT.Ln, [(dve.sem, dve.count)], bias=1.0)
        tt(hE, hE, hb, ALU.add, [m])
        for f in range(2):
            scan(v2(hb)[:, f], scanmask, v2(hE)[:, f], 0.0, ALU.mult, ALU.add)
        b3 = hb.rearrange("p (n c) -> p n c", c=P)
        E3 = hE.rearrange("p (n c) -> p n c", c=P)
        qb = Z[0]
        dec = stat[:, 132:148]
        m = fn(hE, hb, ACT.Exp, [(dve.sem, dve.count)])
        m = fn(dec, b3[:, :, P - 1:P].rearrange("p n c -> p (n c)"), ACT.Exp)
        tt(qb, hq, hE, ALU.mult, [m])
        tt(E3, b3, b3[:, :, P - 1:P].broadcast_to([P, 16, P]), ALU.subtract)
        m = fn(hE, hE, ACT.Exp, [(dve.sem, dve.count)], scale=-1.0)
        kb = hz
        m = tt(kb, hk, hE, ALU.mult, [m])
        kN = arena.take(2 * S)
        kN3 = kN.rearrange("p (t c) -> p t c", t=NT)
        kb3 = v2(kb)
        for c in range(NT):
            b, freed = proj_banks.take()
            for f in range(2):
                mt = tr(bank(b)[:, P * f:P * f + P], kb3[:, f, P * c:P * c + P], [m, freed])
            proj_banks.free[b] = e = evac(kN3[:, c, :], bank(b, 256), [mt])
        kb_read = mt
        U4 = ps[:, 2048:3072].rearrange("p (c f v) -> p c f v", c=8, f=2)
        before = now()
        for c in range(NT - 1):
            for h in range(4):
                mk = mm(ps[64 * (h % 2):64 * (h % 2) + 64, 2048 + 128 * c + 64 * (h // 2):
                           2048 + 128 * c + 64 * (h // 2) + 64],
                        [(kN3[:, c, 64 * h:64 * h + 64], hv3[:, c, 64 * h:64 * h + 64])], before)
        Sh = arena.take(1024).rearrange("p (c f v) -> p c f v", c=8, f=2)
        vset(Sh[:, 0], 0.0)
        dec2 = dec.rearrange("p (f c) -> p f c", f=2)
        for c in range(NT - 1):
            for f in range(2):
                m_state = stt(Sh[:, c + 1, f, :], Sh[:, c, f, :], dec2[:, f, c:c + 1], U4[:, c, f, :],
                              ALU.mult, ALU.add, [mk])
        acc = arena.take(8 * 512)
        acc5 = acc.rearrange("p (r c f t) -> p r c f t", r=2, c=8, f=2)
        vset(acc, 0.0)
        sbanks = Banks([0, 1, 2, 3])
        o_n = kN
        o3 = o_n.rearrange("p (t c) -> p t c", t=NT)
        inter = Banks([6, 7])
        o_int = arena.take(2 * S)
        oi3 = o_int.rearrange("p (t c) -> p t c", t=NT)
        qb3 = v2(qb)
        oi5 = o_int.rearrange("p (t f r c) -> p t f r c", t=NT, f=2, r=2)
        for c0 in range(0, NT, 4):
            for r in range(2):
                b, freed = inter.take()
                r0 = 64 * r
                for c in range(c0, c0 + 4):
                    for f in range(2):
                        mk = mm(bank(b)[:, 128 * (c - c0) + 64 * f:128 * (c - c0) + 64 * f + 64],
                                [(qb3[r0:r0 + 64, f, P * c:P * c + P], Sh[r0:r0 + 64, c, f, :])],
                                [m_state, freed, m])
                inter.free[b] = evac(oi5[:, c0:c0 + 4, :, r, :],
                                     bank(b).rearrange("p (t f c) -> p t f c", t=4, f=2), [mk])
        z_read = [mk, kb_read]
        hk3, hq3 = v2(hk), v2(hq)
        for level in range(LEVELS + 1):
            if level < LEVELS:
                H = 1 << level
                Zl = Z[(level + 1) % 2]
                nb_ = 2 * S // (2 * H)
                bl = hb.rearrange("p (n c) -> p n c", c=2 * H)
                El = hE.rearrange("p (n c) -> p n c", c=2 * H)
                Zv = Zl.rearrange("p (n c) -> p n c", c=2 * H)
                kv = hk.rearrange("p (n c) -> p n c", c=2 * H)
                qv = hq.rearrange("p (n c) -> p n c", c=2 * H)
                m = tt(El, bl, bl[:, :, H - 1:H].broadcast_to([P, nb_, 2 * H]), ALU.subtract,
                       [(act.sem, act.count)])
                fn(El[:, :, 0:H], El[:, :, 0:H], ACT.Exp, [m], scale=-1.0)
                m = fn(El[:, :, H:2 * H], El[:, :, H:2 * H], ACT.Exp)
                tt(Zv[:, :, 0:H], El[:, :, 0:H], kv[:, :, 0:H], ALU.mult, [m, z_read[(level + 1) % 2]])
                m = tt(Zv[:, :, H:2 * H], El[:, :, H:2 * H], qv[:, :, H:2 * H], ALU.mult)
                left = right = v2(Zl)
            else:
                left, right = hk3, hq3
            for c0 in range(0, NT, 2):
                for r in range(2):
                    b, freed = sbanks.take()
                    r0 = 64 * r
                    for q in range(4):
                        c, f = c0 + q // 2, q % 2
                        mk = mm(bank(b)[:, P * q:P * q + P],
                                [(left[r0:r0 + 64, f, P * c:P * c + P],
                                  right[r0:r0 + 64, f, P * c:P * c + P])], [m, freed])
                    msk = level_mask[:, level:level + 1, :].broadcast_to([P, 4, P])
                    dst = acc5[:, r, c0:c0 + 2].rearrange("p c f t -> p (c f) t")
                    sbanks.free[b] = m_acc = dve.do(
                        lambda e, dst=dst, b=b, msk=msk: e.copy_predicated(
                            dst, msk, bank(b).rearrange("p (h t) -> p h t", h=4)), [mk])
            z_read[(level + 1) % 2] = mk
        for c in range(NT):
            b, freed = inter.take()
            for h in range(4):
                mk = mm(bank(b)[:, 64 * h:64 * h + 64],
                        [(acc5[:, h % 2, c, h // 2, :], hv3[:, c, 64 * h:64 * h + 64])], [m_acc, freed])
            inter.free[b] = tt(o3[:, c, :], oi3[:, c, :], bank(b, 256), ALU.add,
                               [mk, (act.sem, act.count)])
        fence()
        hgt = hb
        hg3 = hgt.rearrange("p (t c) -> p t c", t=NT)
        proj_N(w_in, [(IN1["hg"], 256)], lambda i, b: (hg3[:, i, :], b))
        sigmoid_(hE, hgt)
        tt(hgt, hgt, hE, ALU.mult)
        head_norm_gate(o_n, hE, hgt, 2, None)
        fence()
        arena.at = base_w

        gates = arena.take(NT * 12)
        g3 = gates.rearrange("p (t c) -> p t c", t=NT)
        proj_N(w_in, [(IN1["ff"], 4), (IN1["mi"], 8)], lambda i, b: (g3[:, i, :], b))
        wN = arena.take(32).rearrange("p (t h) -> p t h", t=NT)
        eN = arena.take(32).rearrange("p (t h) -> p t h", t=NT)
        fF, tR = arena.take(S, 4), arena.take(S, 4)
        base_g = arena.at
        rows = arena.take(5 * S, 4)
        wI, mM, lF, sR, zR = (rows[:, S * n:S * n + S] for n in range(5))
        gb = small["gate_b"]

        def gate_rows(dst, c0, bias):
            for n in range(2):
                b, freed = proj_banks.take()
                for q in range(4):
                    mt = tr(bank(b)[0:4, P * q:P * q + P], g3[:, 4 * n + q, c0:c0 + 4], [freed] + now())
                proj_banks.free[b] = ts(dst[:, 512 * n:512 * n + 512], bank(b)[0:4], bias, None,
                                        ALU.add, after=[mt])

        def log_sigmoid_rows(dst, src):
            stt(sR, src, -1.0, src, ALU.mult, ALU.max, now())
            fn(sR, sR, ACT.Exp, [(dve.sem, dve.count)], scale=-1.0)
            m = fn(sR, sR, ACT.Ln, bias=1.0)
            return stt(dst, src, 0.0, sR, ALU.min, ALU.subtract, [m])

        onesrow = zR
        vset(onesrow, 1.0)
        gate_rows(tR, 0, gb[:, 0:1])
        log_sigmoid_rows(tR, tR)
        scan(fF, onesrow, tR, 0.0, ALU.mult, ALU.add)
        ts(fF, fF, -8.0, None, ALU.mult)
        gate_rows(tR, 8, gb[:, 2:3])
        log_sigmoid_rows(tR, tR)
        scan(lF, onesrow, tR, 0.0, ALU.mult, ALU.add)
        gate_rows(tR, 4, gb[:, 1:2])
        tt(wI, tR, lF, ALU.subtract)
        ts(sR, wI, 0.0, None, ALU.mult)
        scan(mM, sR, wI, 0.0, ALU.add, ALU.max)
        ts(tR, mM, -1.0, None, ALU.mult)
        tt(sR, mM, lF, ALU.add)
        m = fn(sR, sR, ACT.Exp, [(dve.sem, dve.count)], scale=-1.0)
        before = now()
        for src, o in ((wI, wN), (sR, eN)):
            b, freed = proj_banks.take()
            for i in range(NT):
                mt = tr(bank(b)[:, 4 * i:4 * i + 4], src[:, P * i:P * i + P], before + [freed])
            proj_banks.free[b] = vcopy(o.rearrange("p t h -> p (t h)"), bank(b, 32), [mt])
        fence()
        arena.at = base_g

        def span(n):
            return next(c for c in (128, 256, 512, 1024) if n <= c)

        class Attention:

            def __init__(self, t_ring):
                self.Pm = [arena.take(S) for _ in range(2)]
                self.PT = [arena.take(S) for _ in range(2)]
                self.mneg, self.z, self.sk = arena.take(64), arena.take(64), arena.take(64)
                self.s_free, self.p_free, self.pt_free = [None] * 2, [None] * 2, [None] * 2
                self.t_ring = t_ring
                self.n = 0
                self.o_free = [None, None]

            def run(self, tiles, finish):
                Lane.turns = False
                batches = []
                for u_ in tiles:
                    st = span(u_["width"])
                    nh = min(1024 // st, u_["rows_of"])
                    for h in range(0, u_["heads"], nh):
                        batches.append((u_, st, list(range(h, h + nh)), h + nh == u_["heads"]))
                scored = turned = None
                for bt_ in batches + [None, None]:
                    cur = None if bt_ is None else self.scores(*bt_)
                    if turned is not None:
                        self.values(turned, finish)
                    turned = None if scored is None else self.turn(scored)
                    scored = cur
                    aside(1)
                Lane.turns = True

            def scores(self, u_, st, heads, last):
                p = self.n % 2
                self.n += 1
                w, i, nh = u_["width"], u_["tile"], len(heads)
                so = 1024 * p
                for m_, h in enumerate(heads):
                    for c0 in range(0, w, 512):
                        c1 = min(w, c0 + 512)
                        base_c = so + st * m_
                        extra = u_["bias"](h, c0, c1)
                        group = [(c0, c1, u_["q"](h), u_["k"](h, c0, c1))] + extra
                        for n, (lo, hi, l, r) in enumerate(group):
                            o = ps[:, base_c + lo:base_c + hi]
                            mk = pe.do(lambda e, o=o, l=l, r=r, a=n == 0, z=n == len(group) - 1:
                                       e.matmul(o, l, r, start=a, stop=z), [self.s_free[p]])
                slot = 8 * (i % 4) + heads[0]
                mn, zz = self.mneg[:, slot:slot + nh], self.z[:, slot:slot + nh]
                sc = ps[:, so:so + st * nh].rearrange("p (h c) -> p h c", c=st)[:, :, 0:w]
                if u_.get("sinks") is None:
                    red(mn, sc, ALU.max, [mk], negate=True)
                    m = ts(mn, mn, 0.125, None, ALU.mult)
                else:
                    sk, sink = self.sk[:, slot:slot + nh], u_["sinks"][:, heads[0]:heads[0] + nh]
                    red(mn, sc, ALU.max, [mk])
                    stt(mn, mn, 0.125, sink, ALU.mult, ALU.max)
                    m = ts(mn, mn, -1.0, None, ALU.mult)
                    m_sk = tt(sk, sink, mn, ALU.add)
                Pm = self.Pm[p]
                for m_ in range(nh):
                    e_ = act.do(lambda e, m_=m_: e.activation(
                        Pm[:, w * m_:w * m_ + w], sc[:, m_, :], ACT.Exp, bias=mn[:, m_:m_ + 1],
                        scale=0.125, accum_out=zz[:, m_:m_ + 1]), [m, mk, self.p_free[p]], chain=False)
                self.s_free[p] = e_
                if u_.get("sinks") is not None:
                    k_ = fn(sk, sk, ACT.Exp, [m_sk])
                    self.s_free[p] = e_
                    tt(zz, zz, sk, ALU.add, [k_])
                    rec(zz, zz)
                else:
                    rec(zz, zz, [e_])
                return dict(u=u_, p=p, e=e_, heads=heads, last=last)

            def turn(self, c):
                u_, p, heads = c["u"], c["p"], c["heads"]
                per = u_["width"] // P
                nbk = per * len(heads)
                Pm, PT = self.Pm[p], self.PT[p]
                ev = []
                for b0 in range(0, nbk, 4):
                    n = min(4, nbk - b0)
                    b, freed = self.t_ring.take()
                    for q in range(n):
                        mt = tr(bank(b)[:, P * q:P * q + P], Pm[:, P * (b0 + q):P * (b0 + q) + P],
                                [c["e"], freed])
                    self.t_ring.free[b] = e_ = evac(PT[:, P * b0:P * (b0 + n)], bank(b, P * n),
                                                    [mt, self.pt_free[p]], chain=False)
                    ev += [e_] * n
                self.p_free[p] = mt
                return dict(c, ev=ev)

            def values(self, c, finish):
                u_, p, heads, ev, PT = c["u"], c["p"], c["heads"], c["ev"], self.PT[c["p"]]
                per = u_["width"] // P
                ob = u_["tile"] % 2
                for m_, h in enumerate(heads):
                    col = 512 * (6 + ob) + 64 * h
                    for n in range(per):
                        j = per * m_ + n
                        mk = pe.do(lambda e, j=j, n=n, h=h, col=col: e.matmul(
                            ps[:, col:col + 64], PT[:, P * j:P * j + P], u_["v"](h, n),
                            start=(n == 0), stop=(n == per - 1)), [ev[j], self.o_free[ob]])
                self.pt_free[p] = mk
                if c["last"]:
                    n = u_["heads"]
                    lo = 8 * (u_["tile"] % 4)
                    self.o_free[ob] = finish(u_["tile"], ps[:, 512 * (6 + ob):512 * (6 + ob) + 64 * n],
                                             self.z[:, lo:lo + n], [mk])

        s5_ring = Banks([4, 5])
        HT = S // 2
        s5w = arena.take(128 + 3 * 512)
        s5c, s5bt, s5glu = (s5w[:, 128 + 512 * n:640 + 512 * n] for n in range(3))
        s5_y = arena.take(2 * S)
        s5_tmp = arena.take(8 * HT)
        base_s = arena.at
        uT = yT[:, 0:2]
        a_s5 = arrival("s5_params_landed")
        a_c5 = arrival("s5_c_landed")
        sB = s5_tmp[:, 2 * HT:3 * HT]
        for n, nm in enumerate(("b_re", "b_im")):
            s5l = sp.dma(sB[:, 256 * n:256 * n + 256], t[nm], a_s5, now())
        for n, nm in enumerate(("c_re", "c_im")):
            c5l = sp.dma(s5c[:, 256 * n:256 * n + 256], t[nm], a_c5, now())
        glu = s5glu.rearrange("p (k c) -> p k c", k=2)
        c5l = sp.dma(glu, t["w_glu"].rearrange("(k p) c -> p k c", p=P), a_c5, now())

        def s5_steps(u_ready):
            last = [u_ready]

            def T(o, a, b, op, *more):
                last[0] = tt(o, a, b, op, [last[0], *more])

            def TS(o, a, s1, s2, op0, op1=None):
                last[0] = ts(o, a, s1, s2, op0, op1, after=[last[0]])

            def STT(o, a, s1, b, op0, op1, *more):
                last[0] = stt(o, a, s1, b, op0, op1, [last[0], *more])

            def A(o, a, f, *more, **k):
                last[0] = fn(o, a, f, [last[0], *more], **k)

            lam = small["lam"]
            lr, li = lam[:, 0:8], lam[:, 8:16]
            sl = lambda n: s5w[:, 8 * n:8 * n + 8]
            (dt_, mag, cs, sn, th, kk, den, cfr, cfi, tmp, abr, abi, lrc, tm2,
             ini) = (sl(n) for n in range(15))
            cR, cI = s5c[:, 0:256], s5c[:, 256:512]
            A(dt_, small["ldt"], ACT.Exp)
            TS(lrc, lr, -1e-4, None, ALU.min)
            T(tmp, lrc, dt_, ALU.mult)
            A(mag, tmp, ACT.Exp)
            T(th, li, dt_, ALU.mult)
            TS(kk, th, 1.0 / TWO_PI, ROUND, ALU.mult, ALU.add)
            TS(kk, kk, ROUND, None, ALU.subtract)
            for part in (6.28125, 0.0019350051879882812, 3.019916e-07):
                STT(th, kk, -part, th, ALU.mult, ALU.add)
            TS(th, th, 3.1415925, -3.1415925, ALU.min, ALU.max)
            STT(tmp, th, -1.0, th, ALU.mult, ALU.max)
            TS(tmp, tmp, -1.0, TWO_PI / 4, ALU.mult, ALU.add)
            A(sn, th, ACT.Sin)
            A(cs, tmp, ACT.Sin)
            yield
            T(abr, mag, cs, ALU.mult)
            T(abi, mag, sn, ALU.mult)
            T(den, lrc, lrc, ALU.mult)
            T(tmp, li, li, ALU.mult)
            T(den, den, tmp, ALU.add)
            last[0] = rec(den, den)
            TS(tm2, abr, -1.0, None, ALU.add)
            T(cfr, tm2, lrc, ALU.mult)
            T(tmp, abi, li, ALU.mult)
            T(cfr, cfr, tmp, ALU.add)
            T(cfr, cfr, den, ALU.mult)
            T(cfi, abi, lrc, ALU.mult)
            T(tmp, tm2, li, ALU.mult)
            T(cfi, cfi, tmp, ALU.subtract)
            T(cfi, cfi, den, ALU.mult)
            yield
            bR, bI = sB[:, 0:256], sB[:, 256:512]
            bb, tb = s5_tmp[:, 3 * HT:4 * HT], s5_tmp[:, 4 * HT:4 * HT + 256]
            r3 = lambda a: a.rearrange("p (j c) -> p j c", j=8)
            bc = lambda a: a.unsqueeze(2).broadcast_to([P, 8, 32])
            T(r3(bb[:, 0:256]), r3(bR), bc(cfr), ALU.mult, s5l)
            T(r3(tb), r3(bI), bc(cfi), ALU.mult)
            T(bb[:, 0:256], bb[:, 0:256], tb, ALU.subtract)
            T(r3(bb[:, 256:512]), r3(bI), bc(cfr), ALU.mult)
            T(r3(tb), r3(bR), bc(cfi), ALU.mult)
            T(bb[:, 256:512], bb[:, 256:512], tb, ALU.add)
            last[0] = ts(cI, cI, -1.0, None, ALU.mult, after=[last[0], c5l])
            yield
            b, freed = s5_ring.take()
            for q in range(4):
                mt = tr(bank(b)[:, P * q:P * q + P], bb[:, P * q:P * q + P], [last[0], freed])
            s5_ring.free[b] = last[0] = vcopy(s5bt, bank(b), [mt])
            yS = v2(s5_y)
            cos_t, sin_t, zr, zi, t1, t2, br_, bi_ = (s5_tmp[:, HT * n:HT * n + HT] for n in range(8))
            yield
            for j in range(8):
                f, r0 = j // 4, 32 * (j % 4)
                last[0] = vset(cos_t[:, 0:1], 1.0, [last[0]])
                last[0] = vset(sin_t[:, 0:1], 0.0)
                cn, s_n = cs[:, j:j + 1], sn[:, j:j + 1]
                n = 1
                while n < HT:
                    if n > 1:
                        TS(tmp[:, 0:1], sin_t[:, n - 1:n], sn[:, j:j + 1], None, ALU.mult)
                        STT(kk[:, 0:1], cos_t[:, n - 1:n], cs[:, j:j + 1], tmp[:, 0:1], ALU.mult,
                            ALU.subtract)
                        TS(tmp[:, 0:1], cos_t[:, n - 1:n], sn[:, j:j + 1], None, ALU.mult)
                        STT(kk[:, 1:2], sin_t[:, n - 1:n], cs[:, j:j + 1], tmp[:, 0:1], ALU.mult,
                            ALU.add)
                        cn, s_n = kk[:, 0:1], kk[:, 1:2]
                    TS(t1[:, 0:n], sin_t[:, 0:n], s_n, None, ALU.mult)
                    STT(cos_t[:, n:2 * n], cos_t[:, 0:n], cn, t1[:, 0:n], ALU.mult, ALU.subtract)
                    TS(t1[:, 0:n], cos_t[:, 0:n], s_n, None, ALU.mult)
                    STT(sin_t[:, n:2 * n], sin_t[:, 0:n], cn, t1[:, 0:n], ALU.mult, ALU.add)
                    n *= 2
                    if n in (8, 64, 256):
                        yield
                for half in range(2):
                    cols = slice(HT * half, HT * half + HT)
                    rhs = uT[r0:r0 + 32, f, cols]
                    for part, dst in ((0, br_), (256, bi_)):
                        b, freed = s5_ring.take()
                        mk = mm(bank(b), [(s5bt[r0:r0 + 32, part + P * f:part + P * f + P], rhs)],
                                [last[0], freed])
                        s5_ring.free[b] = ma = acopy(dst, bank(b), [mk])
                    last[0] = ma
                    yield
                    T(t1, cos_t, br_, ALU.mult)
                    T(t2, sin_t, bi_, ALU.mult)
                    T(t1, t1, t2, ALU.add)
                    T(t2, cos_t, bi_, ALU.mult)
                    T(zi, sin_t, br_, ALU.mult)
                    T(t2, t2, zi, ALU.subtract)
                    yield
                    mg = mag[:, j:j + 1].broadcast_to([P, HT])
                    for n, (z_, x_) in enumerate(((zr, t1), (zi, t2))):
                        i0 = ini[:, n:n + 1] if half else 0.0
                        last[0] = scan(z_, mg, x_, i0, ALU.mult, ALU.add, [last[0]])
                    T(t1, cos_t, zr, ALU.mult)
                    T(t2, sin_t, zi, ALU.mult)
                    T(br_, t1, t2, ALU.subtract)
                    yield
                    T(t1, sin_t, zr, ALU.mult)
                    T(t2, cos_t, zi, ALU.mult)
                    T(bi_, t1, t2, ALU.add)
                    if half == 0:
                        xr, xi = br_[:, HT - 1:HT], bi_[:, HT - 1:HT]
                        TS(tmp[:, 0:1], xi, sn[:, j:j + 1], None, ALU.mult)
                        STT(ini[:, 0:1], xr, cs[:, j:j + 1], tmp[:, 0:1], ALU.mult, ALU.subtract)
                        TS(tmp[:, 0:1], xr, sn[:, j:j + 1], None, ALU.mult)
                        STT(ini[:, 1:2], xi, cs[:, j:j + 1], tmp[:, 0:1], ALU.mult, ALU.add)
                    yield
                    b, freed = s5_ring.take()
                    mk = mm(bank(b)[r0:r0 + 32, :], [(cR[:, 32 * j:32 * j + 32], br_),
                                                     (cI[:, 32 * j:32 * j + 32], bi_)],
                            [last[0], freed])
                    STT(yS[r0:r0 + 32, f, cols], uT[r0:r0 + 32, f, cols],
                        small["s5d"][r0:r0 + 32, f:f + 1], bank(b)[r0:r0 + 32, :], ALU.mult, ALU.add, mk)
                    s5_ring.free[b] = last[0]
            yield
            g_, q_ = s5_tmp[:, 0:2 * S], s5_tmp[:, 2 * S:4 * S]
            T(g_, s5_y, s5_y, ALU.mult)
            TS(g_, g_, 0.044715, 1.0, ALU.mult, ALU.add)
            T(g_, g_, s5_y, ALU.mult)
            A(g_, g_, ACT.Sigmoid, scale=2.0 * 0.7978845608028654)
            T(g_, g_, s5_y, ALU.mult)
            gT, qT = v2(g_), v2(q_)
            yield
            for f in range(2):
                for n in range(2):
                    b, freed = s5_ring.take()
                    mk = mm(bank(b), [(glu[:, k, P * f:P * f + P], gT[:, k, 512 * n:512 * n + 512])
                                      for k in range(2)], [last[0], freed])
                    s5_ring.free[b] = ma = fn(qT[:, f, 512 * n:512 * n + 512], bank(b), ACT.Sigmoid,
                                              [mk])
            last[0] = ma
            yield
            T(g_, g_, q_, ALU.mult)
            T(q_, g_, g_, ALU.mult)
            yield
            for n in range(2):
                b, freed = s5_ring.take()
                mk = mm(bank(b), [(ones, qT[:, k, 512 * n:512 * n + 512]) for k in range(2)],
                        [last[0], freed])
                rr = s5_y[:, 512 * n:512 * n + 512]
                last[0] = ts(rr, bank(b), 1.0 / GW, EPS, ALU.mult, ALU.add, after=[mk])
                s5_ring.free[b] = last[0]
                A(rr, rr, ACT.Ln)
                A(rr, rr, ACT.Exp, scale=-0.5)
                for f in range(2):
                    STT(yT[:, f, 512 * n:512 * n + 512], gT[:, f, 512 * n:512 * n + 512],
                        small["gmix"][:, f:f + 1], rr, ALU.mult, ALU.mult)
                yield

        fq, fk, fv = (arena.take(2 * S) for _ in range(3))
        fv3 = fv.rearrange("p (t c) -> p t c", t=NT)
        u_ready = proj_T(w_in, [(IN1["s5"], 256)], [uT[:, 0], uT[:, 1]])
        Lane.turns = False
        aside_[0] = s5_steps((act.sem, act.count))
        for l in (dve, pe):
            l.held = l.held + [u_ready, (act.sem, act.count), (dve.sem, dve.count)]
        for c, dst in ((IN1["fq"], fq), (IN1["fk"], fk)):
            proj_T(w_in, [(c + 64 * h, 64) for h in (0, 2, 1, 3)], [v2(dst)[:, 0], v2(dst)[:, 1]])
        proj_N(w_in, [(IN1["fv"], 256)], lambda i, b: (fv3[:, i, :], b))
        o_f = arena.take(2 * S)
        of3 = o_f.rearrange("p (t c) -> p t c", t=NT)
        att = Attention(s5_ring)
        fq3, fk3 = v2(fq), v2(fk)
        fence()

        def fox_tile(i):
            w = P * (i + 1)
            part = lambda h: slice(64 * (h // 2), 64 * (h // 2) + 64)

            def bias(h, c0, c1):
                got = [(c0, c1, onehot[:, h, :], fF[:, c0:c1])]
                if c1 == w:
                    got.append((w - P, w, ident_b, causal_n))
                return got

            return dict(q=lambda h: fq3[part(h), h % 2, P * i:P * i + P],
                        k=lambda h, c0, c1: fk3[part(h), h % 2, c0:c1], width=w, bias=bias,
                        v=lambda h, n: fv3[:, n, 64 * h:64 * h + 64], tile=i, heads=4, rows_of=2)

        def fox_finish(i, o, rz, after):
            return tt(of3[:, i, :].rearrange("p (h c) -> p h c", h=4),
                      o.rearrange("p (h c) -> p h c", h=4), rz.unsqueeze(2).broadcast_to([P, 4, 64]),
                      ALU.mult, after)

        att.run([fox_tile(i) for i in range(NT)], fox_finish)
        fence()
        head_norm_gate(o_f, fq, None, 4, None)
        fence()
        arena.at = base_s

        mq, mk_, cq, ck, mtmp = (arena.take(2 * S) for _ in range(5))
        mva = arena.take(8 * 4 * 65)
        mva4 = mva.rearrange("p (t h c) -> p t h c", t=NT, h=4)
        Lane.turns = False
        proj_T(w_in, [(IN1["mq"], 256)], [v2(mq)[:, 0], v2(mq)[:, 1]])
        proj_T(w_in, [(IN1["mk"], 256)], [v2(mk_)[:, 0], v2(mk_)[:, 1]])
        vset(mva4[:, :, :, 64:65], 1.0)
        proj_N(w_in, [(IN1["mv"], 256)], lambda i, b: (mva4[:, i, :, 0:64],
                                                      b.rearrange("p (h c) -> p h c", h=4)))
        Lane.turns = True
        fence()
        cw = small["convw"]
        for n, (src, dst) in enumerate(((mq, cq), (mk_, ck))):
            for f in range(2):
                a, o = v2(src)[:, f], v2(dst)[:, f]
                ct = 2 * n + f
                ts(o, a, cw[:, 4 * ct + 3:4 * ct + 4], None, ALU.mult)
                for lag in (1, 2, 3):
                    stt(o[:, lag:S], a[:, 0:S - lag], cw[:, 4 * ct + 3 - lag:4 * ct + 4 - lag],
                        o[:, lag:S], ALU.mult, ALU.add)
            sigmoid_(src, dst)
            if n == 0:
                tt(dst, dst, src, ALU.mult)
            else:
                stt(dst, dst, 0.125, src, ALU.mult, ALU.mult)
        o_m = mq
        om3 = o_m.rearrange("p (t c) -> p t c", t=NT)
        cq3, ck3 = v2(cq), v2(ck)
        nm = arena.take(2 * S).rearrange("p (h s) -> p h s", h=2)
        Wt = [mk_[:, 0:S], mk_[:, S:2 * S]]
        Pt = [mtmp[:, 0:S], mtmp[:, S:2 * S]]
        s_free, w_free, pt_free, o_free = [None] * 2, [None] * 2, [None] * 2, [None] * 2
        dn = stat[:, 256:288]
        Lane.turns = False
        for h0 in (0, 2):
            fence()
            for h in (h0, h0 + 1):
                for n in range(2):
                    b, freed = proj_banks.take()
                    cols = slice(512 * n, 512 * n + 512)
                    mk1 = mm(bank(b), [(onehot[:, h, :], tR[:, cols])], [freed])
                    proj_banks.free[b] = acopy(nm[:, h - h0, cols], bank(b), [mk1])
            pe.held = pe.held + [(act.sem, act.count)]
            dve.held = dve.held + [(act.sem, act.count)]
            pending = None
            units = [(i, h) for i in range(NT) for h in (h0, h0 + 1)]
            for n, un in enumerate(units + [None]):
                cur = None
                if un is not None:
                    i, h = un
                    p = n % 2
                    r0, f = 64 * (h % 2), h // 2
                    first = [s_free[p]]
                    for j in range(i + 1):
                        mks = mm(ps[:, 1024 * p + P * j:1024 * p + P * j + P],
                                 [(ck3[r0:r0 + 64, f, P * j:P * j + P],
                                   cq3[r0:r0 + 64, f, P * i:P * i + P])], first)
                        src, wd_ = nm[:, h - h0, P * i:P * i + P], Wt[p][:, P * j:P * j + P]
                        md = None
                        if j == i:
                            md = tt(wd_, src, causal_t, ALU.add, [w_free[p]])
                            src = wd_
                        mw = fn(wd_, src, ACT.Exp, [w_free[p], md], bias=wN[:, j, h:h + 1])
                    w_ = P * (i + 1)
                    mt = tt(Pt[p][:, 0:w_], ps[:, 1024 * p:1024 * p + w_], Wt[p][:, 0:w_], ALU.mult,
                            [mks, mw, pt_free[p]])
                    s_free[p] = w_free[p] = mt
                    cur = (i, h, p, mt)
                if pending is not None:
                    i, h, p, mt = pending
                    ob = i % 2
                    col = 512 * (6 + ob) + 65 * h
                    mkv = mm(ps[:, col:col + 65], [(Pt[p][:, P * j:P * j + P], mva4[:, j, h, :])
                                                   for j in range(i + 1)], [mt, o_free[ob]])
                    pt_free[p] = mkv
                    if h == h0 + 1:
                        lo = 512 * (6 + ob) + 65 * h0
                        o2_ = ps[:, lo:lo + 130].rearrange("p (h c) -> p h c", h=2)
                        d_ = dn[:, 4 * i + h0:4 * i + h0 + 2]
                        d3 = d_.unsqueeze(2)
                        vcopy(d3, o2_[:, :, 64:65], [mkv])
                        stt(d_, d_, -1.0, d_, ALU.mult, ALU.max)
                        tt(d_, d_, eN[:, i, h0:h0 + 2], ALU.max)
                        rec(d_, d_)
                        o_free[ob] = tt(om3[:, i, 64 * h0:64 * h0 + 128].rearrange(
                            "p (h c) -> p h c", h=2), o2_[:, :, 0:64], d3.broadcast_to([P, 2, 64]),
                            ALU.mult)
                pending = cur
                aside(2)
        aside(1000)
        Lane.turns = True
        fence()
        mo = cq
        mo3 = mo.rearrange("p (t c) -> p t c", t=NT)
        proj_N(w_in, [(IN1["mo"], 256)], lambda i, b: (mo3[:, i, :], b))
        sigmoid_(mo, mo)
        head_norm_gate(o_m, mtmp, mo, 6, None)
        fence()
        arena.at = base_w

        def post_norm_residual(F3, ready, residual, gb_, gl, sq):
            ss = stat[:, 300:308]
            for i in range(NT):
                m = act.do(lambda e, i=i: e.activation(sq, F3[:, i, :], ACT.Square,
                                                       accum_out=ss[:, i:i + 1]), [ready[i]])
            r = rstd_of(ss, ss, D, [m])
            marks = []
            for i in range(NT):
                m = stt(F3[:, i, :], F3[:, i, :], ss[:, i:i + 1], gb_, ALU.mult, ALU.mult, [r, gl])
                tile, landed = residual(i)
                marks.append(tt(X[:, i, :], tile, F3[:, i, :], ALU.add, [landed, m]))
            return marks

        def proj_out_N(w, srcT, kt, dst):
            tiles = [None] * NT
            for c in range(4):
                slot, wv, landed = wslots.load(
                    lambda b: b[:, 0:kt * 256].rearrange("p (k c) -> p k c", k=kt),
                    [(lambda v: v, w.rearrange("(k p) c -> p k c", p=P)[:, :, 256 * c:256 * c + 256])])
                for i in range(NT):
                    b, freed = proj_banks.take()
                    mk = mm(bank(b, 256), [(srcT[:, k, P * i:P * i + P], wv[:, k, :]) for k in range(kt)],
                            [landed, freed])
                    proj_banks.free[b] = tiles[i] = evac(dst[:, i, 256 * c:256 * c + 256],
                                                         bank(b, 256), [mk], chain=False)
                wslots.free[slot] = mk
            return tiles

        F1 = aTW.rearrange("p (t d) -> p t d", t=NT)
        gain_b, sq = arena.take(D), arena.take(D)
        x_again = arena.take(NT * D).rearrange("p (t d) -> p t d", t=NT)
        scratch = arena.take(3 * D)
        a_gain = arrival("post_norm_gain_landed")
        before = now()
        Lane.turns = False
        f_ready = proj_out_N(t["w_out"], yT, KD, F1)
        gl = sp.dma(gain_b, t["g1post"].partition_broadcast(P), a_gain, before)
        again = [sp.dma(x_again[:, i, :], xin[i], a_x[i], before) for i in range(NT)]
        dve.held = dve.held + [(pe.sem, pe.count)]
        ready = post_norm_residual(F1, f_ready, lambda i: (x_again[:, i, :], again[i]), gain_b, gl, sq)
        norm_to_T(small["g2pre"], ready, scratch)
        Lane.turns = True
        fence()
        arena.at = base_w

        NF = FF // P
        hT = arena.take(NF * S).rearrange("p (f s) -> p f s", f=NF)
        tmp4W = arena.take(4 * 512)
        tmp4 = [tmp4W[:, 512 * n:512 * n + 512] for n in range(4)]
        post_gain, sq = tmp4W[:, 0:D], tmp4W[:, D:2 * D]
        fb = Banks([0, 1, 2, 3, 4, 5, 6, 7])
        tfree = [None] * 4

        def swiglu(gate_b, up_b, o, after, k):
            tp = tmp4[k % 4]
            m = fn(tp, bank(gate_b), ACT.Silu, after + [tfree[k % 4]], chain=False)
            m = tt(o, tp, bank(up_b), ALU.mult, [m], chain=False)
            tfree[k % 4] = m
            fb.free[gate_b] = fb.free[up_b] = m
            return m

        kcount = [0]
        Lane.turns = False
        zeros = stat[:, 512:1024]
        zeroed = vset(zeros, 0.0)
        a_clear = arrival("expert_rows_cleared")
        for f in range(NF):
            if 4 <= f < 4 + NBLK - NFIXED:
                b_ = NFIXED + f - 4
                for n in range(D // 512):
                    sp.dma(yb[P * b_:P * b_ + P, 512 * n:512 * n + 512], zeros, a_clear, [zeroed])
            gsl = wslots.load(lambda b: b[:, 0:2048].rearrange("p (w k c) -> p w k c", w=2, k=KD),
                              [(lambda v, n=n: v[:, n], w.rearrange("(k p) c -> p k c", p=P)
                                [:, :, P * f:P * f + P]) for n, w in enumerate((t["w_fg"], t["w_fu"]))])
            slot, wv, landed = gsl
            for n in range(2):
                cols = slice(512 * n, 512 * n + 512)
                bg, f1 = fb.take()
                mm(bank(bg), [(wv[:, 0, k, :], aT[:, k, cols]) for k in range(KD)], [landed, f1])
                bu, f2 = fb.take()
                mk = mm(bank(bu), [(wv[:, 1, k, :], aT[:, k, cols]) for k in range(KD)], [f2])
                swiglu(bg, bu, hT[:, f, cols], [mk], kcount[0])
                kcount[0] += 1
            wslots.free[slot] = mk
        fence()
        gl = sp.dma(post_gain, t["g2post"].partition_broadcast(P), a_gain, now())
        wd = t["w_fd"].rearrange("(f p) c -> p f c", p=P)
        dfree = [None] * NT
        for n in range(2):
            f = 0
            while f < NF:
                nf = min(4, NF - f)
                slot, wv, landed = wslots.load(
                    lambda b: b[:, 0:nf * 512].rearrange("p (k c) -> p k c", k=nf),
                    [(lambda v: v, wd[:, f:f + nf, 512 * n:512 * n + 512])])
                for i in range(NT):
                    for q in range(nf):
                        mk = pe.do(lambda e, i=i, q=q, f=f, wv=wv: e.matmul(
                            bank(i), hT[:, f + q, P * i:P * i + P], wv[:, q, :],
                            start=(f + q == 0), stop=(f + q == NF - 1)),
                            [landed, dfree[i] if f + q == 0 else None])
                wslots.free[slot] = mk
                f += nf
            for i in range(NT):
                dfree[i] = evac(F1[:, i, 512 * n:512 * n + 512], bank(i), [mk], chain=False)
        ready = post_norm_residual(F1, dfree, lambda i: (X[:, i, :], None), post_gain, gl, sq)

        arena.at = base_w
        scratch = arena.take(3 * D)
        norm_to_T(small["gffn"], ready, scratch)
        Lane.turns = True
        fence()
        arena.at = base_w
        w2 = t["w_in_2"]

        OA = arena.take(NT * 512).rearrange("p (t c) -> p t c", t=NT)
        qa = arena.take(4 * S).rearrange("p (a s) -> p a s", a=4)
        gN = arena.take(NT * 24)
        gN3 = gN.rearrange("p (t c) -> p t c", t=NT)
        BL = arena.take(S // 2).bitcast(BF16)
        a_bl = arrival("bias_rows_landed")
        bl_landed = sp.dma(BL[32:P, :], t["c_bl"][32:P, :], a_bl, now())
        base_2 = arena.at

        def heads_proj(c, dst):
            for i in range(0, 4, 2):
                proj_T(w2, [(c + 64 * h, 64) for h in (i, i + 4, i + 1, i + 5)],
                       [dst[:, i], dst[:, i + 1]])

        kx2 = v2(arena.take(2 * S))
        vx3 = arena.take(NT * 256).rearrange("p (t c) -> p t c", t=NT)
        base_x = arena.at
        kcT = arena.take(64)
        vcN = arena.take(128).rearrange("p (g c) -> p g c", g=2)
        base_c = arena.at
        kv2 = v2(arena.take(2 * S))
        AB = [arena.take(S) for _ in range(4)]
        w2s = arena.take(2 * 2 * 64).rearrange("p (n k c) -> p n k c", n=2, k=2)
        w2_free = now()
        hid = [arena.take(2 * 2 * 64).rearrange("p (m g c) -> p m g c", m=2, g=2) for _ in range(2)]
        w1slots = Slots("cmp_w1_landed", 2048, 2, sp)

        heads_proj(IN2["q"], qa)
        proj_N(w2, [(IN2["g"], 24)], lambda i, b: (gN3[:, i, :], b))
        sigmoid_(gN, gN)

        proj_T(w2, [(IN2["kc"], 256)], [kv2[:, 0], kv2[:, 1]])
        a_w2 = arrival("cmp_w2_landed")
        for n, nm_ in enumerate(("cmp_w2_k", "cmp_w2_v")):
            w2_landed = sp.dma(w2s[:, n], t[nm_].rearrange("(k p) c -> p k c", p=P), a_w2, w2_free)
        vset(kcT, 0.0)
        vset(vcN, 0.0)
        Lane.turns = False
        before = now()
        for n, (wn, pos) in enumerate((("cmp_w1_k", "pos_k"), ("cmp_w1_v", "pos_v"))):
            src = t[wn].rearrange("(l d) c -> d l c", d=64)
            kv3 = kv2[:, n].rearrange("p (c l) -> p c l", l=16)
            halves = []
            for half in range(2):
                pv = small[pos][:, 16 * half:16 * half + 16].unsqueeze(1).broadcast_to([P, 64, 16])
                a3 = AB[2 * n + half].rearrange("p (c l) -> p c l", l=16)
                m = tt(a3, kv3, pv, ALU.add, before)
                halves.append(a3)
            hb_ = [[proj_banks.take() for g in range(2)] for mt_ in range(2)]
            for l0 in range(0, 32, 8):
                slot, w1, landed = w1slots.load(
                    lambda b: b.rearrange("p (l c) -> p l c", l=8),
                    [(lambda v, g=g: v[64 * g:64 * g + 64], src[:, l0:l0 + 8, :]) for g in range(2)])
                for mt_ in range(2):
                    for g in range(2):
                        r0 = 64 * g
                        b, freed = hb_[mt_][g]
                        for l in range(l0, l0 + 8):
                            mk = pe.do(lambda e, b=b, l=l, l0=l0, w1=w1, mt_=mt_, r0=r0, a3=halves[l // 16]:
                                       e.matmul(bank(b, NC), w1[r0:r0 + 64, l - l0, P * mt_:P * mt_ + P],
                                                a3[r0:r0 + 64, l // 16:l // 16 + NC, l % 16],
                                                start=(l == 0), stop=(l == 31)),
                                       [m, landed, freed] if l == l0 else ())
                w1slots.free[slot] = mk
            for mt_ in range(2):
                for g in range(2):
                    b = hb_[mt_][g][0]
                    mh = fn(hid[n][:, mt_, g, 0:NC], bank(b, NC), ACT.Silu, [mk], chain=False)
                    proj_banks.free[b] = mh
            b, freed = proj_banks.take()
            if n == 0:
                for g in range(2):
                    r0 = 64 * g
                    mk = mm(bank(b)[r0:r0 + 64, 0:NC], [(w2s[:, 0, k, :], hid[n][:, k, g, 0:NC])
                                                       for k in range(2)], [mh, w2_landed, freed])
                proj_banks.free[b] = vcopy(kcT[:, 0:NC], bank(b, NC), [mk])
            else:
                for g in range(2):
                    for r0 in (0, 64):
                        mk = mm(bank(b)[r0:r0 + NC, 64 * g:64 * g + 64],
                                [(hid[n][:, k, g, 0:NC], w2s[:, 1, k, :]) for k in range(2)],
                                [mh, w2_landed, freed])
                vcopy(vcN[0:NC].rearrange("p g c -> p (g c)"), bank(b)[0:NC, 0:128], [mk])
                proj_banks.free[b] = vcopy(vcN[64:64 + NC].rearrange("p g c -> p (g c)"),
                                           bank(b)[64:64 + NC, 0:128])
        fence()
        arena.at = base_c
        cslots = Slots("cmp_bias_landed", 512 + 64, 2, sp)
        g24 = gN.rearrange("p (t h b) -> p t h b", t=NT, h=8)
        cmp_bufs = [dict(p=arena.take(512), pT=arena.take(512), sc=arena.take(64), top=arena.take(16),
                         pen=arena.take(32), cm=arena.take(16)) for _ in range(2)]
        side_done = [None, None]

        def cmp_tile(i, side):
            bufs, b0 = cmp_bufs[side], 2 + 3 * side
            p_, pTc, sc_, top, pen = (bufs[n] for n in ("p", "pT", "sc", "top", "pen"))
            mx, zz = bufs["cm"][:, 0:8], bufs["cm"][:, 8:16]
            last = [side_done[side]]
            p3 = p_.rearrange("p (h c) -> p h c", h=8)

            def V(step, *more):
                last[0] = dve.do(step, [last[0], *more], chain=False)

            slot, cv, landed = cslots.load(lambda b: b[:, 0:512 + 64], [
                (lambda v: v, t["c_cmp"].rearrange("(t p) c -> t p c", p=P)[i])])
            for h in range(8):
                r0 = 64 * (h // 4)
                mk = mm(bank(b0 + h // 4)[:, 64 * (h % 4):64 * (h % 4) + 64],
                        [(qa[r0:r0 + 64, h % 4, P * i:P * i + P], kcT[r0:r0 + 64, :])], [last[0]])
            yield
            for g in range(2):
                half = slice(256 * g, 256 * g + 256)
                V(lambda e, g=g, half=half: e.scalar_tensor_tensor(
                    p_[:, half], bank(b0 + g, 256), 0.125, cv[:, half], ALU.mult, ALU.add), mk, landed)
                yield
            V(lambda e: e.tensor_reduce(mx, p3, AX, ALU.max))
            yield
            V(lambda e: e.tensor_scalar(mx, mx, -1e29, None, ALU.max))
            yield
            V(lambda e: e.tensor_tensor(p3, p3, mx.unsqueeze(2).broadcast_to([P, 8, 64]), ALU.subtract))
            last[0] = fn(p_, p_, ACT.Exp, [last[0]], chain=False)
            yield
            V(lambda e: e.tensor_reduce(zz, p3, AX, ALU.add))
            yield
            V(lambda e: e.tensor_scalar(zz, zz, 1e-30, None, ALU.max))
            yield
            V(lambda e: e.reciprocal(zz, zz))
            yield
            V(lambda e: e.tensor_tensor(p3, p3, zz.unsqueeze(2).broadcast_to([P, 8, 64]), ALU.mult))
            for q in range(4):
                mt = tr(bank(b0 + 2)[:, P * q:P * q + P], p_[:, P * q:P * q + P], [last[0]])
            last[0] = acopy(pTc, bank(b0 + 2), [mt], chain=False)
            yield
            for g in range(2):
                mk = mm(bank(b0)[:, 16 * g:16 * g + 16],
                        [(pTc[:, P * q:P * q + P], ov) for q in (2 * g, 2 * g + 1)], [last[0]])
            for h in range(8):
                r0 = 64 * (h % 2)
                mo_ = mm(bank(b0 + 1 + h % 2)[:, 64 * (h // 2):64 * (h // 2) + 64],
                         [(pTc[r0:r0 + 64, P * (h // 2):P * (h // 2) + P],
                           vcN[r0:r0 + 64, h // 4, :])], [last[0]])
            yield
            keep, add = cv[:, 512:544], cv[:, 544:576]
            V(lambda e: e.tensor_tensor(sc_[:, 0:32], bank(b0, 32), keep, ALU.mult), mk)
            yield
            V(lambda e: e.tensor_tensor(sc_[:, 0:32], sc_[:, 0:32], add, ALU.add))
            yield
            for g in range(2):
                V(lambda e, g=g: e.max(top[:, 8 * g:8 * g + 8], sc_[:, 16 * g:16 * g + 16]))
                yield
                V(lambda e, g=g: e.match_replace(sc_[:, 32 + 16 * g:48 + 16 * g],
                                                 top[:, 8 * g:8 * g + 8],
                                                 sc_[:, 16 * g:16 * g + 16], -3e38))
                yield
            V(lambda e: e.tensor_scalar(pen, sc_[:, 32:64], -1e38, NEG, ALU.is_gt, ALU.mult))
            mt = tr(bank(b0)[0:32, P:2 * P], pen, [last[0]])
            yield
            for r in range(2):
                gate = g24[:, i, :, 0:1].rearrange("p (f r) b -> p f r b", r=2)[:, :, r, :]
                oa = OA[:, i, :].rearrange("p (f r c) -> p f r c", f=4, r=2)[:, :, r, :]
                V(lambda e, r=r, oa=oa, gate=gate: e.tensor_tensor(
                    oa, bank(b0 + 1 + r, 256).rearrange("p (f c) -> p f c", f=4),
                    gate.broadcast_to([P, 4, 64]), ALU.mult), mo_)
                yield
            cslots.free[slot] = last[0]
            V(lambda e: e.tensor_copy(BL[0:32, P * i:P * i + P], bank(b0)[0:32, P:2 * P]), mt)
            side_done[side] = last[0]

        def cmp_steps():
            for i in range(0, NT, 2):
                pair = [cmp_tile(i, 0), cmp_tile(i + 1, 1)]
                while pair:
                    pair = [g for g in pair if next(g, "end") != "end"]
                    yield

        aside_[:] = [cmp_steps(), 4]
        all_banks, proj_banks = proj_banks, Banks([0, 1])
        proj_N(w2, [(IN2["vs"], 128), (IN2["vw"], 128)], lambda i, b: (vx3[:, i, :], b))
        proj_T(w2, [(IN2["ks"], 128), (IN2["kw"], 128)], [kx2[:, 0], kx2[:, 1]])
        aside(1000)
        proj_banks = all_banks
        aside_[1] = 1
        fence()
        Lane.turns = True
        arena.at = base_x

        BR = arena.take(8 * S // 2).bitcast(BF16)
        BR3 = BR.rearrange("p (h s) -> p h s", h=8)
        br_landed = sp.dma(BR, t["c_br"], a_bl, now())
        att = Attention(s5_ring)
        coef = arena.take(8)
        prod = arena.take(512)
        fence()

        def tile_2(i, q, kT, V, vcol, w, k_lo, bias, sinks=None):
            part = lambda h: slice(64 * (h // 4), 64 * (h // 4) + 64)
            return dict(q=lambda h: q[part(h), h % 4, P * i:P * i + P],
                        k=lambda h, c0, c1: kT[part(h), k_lo + c0:k_lo + c1], width=w, bias=bias,
                        v=lambda h, n: V[:, k_lo // P + n,
                                         vcol + 64 * (h // 4):vcol + 64 * (h // 4) + 64],
                        tile=i, heads=8, rows_of=4, sinks=sinks)

        def gated_finish(branch):
            def finish(i, o, rz, after):
                tt(coef.unsqueeze(2), rz.unsqueeze(2), g24[:, i, :, branch:branch + 1], ALU.mult)
                m = tt(prod.rearrange("p (h c) -> p h c", h=8), o.rearrange("p (h c) -> p h c", h=8),
                       coef.unsqueeze(2).broadcast_to([P, 8, 64]), ALU.mult, after)
                tt(OA[:, i, :], OA[:, i, :], prod, ALU.add)
                return m
            return finish

        def slc_tile(i):
            w = P * (i + 1)

            def bias(h, c0, c1):
                got = [(c0, c1, BL[:, P * i:P * i + P], BR3[:, h, c0:c1])]
                if c1 == w:
                    got.append((w - P, w, ident_b, causal_n))
                return got
            return tile_2(i, qa, kx2[:, 0], vx3, 0, w, 0, bias)

        def band_tile(i, q, kT, V, vcol, nprev, mask, rows_r, sinks=None):
            nb1 = min(i, nprev) + 1
            skip = P * (nprev + 1 - nb1)
            rs = P * (2 - nprev) + skip

            def bias(h, c0, c1):
                return [(c0, c1, win_l, rows_r[:, h, rs + c0:rs + c1]),
                        (c0, c1, ident_b, mask[:, skip + c0:skip + c1])]
            return tile_2(i, q, kT, V, vcol, P * nb1, P * (i + 1 - nb1), bias, sinks)

        att.run([slc_tile(i) for i in range(NT)], gated_finish(1))
        att.run([band_tile(i, qa, kx2[:, 1], vx3, 128, 2, win_mask, win_r) for i in range(NT)],
                gated_finish(2))
        fence()
        arena.at = base_2

        OB = arena.take(NT * 512).rearrange("p (t c) -> p t c", t=NT)
        base_o = arena.at
        kb_ = arena.take(S)
        vb_ = arena.take(NT * 128)
        vb3 = vb_.rearrange("p (t c) -> p t c", t=NT)
        heads_proj(IN2["qb"], qa)
        proj_T(w2, [(IN2["kb"], 128)], [kb_])
        proj_N(w2, [(IN2["vb"], 128)], lambda i, b: (vb3[:, i, :], b))
        att = Attention(s5_ring)
        fence()

        def swa_finish(i, o, rz, after):
            return tt(OB[:, i, :].rearrange("p (h c) -> p h c", h=8),
                      o.rearrange("p (h c) -> p h c", h=8), rz.unsqueeze(2).broadcast_to([P, 8, 64]),
                      ALU.mult, after)

        att.run([band_tile(i, qa, kb_, vb3, 0, 1, swa_mask, swa_r, small["sinks"])
                 for i in range(NT)], swa_finish)
        fence()

        arena.at = base_o
        OAT = arena.take(4 * S).rearrange("p (k s) -> p k s", k=4)
        OBT = arena.take(4 * S).rearrange("p (k s) -> p k s", k=4)
        for src, dst in ((OA, OAT), (OB, OBT)):
            for k in range(4):
                for n in range(2):
                    b, freed = proj_banks.take()
                    for q in range(4):
                        mt = tr(bank(b)[:, P * q:P * q + P], src[:, 4 * n + q, P * k:P * k + P], [freed])
                    proj_banks.free[b] = evac(dst[:, k, 512 * n:512 * n + 512], bank(b), [mt])
        fence()
        keep_at = arena.at
        arena.at = base_w
        mixT = arena.take(8 * S).rearrange("p (k s) -> p k s", k=8)
        arena.at = keep_at
        assert base_w + 8 * S <= base_2
        pslots = Slots("wab_landed", 1024, 2, act)
        keep_at = arena.at
        arena.at = base_2
        tmp4 = [arena.take(512) for _ in range(4)]
        arena.at = keep_at
        tfree = [None] * 4
        m8b = Banks([0, 1, 2, 3, 4, 5, 6, 7])
        k8 = 0
        r_wa = t["w_a"].rearrange("(k p) c -> p k c", p=P)
        r_wb = t["w_b"].rearrange("(k p) c -> p k c", p=P)
        for c in range(8):
            slot, wv, landed = w_load(w2, [(IN2["ga"] + P * c, P), (IN2["gb"] + P * c, P)])
            s2, wab, landed2 = pslots.load(
                lambda b: b.rearrange("p (n k c) -> p n k c", n=2, k=4),
                [(lambda v, n=n: v[:, n], w[:, :, P * c:P * c + P]) for n, w in enumerate((r_wa, r_wb))])
            for n in range(2):
                cols = slice(512 * n, 512 * n + 512)
                parts = []
                for br2, oT in enumerate((OAT, OBT)):
                    b1, f1 = m8b.take()
                    mg_ = mm(bank(b1), [(wv[:, k, P * br2:P * br2 + P], aT[:, k, cols])
                                        for k in range(KD)], [landed, f1])
                    b2, f2 = m8b.take()
                    mp_ = mm(bank(b2), [(wab[:, br2, k, :], oT[:, k, cols]) for k in range(4)],
                             [landed2, f2])
                    tp = tmp4[k8 % 4]
                    m = fn(tp, bank(b1), ACT.Sigmoid, [mg_, tfree[k8 % 4]])
                    m8b.free[b1] = m
                    m8b.free[b2] = tt(tp, tp, bank(b2), ALU.mult, [mp_, m])
                    parts.append((tp, k8 % 4))
                    k8 += 1
                m = tt(mixT[:, c, cols], parts[0][0], parts[1][0], ALU.add)
                tfree[parts[0][1]] = tfree[parts[1][1]] = m
            wslots.free[slot] = mp_
            pslots.free[s2] = mp_
        fence()
        Lane.turns = False
        for c in range(4):
            slot, wv, landed = w_load(t["w_o"], [(256 * c, 256)])
            for i in range(NT):
                b, freed = proj_banks.take()
                mk = mm(bank(b, 256), [(mixT[:, k, P * i:P * i + P], wv[:, k, :]) for k in range(KD)],
                        [landed, freed])
                xs = X[:, i, 256 * c:256 * c + 256]
                proj_banks.free[b] = ready[i] = tt(xs, xs, bank(b, 256), ALU.add, [mk], chain=False)
            wslots.free[slot] = mk
        arena.at = base_w + 8 * S
        scratch = arena.take(3 * D)
        norm_to_T(small["gmoe"], ready, scratch, hn)
        Lane.turns = True
        fence()
        arena.at = base_w

        eslots = Slots("expert_landed", 6144, 3, sp)
        lg = arena.take(NT * 36)
        lg3 = lg.rearrange("p (t c) -> p t c", t=NT)
        bias36 = arena.take(36)
        a_b36 = arrival("router_bias_landed")
        b36 = sp.dma(bias36, t["b_router"].partition_broadcast(P), a_b36, now())
        proj_N(t["w_router"], [(0, 36)], lambda i, b: (lg3[:, i, :], b))
        tt(lg3, lg3, bias36.unsqueeze(1).broadcast_to([P, NT, 36]), ALU.add, now())
        rt = arena.take(1024)
        gm = rt[:, 0:8]
        oh = rt[:, 32:64].rearrange("p (t c) -> p t c", t=NT)
        eq = rt[:, 64:128]
        ein = rt[:, 128:192].rearrange("p (t c) -> p t c", t=NT)
        m1 = rt[:, 192:256].rearrange("p (t c) -> p t c", t=NT)
        m2 = rt[:, 256:320].rearrange("p (t c) -> p t c", t=NT)
        v1, v2_, pg, p1, p2, ix = (rt[:, 320 + 8 * n:328 + 8 * n] for n in range(6))
        we = rt[:, 384:448].rearrange("p (t c) -> p t c", t=NT)
        tm = rt[:, 448:512].rearrange("p (t c) -> p t c", t=NT)
        bc3 = lambda a, n: a.unsqueeze(2).broadcast_to([P, NT, n])

        def first_max(vals, n, value, hot, io):
            red(value, vals, ALU.max)
            tt(hot, vals, bc3(value, n), ALU.is_equal)
            ts(hot, hot, -64.0, 64.0, ALU.mult, ALU.add)
            tt(hot, hot, io.unsqueeze(1).broadcast_to([P, NT, n]), ALU.add)
            red(ix, hot, ALU.min)
            return tt(hot, hot, bc3(ix, n), ALU.is_equal)

        gl3 = lg3[:, :, 0:4]
        first_max(gl3, 4, gm, oh, iota4)
        t4 = eq[:, 0:32].rearrange("p (t c) -> p t c", t=NT)
        m = tt(t4, gl3, bc3(gm, 4), ALU.subtract)
        m = fn(t4, t4, ACT.Exp, [m])
        red(pg, t4, ALU.add, [m])
        rec(pg, pg)
        for g in range(NG):
            le = lg3[:, :, 4 + EG * g:4 + EG * g + EG]
            sel = oh[:, :, g:g + 1].broadcast_to([P, NT, EG])
            if g == 0:
                tt(ein, le, sel, ALU.mult)
            else:
                tt(tm, le, sel, ALU.mult)
                tt(ein, ein, tm, ALU.add)
        first_max(ein, 8, v1, m1, iota8)
        stt(tm, m1, NEG, ein, ALU.mult, ALU.add)
        first_max(tm, 8, v2_, m2, iota8)
        tt(p2, v2_, v1, ALU.subtract)
        m = fn(p2, p2, ACT.Exp, [(dve.sem, dve.count)])
        ts(p1, p2, 1.0, None, ALU.add, after=[m])
        rec(p1, p1)
        tt(p1, p1, pg, ALU.mult)
        tt(p2, p2, p1, ALU.mult)
        one1 = rt[:, 512:768].rearrange("p (t g e) -> p t g e", t=NT, g=NG)
        one2 = rt[:, 768:1024].rearrange("p (t g e) -> p t g e", t=NT, g=NG)
        for g in range(NG):
            sel = oh[:, :, g:g + 1].broadcast_to([P, NT, EG])
            tt(one1[:, :, g, :], m1, sel, ALU.mult)
            tt(one2[:, :, g, :], m2, sel, ALU.mult)
        o1 = one1.rearrange("p t g e -> p t (g e)")
        o2 = one2.rearrange("p t g e -> p t (g e)")
        chosen = arena.take(128).bitcast(BF16).rearrange("p (t e) -> p t e", t=NT)
        m = tt(chosen, o1, o2, ALU.add)
        before = now()
        for i in range(NT):
            pairs = [(ones_b, chosen[:, j, :]) for j in range(i)] + [(before_b, chosen[:, i, :])]
            mk = mm(bank(0)[:, NE * i:NE * i + NE], pairs, before)
        mk = mm(bank(1, NE), [(ones_b, chosen[:, j, :]) for j in range(NT)], before)
        posw = arena.take(2 * 256)
        pos = posw[:, 0:256].rearrange("p (t e) -> p t e", t=NT)
        far = posw[:, 256:512].rearrange("p (t e) -> p t e", t=NT)
        ew = arena.take(5 * NE)
        cnt, more, upto, shift, one_row = (ew[:, NE * n:NE * n + NE] for n in range(5))
        grid = arena.take(NE * NOV)
        vcopy(posw[:, 0:256], bank(0, 256), [mk])
        vcopy(cnt, bank(1, NE))
        g1 = grid.rearrange("p (e b) -> p e b", e=NE)
        tt(g1, cnt.unsqueeze(2).broadcast_to([P, NE, NOV]),
           steps128.unsqueeze(1).broadcast_to([P, NE, NOV]), ALU.is_gt)
        red(more, g1, ALU.add)
        vset(one_row, 1.0)
        scan(upto, one_row, more, 0.0, ALU.mult, ALU.add)
        g2 = grid.rearrange("p (b e) -> p b e", b=NOV)
        ov_e = arena.take(NOV)
        tt(g2, upto.unsqueeze(1).broadcast_to([P, NOV, NE]),
           iota16[:, 0:NOV].unsqueeze(2).broadcast_to([P, NOV, NE]), ALU.is_le)
        red(ov_e, g2, ALU.add)
        ts(ov_e, ov_e, float(NE - 1), None, ALU.min)
        ov_i = arena.take(NOV).bitcast(mybir.dt.int32)
        vcopy(ov_i, ov_e)
        extra_i = arena.take(1).bitcast(mybir.dt.int32)
        m_ov = vcopy(extra_i, upto[:, NE - 1:NE])
        n_extra = extra_i[0:1, 0:1]
        tt(shift, upto, more, ALU.subtract)
        ts(shift, shift, 128.0, 128.0 * (NE - 1), ALU.mult, ALU.add)
        tt(shift, shift, e128, ALU.subtract)
        rows3 = lambda a: a.unsqueeze(1).broadcast_to([P, NT, NE])
        ts(far, pos, 128.0, None, ALU.is_ge)
        tt(far, far, rows3(shift), ALU.mult)
        tt(pos, pos, far, ALU.add)
        tt(pos, pos, rows3(e128), ALU.add)
        dstf = arena.take(16)
        tt(far, pos, o1, ALU.mult)
        red(dstf[:, 0:8], far, ALU.add)
        tt(far, pos, o2, ALU.mult)
        red(dstf[:, 8:16], far, ALU.add)
        dsti = arena.take(16).bitcast(mybir.dt.uint32)
        m_dst = vcopy(dsti, dstf)
        zslot = grid[0:NBLK, 0:P]
        m = vset(zslot, 0.0)
        a_map = arrival("slot_map_cleared")
        cleared = sp.dma(slot_map.rearrange("(b s) o -> b (s o)", s=P), zslot, a_map, [m])
        a_sc = arrival("tokens_scattered")
        for k in range(2):
            for i in range(NT):
                scattered = indirect(slot_map, dsti[:, 8 * k + i:8 * k + i + 1], tokid[:, i:i + 1],
                                     None, a_sc, [cleared, m_dst])
        smap = arena.take(P)
        a_sm = arrival("slot_map_loaded")
        got = sp.dma(smap[0:NBLK, :], slot_map.rearrange("(b s) o -> b (s o)", s=P), a_sm, [scattered])
        mt = tr(bank(2)[:, 0:NBLK], smap[0:NBLK, :], [got] + now())
        idx = arena.take(NBLK).bitcast(mybir.dt.uint32)
        m_idx = vcopy(idx, bank(2, NBLK), [mt])
        fence()
        Lane.turns = False
        xg = [aTW[:, D * n:D * n + D] for n in range(3)]
        xgT = [aTW[:, D * (3 + n):D * (4 + n)].rearrange("p (k s) -> p k s", k=KD) for n in range(2)]
        yo = [aTW[:, D * (5 + n):D * (6 + n)] for n in range(3)]
        a_xg = [arrival(f"rows{n}_gathered") for n in range(3)]
        a_yo = [arrival(f"rows{n}_written") for n in range(3)]
        hid_ = [arena.take(256) for _ in range(2)]
        sg = [arena.take(256) for _ in range(2)]
        xg_free, xgT_free, yo_free, hid_free, sg_free = ([None] * 3, [None] * 2, [None] * 3,
                                                         [None] * 2, [None] * 2)
        tb_, ub_, db_ = Banks([0, 1]), Banks([2, 3]), Banks([4, 5, 6, 7])

        def expert_weights(b_):
            def shape(b):
                return b
            if b_ < NE:
                srcs = [(t["w_ge"][b_], 0, KD), (t["w_ue"][b_], 2048, KD), (t["w_de"][b_], 4096, 2)]
                return eslots.load(shape, [
                    (lambda v, lo=lo, k=k: v[:, lo:lo + 2048].rearrange("p (k c) -> p k c", k=k),
                     w.rearrange("(k p) c -> p k c", p=P)) for w, lo, k in srcs])
            i = eslots.n % len(eslots.bufs)
            eslots.n += 1
            v = eslots.bufs[i]
            arr = eslots.arr[i]
            number = {}
            free_ = eslots.free[i] if isinstance(eslots.free[i], list) else [eslots.free[i]]
            for n, (w, lo, k) in enumerate(((t["w_ge"], 0, KD), (t["w_ue"], 2048, KD),
                                            (t["w_de"], 4096, 2))):
                arr.count += 16

                def step(e, n=n, w=w, lo=lo, k=k):
                    if n == 0:
                        number["e"] = e.value_load(ov_i[0:1, b_ - NE:b_ - NE + 1], min_val=0,
                                                   max_val=NE - 1)
                    src = w[bass.ds(number["e"], 1)].rearrange("o (k p) c -> p (o k) c", p=P)
                    return e.dma_start(v[:, lo:lo + 2048].rearrange("p (k c) -> p k c", k=k), src)
                sp.steps.append((free_ + [m_ov], step,
                                 arr.sem, 16))
            return i, v, (arr.sem, arr.count)

        def block_up(b_):
            n3, n2 = b_ % 3, b_ % 2
            slot, wv, landed = expert_weights(b_)
            rows = indirect(xg[n3], None, hn, idx[:, b_:b_ + 1], a_xg[n3], [m_idx, xg_free[n3]])
            for half in range(2):
                b, freed = tb_.take()
                for q in range(4):
                    k = 4 * half + q
                    mt = tr(bank(b)[:, P * q:P * q + P], xg[n3][:, P * k:P * k + P], [rows, freed])
                g = small["gmoe"][:, 4 * half:4 * half + 4].unsqueeze(2).broadcast_to([P, 4, P])
                tb_.free[b] = e_ = tt(xgT[n2][:, 4 * half:4 * half + 4, :],
                                      bank(b).rearrange("p (q c) -> p q c", q=4), g, ALU.mult,
                                      [mt, xgT_free[n2]])
            xg_free[n3] = mt
            wg = wv[:, 0:2048].rearrange("p (k c) -> p k c", k=KD)
            wu = wv[:, 2048:4096].rearrange("p (k c) -> p k c", k=KD)
            b, freed = ub_.take()
            for n, w in enumerate((wg, wu)):
                for mt_ in range(2):
                    mk = mm(bank(b)[:, 256 * n + P * mt_:256 * n + P * mt_ + P],
                            [(w[:, k, P * mt_:P * mt_ + P], xgT[n2][:, k, :]) for k in range(KD)],
                            [e_, landed, freed])
            xgT_free[n2] = mk
            tp = sg[n2]
            m = fn(tp, bank(b, 256), ACT.Silu, [mk, sg_free[n2]], chain=False)
            m = tt(hid_[n2], tp, bank(b)[:, 256:512], ALU.mult, [m, hid_free[n2]], chain=False)
            sg_free[n2] = ub_.free[b] = m
            return b_, slot, wv, m

        def block_down(b_, slot, wv, ready_):
            n3, n2 = b_ % 3, b_ % 2
            wd_ = wv[:, 4096:6144].rearrange("p (k c) -> p k c", k=2)
            ev = []
            for n in range(2):
                b, freed = db_.take()
                mk = mm(bank(b), [(hid_[n2][:, P * k:P * k + P], wd_[:, k, 512 * n:512 * n + 512])
                                  for k in range(2)], [ready_, freed])
                db_.free[b] = acopy(yo[n3][:, 512 * n:512 * n + 512], bank(b), [mk, yo_free[n3]])
                ev.append(db_.free[b])
            eslots.free[slot] = mk
            hid_free[n2] = mk
            yo_free[n3] = act.dma(yb[P * b_:P * b_ + P, :], yo[n3], a_yo[n3], ev)

        def run_blocks(lo, hi):
            pending = None
            for b_ in range(lo, hi + 1):
                cur = block_up(b_) if b_ < hi else None
                if pending is not None:
                    block_down(*pending)
                pending = cur

        run_blocks(0, NFIXED)
        for n, (lo, hi) in enumerate(GROUPS):
            a_xg[:] = [Arrival(sem(f"rows{b_}_of_group{n}_gathered")) for b_ in range(3)]
            for l in lanes:
                l.begin_group()
            run_blocks(lo, hi)
            for l in lanes:
                l.end_group(lo - NE, m_ov, n_extra, [a.sem.name for a in a_xg])
        yg = [aTW[:, D * n:D * n + D] for n in range(4)]
        sq, gfin = aTW[:, 4 * D:5 * D], aTW[:, 5 * D:6 * D]
        a_gf = arrival("final_gain_landed")
        gl = sp.dma(gfin, t["g_final"].partition_broadcast(P), a_gf, now())
        a_yg = [arrival(f"results{n}_gathered") for n in range(4)]
        yg_free = [None] * 4
        pw = [p1, p2]
        allw = [(a.sem, a.count) for a in a_yo] + [(pe.sem, pe.count), (dve.sem, dve.count)]
        ss = stat[:, 0:8]
        a_out = arrival("out_written")
        outv = out.rearrange("(t p) d -> t p d", p=P)
        for i in range(NT):
            for k in range(2):
                n = (2 * i + k) % 4
                rows = indirect(yg[n], None, yb, dsti[:, 8 * k + i:8 * k + i + 1], a_yg[n],
                                allw + [yg_free[n]])
                yg_free[n] = stt(X[:, i, :], yg[n], pw[k][:, i:i + 1], X[:, i, :], ALU.mult, ALU.add,
                                 [rows])
            m = act.do(lambda e, i=i: e.activation(sq, X[:, i, :], ACT.Square,
                                                   accum_out=ss[:, i:i + 1]), [yg_free[n]])
        r = rstd_of(ss, ss, D, [m])
        for i in range(NT):
            m = stt(X[:, i, :], X[:, i, :], ss[:, i:i + 1], gfin, ALU.mult, ALU.mult, [r, gl])
            stored = sp.dma(outv[i], X[:, i, :], a_out, [m])

        block = ctx.enter_context(nc.Block())

        @block.sync
        def _(eng):
            sp.emit(eng)
            eng.wait_ge(*stored)

        @block.tensor
        def _(eng):
            pe.emit(eng)

        @block.vector
        def _(eng):
            dve.emit(eng)

        @block.scalar
        def _(eng):
            act.emit(eng)

        if pool.steps:
            @block.gpsimd
            def _(eng):
                pool.emit(eng)


def shape_constants():
    bf = np.dtype("bfloat16")
    f32 = np.float32
    r = np.arange(P)
    c = np.zeros((P, 1280 + 512 + 16 + 8 + 72), f32)
    c[:, 1816:1832] = np.arange(16)[None, :]
    c[:, 1832:1832 + NOV] = 128.0 * np.arange(1, NOV + 1)[None, :]
    c[:, 1848:1880] = 128.0 * np.arange(32)[None, :]
    c[:, 1880:1888] = r[:, None] + 128 * np.arange(8)[None, :]
    c[:, 0:128] = np.eye(P)
    c[:, 128:256] = 1.0
    c[:, 256:1280] = (np.arange(S) % P != 0)[None, :]
    for h in range(4):
        c[h, 1280 + 128 * h:1280 + 128 * h + 128] = 1.0
    ov = np.zeros((64, 16))
    for b in range(NC):
        for j in range(16):
            ov[b, j] = max(min(16 * b + 32, 64 * j + 64) - max(16 * b, 64 * j), 0) / 32
    c[0:64, 1792:1808] = ov
    c[64:128, 1792:1808] = ov
    c[:, 1808:1816] = np.arange(8)[None, :]

    slopes = (2.0 ** (-8.0 * np.arange(1, 17) / 16)).astype(f32)
    swa, nsa = slopes[:8], slopes[8:]

    def parts(a):
        a = np.asarray(a, np.float64)
        got = []
        for _ in range(3):
            q = a.astype(bf)
            got.append(q)
            a = a - q.astype(np.float64)
        return got

    b = np.zeros((P, 4224 + 8 * 384 + 256), bf)
    b[:, 7296:7424] = 1.0
    b[:, 7424:7552] = r[:, None] < r[None, :]
    b[:, 0:128] = np.eye(P)
    b[:, 128:256] = np.where(r[None, :] > r[:, None], NEG, 0)
    b[:, 256:384] = np.where(r[:, None] > r[None, :], NEG, 0)
    kw = np.arange(384) - 256
    dist = r[:, None] - kw[None, :]
    b[:, 384:768] = np.where((dist >= 0) & (dist < 256), 0, NEG)
    b[:, 768:1024] = np.where((dist >= 0) & (dist < 128), 0, NEG)[:, 128:]
    for n in range(3):
        b[n, 1024:1152] = r
        b[3 + n, 1024:1152] = 1.0
    for lo, sl in ((1152, nsa), (4224, swa)):
        for h in range(8):
            for n, q in enumerate(parts(-8.0 * sl[h])):
                b[n, lo + 384 * h:lo + 384 * h + 384] = q
            for n, q in enumerate(parts(8.0 * sl[h].astype(np.float64) * kw)):
                b[3 + n, lo + 384 * h:lo + 384 * h + 384] = q

    mask = np.zeros((P, 8, P), bf)
    for l in range(LEVELS):
        same = (r[:, None] >> (l + 1)) == (r[None, :] >> (l + 1))
        mask[:, l] = same & (((r[None, :] >> l) & 1) == 1) & (((r[:, None] >> l) & 1) == 0)
    mask[:, 7] = np.eye(P)

    tok = np.arange(S)
    bl = np.zeros((P, S), bf)
    for n in range(3):
        bl[32 + n] = tok // 256 * 256
        bl[35 + n] = tok % 256
        bl[38 + n] = 1.0
    br = np.zeros((P, 8, S), bf)
    for h in range(8):
        for j in range(16):
            br[16 * (h // 4) + j, h, 64 * j:64 * j + 64] = 1.0
        for n, q in enumerate(parts(-8.0 * nsa[h])):
            br[32 + n, h] = q
            br[35 + n, h] = q
        for n, q in enumerate(parts(8.0 * nsa[h].astype(np.float64) * tok)):
            br[38 + n, h] = q

    cmp_ = np.full((S, 8, 64), NEG, f32)
    d = tok[:, None] - (np.arange(NC) * 16 + 31)[None, :]
    for h in range(8):
        cmp_[:, h, :NC] = np.where(d >= 0, -(nsa[h] * d.astype(f32)), f32(NEG))
    j = np.arange(16)[None, :]
    cur = tok[:, None] // 64
    forced = (j == 0) | (j == cur) | (j == cur - 1)
    valid = j * 64 <= tok[:, None]
    keep = (valid & ~forced).astype(f32)
    add = np.where(forced, 1e9, np.where(valid, 0, NEG)).astype(f32)
    table = np.concatenate([cmp_.reshape(S, 512), keep, keep, add, add], axis=1)
    return dict(c_f32=c, c_bf16=b, c_mask=mask.reshape(P, -1), c_bl=bl, c_br=br.reshape(P, -1),
                c_cmp=table)


def kernel(**inputs):
    import concourse.bacc as bacc
    from concourse.bass_utils import run_bass_kernel_spmd

    a = {k: np.asarray(v) for k, v in inputs.items()}
    f32 = np.float32

    def cols(v):
        return np.ascontiguousarray(v.reshape(-1, P).T)

    def states(v):
        return v.reshape(8, P).T

    def blocks(v):
        o = np.zeros((P, 8, 32), f32)
        w = v.reshape(8, 2, 64, 16)
        for g in range(2):
            o[64 * g:64 * g + 64, :, 16 * g:16 * g + 16] = w[:, g].transpose(1, 0, 2)
        return o.reshape(P, 256)

    x = {
        "x": a["x"][0], "w_in": a["w_in"][0],
        "g1pre": cols(a["ln_mix_pre"][0]), "g2pre": cols(a["ln_ffn_pre"][0]),
        "gmix": cols(a["mix_gain"][0]), "gffn": cols(a["norm_mix_g_2"][0]),
        "gmoe": cols(a["norm_ffn_g_2"][0]),
        "g1post": a["ln_mix_post"][0], "g2post": a["ln_ffn_post"][0], "g_final": a["norm_final_g_2"],
        "lam": np.concatenate([states(a["s5_lambda_re"][0]), states(a["s5_lambda_im"][0])], axis=1),
        "s5d": cols(a["s5_d"][0]),
        "ldt": states(np.repeat(a["s5_log_dt"][0][:, None], 64, axis=1)),
        "lbl": cols(a["hgrn_lb_logits"][0]),
        "convw": np.concatenate([a["mlstm_conv_w"][0][:, P * n:P * n + P].T for n in range(4)], axis=1),
        "gate_b": a["gate_bias"][0].reshape(3, 4).T,
        "sinks": np.broadcast_to(a["sinks_2"][0][None, :], (P, 8)),
        "pos_k": np.concatenate([a["cmp_pos_k_2"][0].T] * 2, axis=0),
        "pos_v": np.concatenate([a["cmp_pos_v_2"][0].T] * 2, axis=0),
        "b_re": blocks(a["s5_b_re"][0]), "b_im": blocks(a["s5_b_im"][0]),
        "c_re": blocks(a["s5_c_re"][0].transpose(0, 2, 1)),
        "c_im": blocks(a["s5_c_im"][0].transpose(0, 2, 1)),
        "w_glu": a["s5_w_glu"][0], "w_out": a["w_out"][0],
        "w_fg": a["w_ffn_gate"][0], "w_fu": a["w_ffn_up"][0], "w_fd": a["w_ffn_down"][0],
        "w_in_2": a["w_in_2"][0],
        "cmp_w1_k": a["cmp_w1_k_2"][0], "cmp_w1_v": a["cmp_w1_v_2"][0],
        "cmp_w2_k": a["cmp_w2_k_2"][0], "cmp_w2_v": a["cmp_w2_v_2"][0],
        "w_a": a["w_a_2"][0], "w_b": a["w_b_2"][0], "w_o": a["w_o_2"][0],
        "w_router": np.concatenate([a["w_group_2"][0], a["w_expert_2"][0]], axis=1),
        "b_router": np.concatenate([a["b_group_2"][0], a["b_expert_2"][0]]),
        "w_ge": a["w_gate_e_2"][0], "w_ue": a["w_up_e_2"][0], "w_de": a["w_down_e_2"][0],
    }
    x.update(shape_constants())
    nc = bacc.Bacc("TRN2", target_bir_lowering=False, num_devices=1)
    arrays, handles = {}, {}
    for name, v in x.items():
        v = np.ascontiguousarray(v)
        arrays["in_" + name] = v
        handles[name] = nc.dram_tensor("in_" + name, v.shape, mybir.dt.from_np(v.dtype),
                                       kind="ExternalInput").ap()
    out = nc.dram_tensor("out", (S, D), F32, kind="ExternalOutput").ap()
    build(nc, handles, out)
    r = run_bass_kernel_spmd(nc, [arrays], core_ids=[0])
    return r.results[0]["out"].reshape(1, S, D)
```
